# Optimizing a Trainium2 kernel written in Bass

```python
import jax, jax.numpy as jnp
from jax import lax
import numpy as np

D_MODEL = 1024
BATCH = 1
SEQ = 512
DEPTH = 2

GRID_W = 64
CTX_LEN = 256
HEAD_DIM = 64
RET_HEADS = 4
RET_W = RET_HEADS * HEAD_DIM
ATT_Q_HEADS = 8
ATT_KV_HEADS = 2
ATT_GROUP = ATT_Q_HEADS // ATT_KV_HEADS
ATT_W = ATT_Q_HEADS * HEAD_DIM
KV_W = ATT_KV_HEADS * HEAD_DIM
CM_GROUPS = 4
CM_CH = 64
CM_W = CM_GROUPS * CM_CH
MIX_W = RET_W + ATT_W + CM_W
IN_SPLITS = (RET_W, RET_W, RET_W, RET_W, ATT_W, KV_W, KV_W, CM_W, CM_W)
IN_W = 4 * RET_W + ATT_W + 2 * KV_W + 2 * CM_W
CHUNK = 128
WINDOW = 128
BLOCK = 128
FFN_HID = -(-8 * D_MODEL // (3 * 256)) * 256
ROPE_BASE = 10000.0
AX_PAIRS = HEAD_DIM // 4
EPS = 1e-6

kernel_name = 'hymba_style_retention_swa_gmlp_dit_trunk'

F32 = jnp.float32

def rms_norm(x, g):
    xf = x.astype(F32)
    y = xf * lax.rsqrt(jnp.mean(xf * xf, axis=-1, keepdims=True) + EPS)
    return (y * g.astype(F32)).astype(x.dtype)

def modulate(z, shift, scale):
    return z * (1 + scale) + shift

def split_in(p):
    return jnp.split(p, np.cumsum(IN_SPLITS)[:-1].tolist(), axis=-1)

def axial_rope_tables(n):
    rows = n // GRID_W
    row = jnp.repeat(jnp.arange(rows, dtype=F32), GRID_W)
    col = jnp.tile(jnp.arange(GRID_W, dtype=F32), rows)
    inv = 1.0 / (ROPE_BASE ** (jnp.arange(AX_PAIRS, dtype=F32) / AX_PAIRS))
    ang = jnp.stack([row[:, None] * inv, col[:, None] * inv], axis=1)
    return jnp.cos(ang), jnp.sin(ang)

def apply_rope(x, cos, sin):
    xr = x.astype(F32).reshape(*x.shape[:-1], 2, 2, AX_PAIRS)
    x1, x2 = xr[..., 0, :], xr[..., 1, :]
    cs, sn = cos[:, None], sin[:, None]
    out = jnp.stack([x1 * cs - x2 * sn, x2 * cs + x1 * sn], axis=-2)
    return out.reshape(x.shape).astype(x.dtype)

def retention_scan(q, k, v, log_gamma, s0):
    b, h, n, dk = q.shape
    dv = v.shape[-1]
    nc = n // CHUNK
    to_chunks = lambda t: t.reshape(b, h, nc, CHUNK, t.shape[-1]).transpose(2, 0, 1, 3, 4)
    qc, kc, vc = to_chunks(q), to_chunks(k), to_chunks(v)
    idx = jnp.arange(CHUNK, dtype=F32)
    lg = log_gamma[:, None]
    diff = idx[:, None] - idx[None, :]
    intra = jnp.where(diff >= 0, jnp.exp(lg[:, :, None] * jnp.maximum(diff, 0.0)), 0.0)
    q_decay = jnp.exp(lg * (idx + 1.0))[:, :, None]
    k_decay = jnp.exp(lg * (CHUNK - 1.0 - idx))[:, :, None]
    chunk_decay = jnp.exp(lg[:, 0] * CHUNK)[:, None, None]

    def step(s, inp):
        qi, ki, vi = inp
        sc = jnp.einsum('bhqd,bhkd->bhqk', qi, ki) * intra
        o = jnp.einsum('bhqk,bhkv->bhqv', sc, vi) + jnp.einsum('bhqd,bhdv->bhqv', qi * q_decay, s)
        s = s * chunk_decay + jnp.einsum('bhkd,bhkv->bhdv', ki * k_decay, vi)
        return s, o

    s_final, o = lax.scan(step, s0, (qc, kc, vc))
    return o.transpose(1, 2, 0, 3, 4).reshape(b, h, n, dv), s_final

def retention_mixer(q, k, v, gate, decay_f, decay_b, norm_g, s0_f, s0_b, rope):
    b, n, _ = q.shape
    shp = (b, n, RET_HEADS, HEAD_DIM)
    q, k, v = q.reshape(shp), k.reshape(shp) * (HEAD_DIM ** -0.5), v.reshape(shp)
    if rope is not None:
        q, k = apply_rope(q, *rope), apply_rope(k, *rope)
    q, k, v = (t.astype(F32).transpose(0, 2, 1, 3) for t in (q, k, v))
    lg_f = jax.nn.log_sigmoid(decay_f.astype(F32))
    lg_b = jax.nn.log_sigmoid(decay_b.astype(F32))
    o_f, st_f = retention_scan(q, k, v, lg_f, s0_f)
    o_b, st_b = retention_scan(q[:, :, ::-1], k[:, :, ::-1], v[:, :, ::-1], lg_b, s0_b)
    o = (o_f + o_b[:, :, ::-1]).transpose(0, 2, 1, 3)
    mu = jnp.mean(o, axis=-1, keepdims=True)
    var = jnp.mean(jnp.square(o - mu), axis=-1, keepdims=True)
    o = ((o - mu) * lax.rsqrt(var + EPS)).reshape(b, n, RET_W) * norm_g.astype(F32)
    return (jax.nn.silu(gate.astype(F32)) * o).astype(gate.dtype), st_f, st_b

def window_attention(q, k, v, kc, vc, sink):
    b, n, _, d = q.shape
    nb = n // BLOCK
    scale = d ** -0.5
    pad = ((0, 0), (BLOCK, BLOCK), (0, 0), (0, 0))
    kp, vp = jnp.pad(k, pad), jnp.pad(v, pad)
    kpos = jnp.arange(3 * BLOCK) - BLOCK
    band = jnp.abs(kpos[None, :] - jnp.arange(BLOCK)[:, None]) <= WINDOW
    sink_l = jnp.broadcast_to(sink.astype(F32).reshape(ATT_KV_HEADS, ATT_GROUP)[None, :, :, None, None],
                              (b, ATT_KV_HEADS, ATT_GROUP, BLOCK, 1))

    def one_block(i):
        start = i * BLOCK
        qi = lax.dynamic_slice_in_dim(q, start, BLOCK, 1).reshape(b, BLOCK, ATT_KV_HEADS, ATT_GROUP, d)
        ki = lax.dynamic_slice_in_dim(kp, start, 3 * BLOCK, 1)
        vi = lax.dynamic_slice_in_dim(vp, start, 3 * BLOCK, 1)
        absk = start + kpos
        valid = band & ((absk >= 0) & (absk < n))[None, :]
        s_loc = jnp.einsum('bqhgd,bkhd->bhgqk', qi, ki).astype(F32) * scale
        s_loc = jnp.where(valid, s_loc, -jnp.inf)
        s_ctx = jnp.einsum('bqhgd,bchd->bhgqc', qi, kc).astype(F32) * scale
        p = jax.nn.softmax(jnp.concatenate([s_loc, s_ctx, sink_l], axis=-1), axis=-1).astype(v.dtype)
        return (jnp.einsum('bhgqk,bkhd->bqhgd', p[..., :3 * BLOCK], vi)
                + jnp.einsum('bhgqc,bchd->bqhgd', p[..., 3 * BLOCK:-1], vc))

    out = lax.map(one_block, jnp.arange(nb))
    return jnp.moveaxis(out, 0, 1).reshape(b, n, ATT_W)

def context_attention(q, k, v, sink):
    b, m, _, d = q.shape
    qg = q.reshape(b, m, ATT_KV_HEADS, ATT_GROUP, d)
    s = jnp.einsum('bqhgd,bkhd->bhgqk', qg, k).astype(F32) * (d ** -0.5)
    sink_l = jnp.broadcast_to(sink.astype(F32).reshape(ATT_KV_HEADS, ATT_GROUP)[None, :, :, None, None],
                              (b, ATT_KV_HEADS, ATT_GROUP, m, 1))
    p = jax.nn.softmax(jnp.concatenate([s, sink_l], axis=-1), axis=-1)[..., :-1].astype(v.dtype)
    return jnp.einsum('bhgqk,bkhd->bqhgd', p, v).reshape(b, m, ATT_W)

def chunk_gating(u, v, norm_g, w_s, b_s):
    b, n, w = u.shape
    u = jax.nn.gelu(u.astype(F32))
    vg = jax.nn.gelu(v.astype(F32)).reshape(b, n // CHUNK, CHUNK, CM_GROUPS, CM_CH)
    mu = jnp.mean(vg, axis=-1, keepdims=True)
    var = jnp.mean(jnp.square(vg - mu), axis=-1, keepdims=True)
    vn = (vg - mu) * lax.rsqrt(var + EPS) * norm_g.astype(F32).reshape(CM_GROUPS, CM_CH)
    s = jnp.einsum('gpq,bcqgd->bcpgd', w_s.astype(F32), vn) + b_s.astype(F32).T[:, :, None]
    return (u * s.reshape(b, n, w)).astype(v.dtype)

def swiglu(z, wg, wu, wd):
    return (jax.nn.silu(z @ wg) * (z @ wu)) @ wd

def setup_inputs(seed: int = 0) -> dict:
    key = jax.random.key(seed)
    ks = jax.random.split(key, 22)
    nrm = lambda k, shape, s: jax.random.normal(k, shape, F32) * s
    base_logit = jnp.log(jnp.exp2(5.0 + jnp.arange(RET_HEADS, dtype=F32)) - 1.0)
    return {
        'x': nrm(ks[0], (BATCH, SEQ, D_MODEL), 1.0),
        'c': nrm(ks[1], (BATCH, D_MODEL), 1.0),
        'ctx': nrm(ks[2], (BATCH, CTX_LEN, D_MODEL), 1.0),
        'c_ctx': nrm(ks[3], (D_MODEL,), 1.0),
        'w_mod': nrm(ks[4], (DEPTH, D_MODEL, 6 * D_MODEL), 0.5 * D_MODEL ** -0.5),
        'b_mod': nrm(ks[5], (DEPTH, 6 * D_MODEL), 0.02),
        'norm1_g': 1.0 + nrm(ks[6], (DEPTH, D_MODEL), 0.02),
        'norm2_g': 1.0 + nrm(ks[7], (DEPTH, D_MODEL), 0.02),
        'w_in': nrm(ks[8], (DEPTH, D_MODEL, IN_W), D_MODEL ** -0.5),
        'ret_decay_f': base_logit + nrm(ks[9], (DEPTH, RET_HEADS), 0.1),
        'ret_decay_b': base_logit + nrm(ks[10], (DEPTH, RET_HEADS), 0.1),
        'ret_norm_g': 1.0 + nrm(ks[11], (DEPTH, RET_W), 0.02),
        'attn_sink': nrm(ks[12], (DEPTH, ATT_Q_HEADS), 0.5),
        'cm_norm_g': 1.0 + nrm(ks[13], (DEPTH, CM_W), 0.02),
        'cm_w_s': nrm(ks[14], (DEPTH, CM_GROUPS, CHUNK, CHUNK), CHUNK ** -0.5),
        'cm_b_s': 1.0 + nrm(ks[15], (DEPTH, CM_GROUPS, CHUNK), 0.1),
        'w_out': nrm(ks[16], (DEPTH, MIX_W, D_MODEL), MIX_W ** -0.5),
        'w_gate': nrm(ks[17], (DEPTH, D_MODEL, FFN_HID), D_MODEL ** -0.5),
        'w_up': nrm(ks[18], (DEPTH, D_MODEL, FFN_HID), D_MODEL ** -0.5),
        'w_down': nrm(ks[19], (DEPTH, FFN_HID, D_MODEL), FFN_HID ** -0.5),
        'final_norm_g': 1.0 + nrm(ks[20], (D_MODEL,), 0.02),
    }

def reference(x, c, ctx, c_ctx, w_mod, b_mod, norm1_g, norm2_g, w_in, ret_decay_f, ret_decay_b,
              ret_norm_g, attn_sink, cm_norm_g, cm_w_s, cm_b_s, w_out, w_gate, w_up, w_down, final_norm_g):
    bsz, n, _ = x.shape
    m = ctx.shape[1]
    rope = axial_rope_tables(n)
    silu_c = jax.nn.silu(c)[:, None, :]
    silu_cc = jax.nn.silu(c_ctx)
    zero_state = jnp.zeros((bsz, RET_HEADS, HEAD_DIM, HEAD_DIM), F32)
    h = ctx
    for l in range(DEPTH):
        last = l == DEPTH - 1
        mx = jnp.split(silu_c @ w_mod[l] + b_mod[l], 6, axis=-1)
        mc = jnp.split(silu_cc @ w_mod[l] + b_mod[l], 6, axis=-1)

        zx = modulate(rms_norm(x, norm1_g[l]), mx[0], mx[1])
        zc = modulate(rms_norm(h, norm1_g[l]), mc[0], mc[1])
        rq, rk, rv, rg, aq, ak, av, cu, cv = split_in(zx @ w_in[l])
        crq, crk, crv, crg, caq, cak, cav, ccu, ccv = split_in(zc @ w_in[l])

        ret_c, st_f, st_b = retention_mixer(crq, crk, crv, crg, ret_decay_f[l], ret_decay_b[l], ret_norm_g[l],
                                            zero_state, zero_state, None)
        ret_x, _, _ = retention_mixer(rq, rk, rv, rg, ret_decay_f[l], ret_decay_b[l], ret_norm_g[l],
                                      st_f, st_b, rope)

        ck = cak.reshape(bsz, m, ATT_KV_HEADS, HEAD_DIM)
        cvv = cav.reshape(bsz, m, ATT_KV_HEADS, HEAD_DIM)
        q = apply_rope(aq.reshape(bsz, n, ATT_Q_HEADS, HEAD_DIM), *rope)
        k = apply_rope(ak.reshape(bsz, n, ATT_KV_HEADS, HEAD_DIM), *rope)
        att_x = window_attention(q, k, av.reshape(bsz, n, ATT_KV_HEADS, HEAD_DIM), ck, cvv, attn_sink[l])

        cm_x = chunk_gating(cu, cv, cm_norm_g[l], cm_w_s[l], cm_b_s[l])

        x = x + mx[2] * (jnp.concatenate([ret_x, att_x, cm_x], axis=-1) @ w_out[l])
        x = x + mx[5] * swiglu(modulate(rms_norm(x, norm2_g[l]), mx[3], mx[4]), w_gate[l], w_up[l], w_down[l])

        if not last:
            att_c = context_attention(caq.reshape(bsz, m, ATT_Q_HEADS, HEAD_DIM), ck, cvv, attn_sink[l])
            cm_c = chunk_gating(ccu, ccv, cm_norm_g[l], cm_w_s[l], cm_b_s[l])
            h = h + mc[2] * (jnp.concatenate([ret_c, att_c, cm_c], axis=-1) @ w_out[l])
            h = h + mc[5] * swiglu(modulate(rms_norm(h, norm2_g[l]), mc[3], mc[4]), w_gate[l], w_up[l], w_down[l])
    return rms_norm(x, final_norm_g)


_drawn_inputs = setup_inputs


def setup_inputs(seed=0):
    import zlib

    import numpy as np

    out = dict(_drawn_inputs(seed))
    spreads = {}
    factors = {'norm1_g': 6.922,
     'norm2_g': 6.584,
     'ret_norm_g': 8.0,
     'attn_sink': 8.0,
     'cm_norm_g': 8.0,
     'cm_b_s': 3.667,
     'final_norm_g': 2.953}
    for name, (base, spread) in spreads.items():
        noise = np.random.default_rng([zlib.crc32(name.encode()), seed]).standard_normal(out[name].shape)
        drawn = base * np.exp(spread * noise) if base else spread * noise
        out[name] = __import__('jax').numpy.asarray(drawn.astype(out[name].dtype))
    for name, factor in factors.items():
        out[name] = (out[name] * factor).astype(out[name].dtype)
    return out
```

```python
from contextlib import ExitStack

import concourse.bass as bass
from concourse import mybir

F32 = mybir.dt.float32
F32R = mybir.dt.float32r
ALU = mybir.AluOpType
ACT = mybir.ActivationFunctionType
AX_X = mybir.AxisListType.X

P = 128
D = 1024
KC = D // P
DEPTH = 2
SX = 512
SC = 256
NT = SX + SC
HD = 64
EPS = 1e-6
SCALE = HD ** -0.5
FFN = 2816
FSTEPS = FFN // 256
IN_W = 2304
MASKED = -1e30

C_RQ, C_RK, C_RV, C_RG, C_AQ, C_AK, C_CU, C_CV = 0, 256, 512, 768, 1024, 1536, 1792, 2048
PANELS = ["rv", "rk", "akav", "rq", "cv", "cu", "aq0", "aq1", "rg"]
PANEL_COL = {"rv": C_RV, "rk": C_RK, "akav": C_AK, "rq": C_RQ, "cv": C_CV, "cu": C_CU, "rg": C_RG}
NP_IN = len(PANELS)
NP_CTX = 3

R_N1, R_N2, R_NF, R_RN, R_CN, N_ROWS = 0, 16, 32, 40, 44, 48
N_BROWS = DEPTH * 48

K_EYE, K_ONES, K_BLK, K_SEL, K_MASK, K_MASK3, K_DIST, K_RC, K_RS = 0, 128, 256, 384, 386, 1026, 1538, 2434, 2946
K_ALL = 3458
DIST_W = 896


class Chain:

    def __init__(self, eng, sem):
        self.eng, self.sem, self.n, self.shift = eng, sem, 0, 0

    def then(self, ins):
        ins.then_inc(self.sem, 1)
        self.n += 1
        return ins

    def wait(self):
        self.eng.wait_ge(self.sem, self.n + self.shift)

    def link(self, ins):
        self.then(ins)
        self.wait()
        return ins


def trunk(nc, x, c, ctx_in, c_ctx, w_mod, b_mod, norm1_g, norm2_g, w_in, ret_decay_f, ret_decay_b, ret_norm_g,
          attn_sink, cm_norm_g, cm_w_s, cm_b_s, w_out, w_gate, w_up, w_down, final_norm_g, consts, out):
    stack = ExitStack()
    with stack:
        def sb(name, shape, dt=F32):
            return stack.enter_context(nc.sbuf_tensor(name, shape, dt))

        sems = {}

        def sem(name):
            if name not in sems:
                sems[name] = stack.enter_context(nc.semaphore(name))
            return sems[name]

        def overlay(specs, under=()):
            with ExitStack() as phase:
                for name, shape, dt in list(under) + list(specs):
                    t = phase.enter_context(nc.sbuf_tensor(name, shape, dt))
                    made[name] = t
            return [made[s[0]] for s in specs]

        made = {}

        K = sb("consts_sb", [P, K_ALL])
        xT = sb("xT", [P, KC, NT])
        zh = sb("zh", [P, KC, NT], F32R)
        zl = sb("zl", [P, KC, NT], F32R)
        raw = [sb(f"raw{i}", [P, 2048]) for i in range(2)]
        wh = [sb(f"wh{i}", [P, 2, 1024], F32R) for i in range(2)]
        wl = [sb(f"wl{i}", [P, 2, 1024], F32R) for i in range(2)]
        wsT = sb("wsT", [P, DEPTH, 512])
        bsb = sb("bsb", [P, DEPTH, 2, P])
        vcol = sb("vcol", [P, N_ROWS + N_BROWS])
        modcol = sb("modcol", [P, DEPTH * 48, 2])
        acol = sb("acol", [P, KC, 2])
        modrow = sb("modrow", [4, 512])
        c4 = sb("c4", [P, 4 * KC + P], F32R)
        c4j = c4[:, 0:4 * KC].rearrange("p (j s) -> p j s", s=4)
        lg = sb("lg", [P, 16])
        nlg = sb("nlg", [P, 16])
        blg = sb("blg", [P, 16])
        sinkb = sb("sinkb", [P, DEPTH * 8])
        stats = sb("stats", [P, 2, 20])

        eye = K[:, K_EYE:K_EYE + P]
        ones = K[:, K_ONES:K_ONES + P]
        blk = K[:, K_BLK:K_BLK + P]
        sel = K[0:4, K_SEL:K_SEL + 2]
        dist = K[:, K_DIST:K_DIST + DIST_W]
        ropeC = K[:, K_RC:K_RC + SX]
        ropeS = K[:, K_RS:K_RS + SX]

        xin, raw_s, wh_s, wl_s, crow, cws, rows_a, rows_b, csil, dec, lt1, lt2, lt3 = overlay([
            ("xin", [P, 6, D], F32), ("raw_s", [P, 2048], F32), ("wh_s", [P, 2, 1024], F32R),
            ("wl_s", [P, 2, 1024], F32R), ("crow", [P, 2, KC], F32), ("cws", [P, DEPTH * 4, P], F32),
            ("rows_a", [N_ROWS, P], F32), ("rows_b", [N_BROWS, P], F32), ("csil", [P, KC, 2], F32),
            ("dec", [P, 16], F32), ("lt1", [P, 16], F32), ("lt2", [P, 16], F32), ("lt3", [P, 16], F32)])
        nsq, nacc, nrb, nxz = overlay([
            ("nsq", [P, 2, NT], F32), ("nacc", [P, NT], F32), ("nrb", [P, NT], F32), ("nxz", [P, 2, NT], F32)])
        attn_base = [("aq", [P, 4, NT], F32), ("ak", [P, NT], F32), ("vtok", [P, 6, 384], F32)]
        mix_base = attn_base + [("rq", [P, 2, NT], F32), ("rk", [P, 2, NT], F32), ("rg", [P, 2, NT], F32),
                                ("cu", [P, 2, NT], F32)]
        mixers = mix_base + [("cvt", [P, 6, 256], F32), ("vT", [P, 3, NT], F32), ("rtmp", [P, 2, SX], F32),
                             ("shuf", [P, SX], F32), ("cmst", [P, 2, 24], F32)]
        aq, ak, vtok, rq, rk, rg, cu, cvt, vT, rtmp, shuf, cmst = overlay(mixers)
        cmf = rtmp
        cmsq = vT[:, 0:2, :].rearrange("p a (t n) -> p (a t) n", n=256)
        T, TC, TD, Pm, osb = overlay([
            ("T", [P, 2, DIST_W], F32), ("TC", [P, 2, 640], F32), ("TD", [P, 640], F32), ("Pm", [P, 3, SX], F32),
            ("osb", [P, 2, NT], F32)],
            under=[(n + "_r", s, d) for n, s, d in mix_base])
        oc, gsq = T[:, 0, 0:NT], T[:, 1, 0:NT]
        s_at, pT = overlay([("s_at", [P, 2, 4, 640], F32), ("pT", [P, 5, SX], F32)],
                           under=[(n + "_a", s, d) for n, s, d in attn_base])
        hh, hl, gs, hf, raw_d, raw_m, wh_d, wl_d, wh_m, wl_m = overlay([
            ("hh", [P, 2, 2, NT], F32R), ("hl", [P, 2, 2, NT], F32R), ("gs", [P, NT], F32), ("hf", [P, NT], F32),
            ("raw_d", [P, 2048], F32), ("raw_m", [P, 2048], F32), ("wh_d", [P, 2, 1024], F32R),
            ("wl_d", [P, 2, 1024], F32R), ("wh_m", [P, 2, 1024], F32R), ("wl_m", [P, 2, 1024], F32R)])
        fz, = overlay([("fz", [P, KC, SX], F32)], under=[("nsq_f", [P, 2, NT], F32), ("nacc_f", [P, NT], F32),
                                                      ("nrb_f", [P, NT], F32), ("nxz_f", [P, 2, NT], F32)])
        otok, = overlay([("otok", [P, 4, D], F32)],
                        under=[("nsq_g", [P, 2, NT], F32), ("nacc_g", [P, NT], F32), ("nrb_g", [P, NT], F32),
                               ("nxz_g", [P, 2, NT], F32), ("fz_g", [P, KC, SX], F32)])

        ps = stack.enter_context(nc.psum_tensor("ps", [P, 8, 512], F32))

        def parts(l_or_w):
            return [(0, SX, 0)] + ([(SX, NT, 1)] if l_or_w else [])

        mod_v = [w_mod[l].rearrange("(p j) n -> p j n", j=KC) for l in range(DEPTH)]
        win_v = [w_in[l].rearrange("(k p) n -> p k n", p=P) for l in range(DEPTH)]
        wout_v = [w_out[l].rearrange("(k p) n -> p k n", p=P) for l in range(DEPTH)]
        gate_v = [w_gate[l].rearrange("(k p) n -> p k n", p=P) for l in range(DEPTH)]
        up_v = [w_up[l].rearrange("(k p) n -> p k n", p=P) for l in range(DEPTH)]
        down_v = [w_down[l].rearrange("(k p) n -> p k n", p=P) for l in range(DEPTH)]

        A_IN = [0, NP_IN + 4 + FSTEPS]
        A_OUT = [a + NP_IN for a in A_IN]
        A_GATE = [a + 4 for a in A_OUT]
        N_MODB = 2 * NP_IN
        B_UP = [N_MODB, N_MODB + FSTEPS]
        J_IN, J_FFN = 4, 4 + NP_IN

        block = stack.enter_context(nc.Block())

        @block.sync
        def _(sp):
            def startup_panel(q):
                dst = [raw[0], raw[1], raw_s][q % 3]
                J, half = q // 2, q % 2
                sp.dma_start(dst[:, :].rearrange("p (j n) -> p j n", j=4),
                             mod_v[0][:, 4 * half:4 * half + 4, 512 * J:512 * J + 512]).then_inc(sem(f"st_ld{q % 3}"), 16)

            sp.dma_start(crow[:, 0, :], c[0].rearrange("(p j) -> p j", j=KC)).then_inc(sem("ld_c"), 16)
            sp.dma_start(crow[:, 1, :], c_ctx.rearrange("(p j) -> p j", j=KC)).then_inc(sem("ld_c"), 16)
            sp.dma_start(K[:, :], consts).then_inc(sem("ld_k"), 16)
            sp.dma_start(xin[:, 0:4, :], x[0].rearrange("(t p) d -> p t d", p=P)).then_inc(sem("ld_x"), 16)
            for q in range(3):
                startup_panel(q)
            sp.dma_start(xin[:, 4:6, :], ctx_in[0].rearrange("(t p) d -> p t d", p=P)).then_inc(sem("ld_ctx"), 16)
            rows = 0
            for v, n in ((norm1_g.rearrange("l (k p) -> (l k) p", p=P), 16), (norm2_g.rearrange("l (k p) -> (l k) p", p=P), 16),
                         (final_norm_g.rearrange("(k p) -> k p", p=P), 8), (ret_norm_g.rearrange("l (k p) -> (l k) p", p=P), 4),
                         (cm_norm_g.rearrange("l (k p) -> (l k) p", p=P), 4)):
                sp.dma_start(rows_a[rows:rows + n, :], v).then_inc(sem("ld_small"), 16)
                rows += n
            sp.dma_start(rows_b[:, :], b_mod.rearrange("l (k p) -> (l k) p", p=P)).then_inc(sem("ld_small"), 16)
            sp.dma_start(dec[:, 0:8], ret_decay_f.rearrange("l h -> (l h)").partition_broadcast(P)).then_inc(sem("ld_small"), 16)
            sp.dma_start(dec[:, 8:16], ret_decay_b.rearrange("l h -> (l h)").partition_broadcast(P)).then_inc(sem("ld_small"), 16)
            sp.dma_start(sinkb[:, :], attn_sink.rearrange("l h -> (l h)").partition_broadcast(P)).then_inc(sem("ld_small"), 16)
            sp.dma_start(cws[:, :, :], cm_w_s.rearrange("l g p q -> p (l g) q")).then_inc(sem("ld_small"), 16)
            for l in range(DEPTH):
                for g in range(4):
                    sp.dma_start(bsb[64 * (g % 2):64 * (g % 2) + 64, l, g // 2, :],
                                 cm_b_s[l, g].partition_broadcast(64)).then_inc(sem("ld_small"), 16)
            for q in range(3, 8):
                sp.wait_ge(sem("st_hi"), q - 2)
                sp.wait_ge(sem("st_lo"), q - 2)
                startup_panel(q)

            def a_free(a, first=False):
                sp.wait_ge(sem("st_hi" if first else "hiA"), 7 if first else 2 * a)
                sp.wait_ge(sem("st_lo" if first else "loA"), 7 if first else 2 * a)

            def b_free(b, first=False):
                sp.wait_ge(sem("st_hi" if first else "hiB"), 8 if first else 2 * b)
                sp.wait_ge(sem("st_lo" if first else "loB"), 8 if first else 2 * b)

            def load_in(l, p):
                a_free(A_IN[l] + p, first=(l == 0 and p == 0))
                dst = raw[0][:, :].rearrange("p (k n) -> p k n", k=KC)
                name = PANELS[p]
                if name.startswith("aq"):
                    for h in range(2):
                        q = 2 * int(name[2]) + h
                        for part in range(2):
                            col = C_AQ + HD * (q + 4 * part)
                            at = P * h + HD * part
                            sp.dma_start(dst[:, :, at:at + HD], win_v[l][:, :, col:col + HD]).then_inc(sem(f"ld_in{l}"), 16)
                else:
                    sp.dma_start(dst, win_v[l][:, :, PANEL_COL[name]:PANEL_COL[name] + 256]).then_inc(sem(f"ld_in{l}"), 16)

            def load_modb(b):
                b_free(b, first=(b == 0))
                J, half = J_IN + b // 2, b % 2
                l, Jl = J // 12, J % 12
                sp.dma_start(raw[1][:, :].rearrange("p (j n) -> p j n", j=4),
                             mod_v[l][:, 4 * half:4 * half + 4, 512 * Jl:512 * Jl + 512]).then_inc(sem("ld_modb"), 16)

            def load_out(l, p):
                a_free(A_OUT[l] + p)
                dst = raw[0][:, :].rearrange("p (k n) -> p k n", k=KC)
                cols = slice(256 * p, 256 * p + 256)
                sp.dma_start(dst[:, 0:2, :], wout_v[l][:, 0:2, cols]).then_inc(sem(f"ld_out{l}"), 16)
                for part in range(2):
                    rows = w_out[l, 256 + 256 * part:512 + 256 * part, cols].rearrange("(k p) n -> p k n", p=HD)
                    sp.dma_start(dst[64 * part:64 * part + 64, 2:6, :], rows).then_inc(sem(f"ld_out{l}"), 16)
                sp.dma_start(dst[:, 6:8, :], wout_v[l][:, 6:8, cols]).then_inc(sem(f"ld_out{l}"), 16)

            def load_ffn(l, s):
                a_free(A_GATE[l] + s)
                sp.dma_start(raw[0][:, :].rearrange("p (k n) -> p k n", k=KC),
                             gate_v[l][:, :, bass.ds(256 * s, 256)]).then_inc(sem(f"ld_gate{l}"), 16)
                b_free(B_UP[l] + s)
                sp.dma_start(raw[1][:, :].rearrange("p (k n) -> p k n", k=KC),
                             up_v[l][:, :, bass.ds(256 * s, 256)]).then_inc(sem(f"ld_up{l}"), 16)

            def load_down(l, s, first=False):
                if not first:
                    sp.wait_ge(sem(f"hiD{l}"), 2 * s)
                    sp.wait_ge(sem(f"loD{l}"), 2 * s)
                sp.dma_start(raw_d[:, :].rearrange("p (k n) -> p k n", k=2),
                             down_v[l][:, bass.ds(2 * s, 2), :]).then_inc(sem(f"ld_down{l}"), 16)

            def load_modm(s, half, first=False):
                if not first:
                    sp.wait_ge(sem("hiM"), 4 * s + 2 * half)
                    sp.wait_ge(sem("loM"), 4 * s + 2 * half)
                sp.dma_start(raw_m[:, :].rearrange("p (j n) -> p j n", j=4),
                             mod_v[1][:, 4 * half:4 * half + 4, bass.ds(512 * (s + 1), 512)]).then_inc(sem("ld_modm"), 16)

            load_in(0, 0)
            load_modb(0)
            for p in range(NP_IN):
                load_modb(2 * p + 1)
                if p + 1 < NP_IN:
                    load_in(0, p + 1)
                    load_modb(2 * p + 2)
            for l in range(DEPTH):
                if l:
                    for p in range(NP_IN):
                        load_in(l, p)
                for p in range(4):
                    load_out(l, p)
                load_ffn(l, 0)
                sp.wait_ge(sem("use_a"), 2 * A_GATE[l])
                load_down(l, 0, first=True)
                if l == 0:
                    load_modm(0, 0, first=True)
                    load_modm(0, 1)
                with sp.Fori(1, FSTEPS) as s:
                    load_ffn(l, s)
                    if l == 0:
                        load_modm(s, 0)
                        load_modm(s, 1)
                    load_down(l, s)

            for t in range(4):
                sp.wait_ge(sem("fin_evac"), 2 * t + 2)
                sp.dma_start(out[0, P * t:P * t + P, :], otok[:, t, :]).then_inc(sem("stored"), 16)
            sp.wait_ge(sem("stored"), 64)

        @block.gpsimd
        def _(pool):
            def lo(dst, src, hi, done):
                nc.gpsimd.tensor_tensor(dst, src, hi.bitcast(F32), ALU.subtract).then_inc(sem(done), 1)

            def raw_half(buf, h):
                return buf[:, :].rearrange("p (k j n) -> p j k n", k=KC, j=2)[:, h]

            def slot_half(t, h):
                return t[:, h, :].rearrange("p (k n) -> p k n", k=KC)

            def lo_a(a, h):
                pool.wait_ge(sem("hiA"), 2 * a + h + 1)
                lo(slot_half(wl[0], h), raw_half(raw[0], h), slot_half(wh[0], h), "loA")

            def lo_b(b, h):
                pool.wait_ge(sem("hiB"), 2 * b + h + 1)
                lo(slot_half(wl[1], h), raw_half(raw[1], h), slot_half(wh[1], h), "loB")

            def lo_modb(b, h):
                pool.wait_ge(sem("hiB"), 2 * b + h + 1)
                lo(wl[1][:, h, :], raw[1][:, 1024 * h:1024 * h + 1024], wh[1][:, h, :], "loB")

            def lo_modm(m, h):
                pool.wait_ge(sem("hiM"), m + 1)
                lo(wl_m[:, h, :], raw_m[:, 1024 * h:1024 * h + 1024], wh_m[:, h, :], "loM")

            def lo_down(l, s):
                for h in range(2):
                    pool.wait_ge(sem(f"hiD{l}"), 2 * s + h + 1)
                    lo(wl_d[:, h, :], raw_d[:, 1024 * h:1024 * h + 1024], wh_d[:, h, :], f"loD{l}")

            lo_a(0, 0)
            lo_a(0, 1)
            lo_modb(0, 0)
            lo_modb(0, 1)
            with pool.Fori(0, NP_IN - 1) as p:
                lo_a(p + 1, 0)
                lo_modb(2 * p + 1, 0)
                lo_modb(2 * p + 1, 1)
                lo_a(p + 1, 1)
                lo_modb(2 * p + 2, 0)
                lo_modb(2 * p + 2, 1)
            lo_a(NP_IN, 0)
            lo_modb(N_MODB - 1, 0)
            lo_modb(N_MODB - 1, 1)
            lo_a(NP_IN, 1)
            for l in range(DEPTH):
                if l:
                    with pool.Fori(A_IN[l] + 1, A_OUT[l] + 1) as a:
                        lo_a(a, 0)
                        lo_a(a, 1)
                with pool.Fori(A_OUT[l] + 1, A_GATE[l] + 1) as a:
                    lo_a(a, 0)
                    lo_a(a, 1)
                lo_b(B_UP[l], 0)
                lo_b(B_UP[l], 1)
                if l == 0:
                    lo_modm(0, 0)
                    lo_modm(1, 1)

                def ffn_step(s, first=False, last=False):
                    if not first:
                        lo_down(l, s - 1)
                    for h in range(2):
                        if not (last and l):
                            lo_a(A_GATE[l] + s + 1, h)
                        if not last:
                            lo_b(B_UP[l] + s + 1, h)
                        if l == 0 and not (last and h):
                            lo_modm(4 * s + 2 * h + 2, 0)
                            lo_modm(4 * s + 2 * h + 3, 1)

                ffn_step(0, first=True)
                with pool.Fori(1, FSTEPS - 1) as s:
                    ffn_step(s)
                ffn_step(FSTEPS - 1, last=True)
                lo_down(l, FSTEPS - 1)

        @block.scalar
        def _(act):
            ch = Chain(act, sem("act_chain"))

            def copy(dst, src):
                return nc.scalar.activation(dst, src, ACT.Copy)

            def raw_half(buf, h):
                return buf[:, :].rearrange("p (k j n) -> p j k n", k=KC, j=2)[:, h]

            def slot_half(t, h):
                return t[:, h, :].rearrange("p (k n) -> p k n", k=KC)

            def hi_a(a, h, loaded, value, first=False):
                act.wait_ge(sem(loaded), value)
                if first:
                    act.wait_ge(sem("st_use"), 7)
                else:
                    act.wait_ge(sem("use_a"), 2 * a + h - 1)
                copy(slot_half(wh[0], h), raw_half(raw[0], h)).then_inc(sem("hiA"), 1)

            def hi_modb(b, h, first=False):
                act.wait_ge(sem("ld_modb"), 16 * (b + 1))
                if first:
                    act.wait_ge(sem("st_use"), 8)
                else:
                    act.wait_ge(sem("use_b"), 2 * b + h - 1)
                copy(wh[1][:, h, :], raw[1][:, 1024 * h:1024 * h + 1024]).then_inc(sem("hiB"), 1)

            def hi_b(l, s, h):
                act.wait_ge(sem(f"ld_up{l}"), 16 * (s + 1))
                act.wait_ge(sem("use_b"), 2 * (B_UP[l] + s) + h - 1)
                copy(slot_half(wh[1], h), raw_half(raw[1], h)).then_inc(sem("hiB"), 1)

            def hi_modm(m, h, first=False, panel=None):
                act.wait_ge(sem("ld_modm"), 16 * (panel + 1))
                if not first:
                    act.wait_ge(sem("use_m"), m - 1)
                copy(wh_m[:, h, :], raw_m[:, 1024 * h:1024 * h + 1024]).then_inc(sem("hiM"), 1)

            def hi_down(l, s, first=False):
                act.wait_ge(sem(f"ld_down{l}"), 16 * (s + 1))
                if not first:
                    act.wait_ge(sem("dn1_mm0" if l == 0 else "dn0_mm1"), KC * s)
                elif l:
                    act.wait_ge(sem("dn1_mm0"), KC * FSTEPS)
                for h in range(2):
                    copy(wh_d[:, h, :], raw_d[:, 1024 * h:1024 * h + 1024]).then_inc(sem(f"hiD{l}"), 1)

            act.wait_ge(sem("ld_c"), 32)
            ch.link(nc.scalar.activation(csil[:, :, 0], crow[:, 0, :], ACT.Silu))
            nc.scalar.activation(csil[:, :, 1], crow[:, 1, :], ACT.Silu).then_inc(sem("csil_rdy"), 1)
            for q in range(3):
                act.wait_ge(sem(f"st_ld{q}"), 16)
                copy([wh[0], wh[1], wh_s][q][:, :, :].rearrange("p h n -> p (h n)"),
                     [raw[0], raw[1], raw_s][q][:, :]).then_inc(sem("st_hi"), 1)
            for k in range(KC):
                act.wait_ge(sem("xt_mm"), k + 1)
                copy(xT[:, k, 0:SX], ps[:, k % 2, :])
                copy(xT[:, k, SX:NT], ps[:, 2 + k % 2, 0:SC]).then_inc(sem("xt_evac"), 1)
            act.wait_ge(sem("ws_mm"), 1)
            for l in range(DEPTH):
                copy(wsT[:, l, :], ps[:, 5 + l, :]).then_inc(sem("ws_evac"), 1)
            for q in range(3, 8):
                act.wait_ge(sem(f"st_ld{q % 3}"), 16 * (q // 3 + 1))
                act.wait_ge(sem("st_use"), q - 2)
                copy([wh[0], wh[1], wh_s][q % 3][:, :, :].rearrange("p h n -> p (h n)"),
                     [raw[0], raw[1], raw_s][q % 3][:, :]).then_inc(sem("st_hi"), 1)
            act.wait_ge(sem("lg_ax"), 1)
            nc.scalar.activation(lt2[:, :], lt1[:, :], ACT.Exp, scale=-1.0).then_inc(sem("lg_e"), 1)

            def norm(u, W):
                if u == 0:
                    act.wait_ge(sem("xt_evac"), 8)
                else:
                    act.wait_ge(sem("x_done"), u)
                for k in range(KC):
                    if k >= 2:
                        act.wait_ge(sem("nacc_rdy"), 8 * u + k - 1)
                    nc.scalar.activation(nsq[:, k % 2, 0:W], xT[:, k, 0:W], ACT.Square).then_inc(sem("nsq_rdy"), 1)
                act.wait_ge(sem("nvar_rdy"), u + 1)
                nc.scalar.activation(nrb[:, 0:W], nrb[:, 0:W], ACT.Sqrt).then_inc(sem("nrms_rdy"), 1)
                if u < 4:
                    for k in range(KC):
                        act.wait_ge(sem("nzf_rdy"), 8 * u + k + 1)
                        copy(zh[:, k, 0:W], nxz[:, k % 2, 0:W]).then_inc(sem("zh_rdy"), 1)

            for l in range(DEPTH):
                W = NT if l == 0 else SX
                norm(2 * l, NT)

                ld = [0]
                for name in PANELS:
                    ld.append(ld[-1] + (64 if name.startswith("aq") else 16))
                if l == 0:
                    hi_a(0, 0, "ld_in0", ld[1], first=True)
                    hi_a(0, 1, "ld_in0", ld[1], first=True)
                    hi_modb(0, 0, first=True)
                    hi_modb(0, 1, first=True)
                a0 = A_IN[l]
                rope_n = 0
                for p, name in enumerate(PANELS):
                    for h in range(2):
                        n = 2 * p + h
                        act.wait_ge(sem("use_a"), 2 * (a0 + p) + h + 1)
                        if p + 1 < NP_IN:
                            hi_a(a0 + p + 1, h, f"ld_in{l}", ld[p + 2])
                        else:
                            hi_a(a0 + p + 1, h, f"ld_out{l}", 64)
                        ctx = l == 0 or p < NP_CTX
                        px, pc = ps[:, h, :], ps[:, 2 + h, 0:SC]
                        is_rope = name in ("rk", "rq", "aq0", "aq1") or (name == "akav" and h == 0)
                        if is_rope:
                            dst = {"rk": rk[:, h], "rq": rq[:, h], "akav": ak, "aq0": aq[:, h], "aq1": aq[:, 2 + h]}[name]
                            if ctx:
                                copy(dst[:, SX:NT], pc)
                            if rope_n >= 2:
                                act.wait_ge(sem(f"rope_done{l}"), rope_n - 1)
                            copy(rtmp[:, rope_n % 2, :], px).then_inc(sem(f"ev_in{l}"), 1)
                            rope_n += 1
                        else:
                            func = {"cv": ACT.Gelu_apprx_tanh, "cu": ACT.Gelu_apprx_tanh, "rg": ACT.Silu}.get(name, ACT.Copy)
                            dst = {"rv": vT[:, h], "akav": vT[:, 2], "cv": vT[:, h], "cu": cu[:, h], "rg": rg[:, h]}[name]
                            if name == "cv" and h == 0:
                                act.wait_ge(sem(f"vtr_mm{l}"), 3)
                            if ctx:
                                nc.scalar.activation(dst[:, SX:NT], pc, func)
                            nc.scalar.activation(dst[:, 0:SX], px, func).then_inc(sem(f"ev_in{l}"), 1)
                        if l == 0 and h == 0:
                            hi_modb(2 * p + 1, 0)
                            hi_modb(2 * p + 1, 1)
                        if l == 0 and h == 1 and p + 1 < NP_IN:
                            hi_modb(2 * p + 2, 0)
                            hi_modb(2 * p + 2, 1)
                    if p == NP_CTX - 1:
                        for v in range(3):
                            act.wait_ge(sem(f"vtr_mm{l}"), v + 1)
                            cols = slice(P * v, P * v + P)
                            copy(vtok[:, 4:6, cols], ps[:, 7, 0:SC].rearrange("p (t n) -> p t n", t=2))
                            copy(vtok[:, 0:4, cols], ps[:, 5 + v % 2, :].rearrange("p (t n) -> p t n", t=4)).then_inc(sem(f"vtr_ev{l}"), 1)
                for v in range(2):
                    act.wait_ge(sem(f"vtr_mm{l}"), 4 + v)
                    cols = slice(P * v, P * v + P)
                    if l == 0:
                        copy(cvt[:, 4:6, cols], ps[:, 7, 0:SC].rearrange("p (t n) -> p t n", t=2))
                    copy(cvt[:, 0:4, cols], ps[:, 5 + v % 2, :].rearrange("p (t n) -> p t n", t=4)).then_inc(sem(f"vtr_ev{l}"), 1)

                nt = W // P
                act.wait_ge(sem("cm_var"), l + 1)
                nc.scalar.activation(cmst[:, 1, 0:4 * nt], cmst[:, 1, 0:4 * nt], ACT.Sqrt).then_inc(sem("cm_std"), 1)
                e = 0
                for c0, c1, s in parts(l == 0):
                    for r in range(2):
                        act.wait_ge(sem(f"cm_f{l}"), e + 1)
                        copy(zh[:, 6 + r, c0:c1], cmf[:, e % 2, 0:c1 - c0]).then_inc(sem(f"cm_hi{l}"), 1)
                        e += 1

                for h in range(4):
                    act.wait_ge(sem(f"T_arg{l}"), h + 1)
                    i, b = l * 4 + h, h % 2
                    nc.scalar.activation(T[:, b, :], T[:, b, :], ACT.Exp)
                    nc.scalar.activation(TC[:, b, :], dist[:, 0:640], ACT.Exp, bias=blg[:, i:i + 1], scale=lg[:, i:i + 1])
                    if h:
                        act.wait_ge(sem(f"T_done{l}"), h)
                    nc.scalar.activation(TD[:, :], dist[:, 0:640], ACT.Exp, bias=blg[:, 8 + i:9 + i],
                                         scale=nlg[:, 8 + i:9 + i]).then_inc(sem(f"T_exp{l}"), 1)
                    if h % 2:
                        r = h // 2
                        act.wait_ge(sem(f"ret_pv{l}"), (r + 1) * (16 if l == 0 else 12))
                        if l == 0:
                            copy(osb[:, r, SX:NT], ps[:, 6, 0:SC])
                        copy(osb[:, r, 0:SX], ps[:, 5, :]).then_inc(sem(f"osb_rdy{l}"), 1)
                for r in range(2):
                    act.wait_ge(sem(f"oc_rdy{l}"), r + 1)
                    nc.scalar.activation(gsq[:, 0:W], oc[:, 0:W], ACT.Square).then_inc(sem(f"gsq_rdy{l}"), 1)
                    act.wait_ge(sem(f"gvar_rdy{l}"), r + 1)
                    nc.scalar.activation(gsq[:, 0:W], gsq[:, 0:W], ACT.Sqrt).then_inc(sem(f"gstd_rdy{l}"), 1)
                    act.wait_ge(sem(f"ret_f{l}"), r + 1)
                    copy(zh[:, r, 0:W], oc[:, 0:W]).then_inc(sem(f"ret_hi{l}"), 1)

                blocks = list(range(4)) + ([4, 5] if l == 0 else [])
                units = [(i, kv) for i in blocks for kv in range(2)]
                g = 0

                def softmax(u):
                    i, kv = units[u]
                    wd = len(local(i)) * P + SC
                    act.wait_ge(sem(f"at_nb{l}"), u + 1)
                    nc.scalar.activation(stats[:, u % 2, 12:16], stats[:, u % 2, 8:12], ACT.Exp)
                    for c in range(4):
                        last = nc.scalar.activation(s_at[:, u % 2, c, 0:wd], s_at[:, u % 2, c, 0:wd], ACT.Exp,
                                                    bias=stats[:, u % 2, 4 + c:5 + c],
                                                    accum_out=stats[:, u % 2, 16 + c:17 + c])
                    last.then_inc(sem(f"at_exp{l}"), 1)

                def local(i):
                    return list(range(max(i - 1, 0), min(i + 1, 3) + 1)) if i < 4 else []

                def after(u):
                    nonlocal g
                    i, kv = units[u]
                    for kk in range(len(local(i)) + 2):
                        act.wait_ge(sem(f"at_tr{l}"), g + 1)
                        if kk == 0 and u:
                            act.wait_ge(sem(f"at_o{l}"), u)
                        copy(pT[:, kk, :], ps[:, 5 + g % 2, :]).then_inc(sem(f"at_pt{l}"), 1)
                        g += 1
                    if kv == 1:
                        act.wait_ge(sem(f"at_o{l}"), u + 1)
                        copy(zh[:, 2:6, P * i:P * i + P], ps[:, 7, :].rearrange("p (c q) -> p c q", c=4)).then_inc(sem(f"at_hi{l}"), 1)

                for u in range(len(units)):
                    softmax(u)
                    if u:
                        after(u - 1)
                after(len(units) - 1)

                for p in range(4):
                    for h in range(2):
                        a = A_OUT[l] + p + 1
                        if p < 3:
                            hi_a(a, h, f"ld_out{l}", 64 * (p + 2))
                        else:
                            hi_a(a, h, f"ld_gate{l}", 16)
                for h in range(2):
                    hi_b(l, 0, h)
                if l == 0:
                    hi_modm(0, 0, first=True, panel=0)
                    hi_modm(1, 1, first=True, panel=0)
                norm(2 * l + 1, W)

                def chunk(s, h, par):
                    n = 2 * s + h
                    act.wait_ge(sem("use_b"), 2 * (B_UP[l] + s) + h + 1)
                    act.wait_ge(sem(f"ev_h{l}"), n + 1)
                    nc.scalar.activation(gs[:, 0:SX], ps[:, 3 * h, :], ACT.Silu).then_inc(sem(f"gs_rdy{l}"), 1)
                    if l == 0:
                        nc.scalar.activation(gs[:, SX:NT], ps[:, 3 * h + 2, 0:SC], ACT.Silu).then_inc(sem(f"gs_rdy{l}"), 1)
                    return n

                def chunk_hi(s, h, par):
                    n = 2 * s + h
                    act.wait_ge(sem(f"ev_h{l}"), n + 2)
                    copy(hh[:, par, h, 0:W], hf[:, 0:W]).then_inc(sem(f"hh_rdy{l}"), 1)

                def ffn_step(s, par, first=False, last=False, first_down=False):
                    if not first:
                        hi_down(l, s - 1, first=first_down)
                    for h in range(2):
                        chunk(s, h, par)
                        if not last:
                            hi_a(A_GATE[l] + s + 1, h, f"ld_gate{l}", 16 * (s + 2))
                            hi_b(l, s + 1, h)
                        elif l == 0:
                            hi_a(A_IN[1], h, "ld_in1", 16)
                        if l == 0 and not (last and h):
                            nxt = 2 * s + h + 1
                            hi_modm(4 * s + 2 * h + 2, 0, panel=nxt)
                            hi_modm(4 * s + 2 * h + 3, 1, panel=nxt)
                        chunk_hi(s, h, par)

                ffn_step(0, 0, first=True)
                ffn_step(1, 1, first_down=True)
                with act.Fori(0, 4) as i:
                    ffn_step(2 * i + 2, 0)
                    ffn_step(2 * i + 3, 1)
                ffn_step(FSTEPS - 1, 0, last=True)
                hi_down(l, FSTEPS - 1)

            norm(4, SX)
            for t in range(4):
                for half in range(2):
                    g = 2 * t + half
                    act.wait_ge(sem("fin_mm"), g + 1)
                    copy(otok[:, t, 512 * half:512 * half + 512], ps[:, 2 + g % 2, :]).then_inc(sem("fin_evac"), 1)

        @block.vector
        def _(dve):
            ch = Chain(dve, sem("dve_chain"))
            V = nc.vector

            def mod_copy(*done):
                dve.wait_ge(sem(done[0]), done[1])
                V.tensor_copy(modrow[:, :], ps[0:4, MODBANK[0], :]).then_inc(sem("modrow_rdy"), 1)

            MODBANK = [4]

            def mod_add(J):
                dve.wait_ge(sem("mod_fin"), J + 1)
                b = vcol[:, bass.ds(N_ROWS + 4 * J, 4)].unsqueeze(2).to_broadcast([P, 4, 2])
                V.tensor_tensor(modcol[:, bass.ds(4 * J, 4), :],
                                ps[:, 7, 256:264].rearrange("p (i s) -> p i s", i=4), b, ALU.add).then_inc(sem("modcol_rdy"), 1)

            ch.link(V.memset(c4[:, :].bitcast(F32), 0.0))
            dve.wait_ge(sem("csil_rdy"), 1)
            ch.link(V.tensor_copy(c4j[:, :, 0:2], csil[:, :, :]))
            V.tensor_tensor(c4j[:, :, 2:4], csil[:, :, :], c4j[:, :, 0:2].bitcast(F32), ALU.subtract).then_inc(sem("c4_rdy"), 1)

            def lo_start(q):
                dve.wait_ge(sem("st_hi"), q + 1)
                wl_q, wh_q, raw_q = [(wl[0], wh[0], raw[0]), (wl[1], wh[1], raw[1]), (wl_s, wh_s, raw_s)][q % 3]
                V.tensor_tensor(wl_q[:, :, :].rearrange("p h n -> p (h n)"), raw_q[:, :],
                                wh_q[:, :, :].rearrange("p h n -> p (h n)").bitcast(F32), ALU.subtract).then_inc(sem("st_lo"), 1)

            for q in range(3):
                lo_start(q)
            dve.wait_ge(sem("vc_mm"), 1)
            V.tensor_copy(vcol[:, :], ps[:, 7, 0:N_ROWS + N_BROWS]).then_inc(sem("vc_evac"), 1)
            for q in range(3, 8):
                lo_start(q)
                if q % 2 == 1:
                    if q > 3:
                        mod_add(q // 2 - 2)
                    else:
                        mod_copy("st_use", 2)
                        continue
                    mod_copy("st_use", 2 * (q // 2))
            mod_add(2)
            mod_copy("st_use", 8)
            mod_add(3)
            dve.wait_ge(sem("ld_small"), 16 * 18)
            ch.link(V.tensor_scalar(lt3[:, :], dec[:, :], -1.0, None, ALU.mult))
            V.tensor_tensor(lt1[:, :], dec[:, :], lt3[:, :], ALU.max).then_inc(sem("lg_ax"), 1)
            dve.wait_ge(sem("lg_e"), 1)
            ch.link(V.tensor_scalar(lt1[:, :], lt2[:, :], 2.0, None, ALU.add))
            ch.link(V.reciprocal(lt3[:, :], lt1[:, :]))
            ch.link(V.tensor_tensor(lt2[:, :], lt2[:, :], lt3[:, :], ALU.mult))
            ch.link(V.tensor_tensor(lt3[:, :], lt2[:, :], lt2[:, :], ALU.mult))
            ch.link(V.tensor_scalar(lt1[:, :], lt3[:, :], 1.0 / 15, 1.0 / 13, ALU.mult, ALU.add))
            for m in (11, 9, 7, 5, 3, 1):
                ch.link(V.tensor_tensor(lt1[:, :], lt1[:, :], lt3[:, :], ALU.mult))
                ch.link(V.tensor_scalar(lt1[:, :], lt1[:, :], 1.0 / m, None, ALU.add))
            ch.link(V.tensor_tensor(lt1[:, :], lt1[:, :], lt2[:, :], ALU.mult))
            ch.link(V.tensor_scalar(lt1[:, :], lt1[:, :], 2.0, None, ALU.mult))
            ch.link(V.tensor_scalar(lt3[:, :], dec[:, :], 0.0, None, ALU.min))
            ch.link(V.tensor_tensor(lg[:, :], lt3[:, :], lt1[:, :], ALU.subtract))
            ch.link(V.tensor_scalar(nlg[:, :], lg[:, :], -1.0, None, ALU.mult))
            ch.link(V.tensor_scalar(blg[:, 0:8], lg[:, 0:8], float(SX), None, ALU.mult))
            ch.link(V.tensor_scalar(blg[:, 8:16], lg[:, 8:16], float(SC), None, ALU.mult))

            def norm(u, W):
                l, second = u // 2, u % 2
                pt = [(0, SX, 0)] + ([(SX, NT, 1)] if W == NT else [])
                if u < 4:
                    g0 = (R_N2 if second else R_N1) + KC * l
                    v = 4 if second else 1
                    gb = vcol[:, g0:g0 + KC].unsqueeze(2).to_broadcast([P, KC, 2])
                    ch.link(V.scalar_tensor_tensor(acol[:, :, :], modcol[:, 48 * l + KC * v:48 * l + KC * v + KC, :], 1.0,
                                                   gb, ALU.add, ALU.mult))
                for k in range(KC):
                    dve.wait_ge(sem("nsq_rdy"), 8 * u + k + 1)
                    if k:
                        ins = V.tensor_tensor(nacc[:, 0:W], nacc[:, 0:W], nsq[:, k % 2, 0:W], ALU.add)
                    else:
                        ins = V.tensor_copy(nacc[:, 0:W], nsq[:, 0, 0:W])
                    ins.then_inc(sem("nacc_rdy"), 1)
                    dve.wait_ge(sem("nacc_rdy"), 8 * u + k + 1)
                dve.wait_ge(sem("nst_mm"), u + 1)
                for c0, c1, s in pt:
                    last = V.tensor_scalar(nrb[:, c0:c1], ps[:, s, 0:c1 - c0], 1.0 / D, EPS, ALU.mult, ALU.add)
                last.then_inc(sem("nvar_rdy"), 1)
                dve.wait_ge(sem("nrms_rdy"), u + 1)
                ch.link(V.reciprocal(nrb[:, 0:W], nrb[:, 0:W]))
                if u == 4:
                    for k in range(KC):
                        V.scalar_tensor_tensor(fz[:, k, :], xT[:, k, 0:SX], vcol[:, R_NF + k:R_NF + k + 1], nrb[:, 0:SX],
                                               ALU.mult, ALU.mult).then_inc(sem("fz_rdy"), 1)
                    return
                sh = 48 * l + KC * (3 if second else 0)

                def lo(k):
                    dve.wait_ge(sem("zh_rdy"), 8 * u + k + 1)
                    V.tensor_tensor(zl[:, k, 0:W], nxz[:, k % 2, 0:W], zh[:, k, 0:W].bitcast(F32), ALU.subtract
                                    ).then_inc(sem("z_rdy"), 1)

                for k in range(KC):
                    if k >= 2:
                        dve.wait_ge(sem("z_rdy"), 8 * u + k - 1)
                    ch.link(V.tensor_tensor(nxz[:, k % 2, 0:W], xT[:, k, 0:W], nrb[:, 0:W], ALU.mult))
                    for c0, c1, s in pt:
                        last = V.tensor_scalar(nxz[:, k % 2, c0:c1], nxz[:, k % 2, c0:c1], acol[:, k, s:s + 1],
                                               modcol[:, sh + k, s:s + 1], ALU.mult, ALU.add)
                    last.then_inc(sem("nzf_rdy"), 1)
                    if k:
                        lo(k - 1)
                lo(KC - 1)

            for l in range(DEPTH):
                W = NT if l == 0 else SX
                norm(2 * l, NT)

                rope_n = 0
                for p, name in enumerate(PANELS):
                    for h in range(2):
                        if name in ("rk", "rq", "aq0", "aq1") or (name == "akav" and h == 0):
                            dst = {"rk": rk[:, h], "rq": rq[:, h], "akav": ak, "aq0": aq[:, h], "aq1": aq[:, 2 + h]}[name]
                            dve.wait_ge(sem(f"ev_in{l}"), 2 * p + h + 1)
                            src = rtmp[:, rope_n % 2, :]
                            ch.then(V.stream_shuffle(shuf[:, :], src, [(j + 16) % 32 for j in range(32)]))
                            ch.link(V.tensor_tensor(dst[:, 0:SX], src, ropeC, ALU.mult))
                            ch.link(V.tensor_tensor(shuf[:, :], shuf[:, :], ropeS, ALU.mult))
                            V.tensor_tensor(dst[:, 0:SX], dst[:, 0:SX], shuf[:, :], ALU.add).then_inc(sem(f"rope_done{l}"), 1)
                            rope_n += 1
                            dve.wait_ge(sem(f"rope_done{l}"), rope_n)
                        if l == 0 and h == 0 and p:
                            mod_add(J_IN + p - 1)
                    if l == 0:
                        mod_copy("use_b", 4 * p + 4)
                if l == 0:
                    mod_add(J_IN + NP_IN - 1)

                nt = W // P
                G = 4 * nt
                dve.wait_ge(sem(f"vtr_ev{l}"), 5)
                cv = cvt[:, 0:nt, :].rearrange("p t (g d) -> p (t g) d", d=HD)
                sq = cmsq[:, 0:nt, :].rearrange("p t (g d) -> p (t g) d", d=HD)

                def wide(i):
                    return cmst[:, i, 0:G].unsqueeze(2).to_broadcast([P, G, HD])

                ch.link(V.tensor_reduce(cmst[:, 0, 0:G], cv, AX_X, ALU.add))
                ch.link(V.tensor_scalar(cmst[:, 0, 0:G], cmst[:, 0, 0:G], 1.0 / HD, None, ALU.mult))
                ch.link(V.tensor_tensor(cv, cv, wide(0), ALU.subtract))
                ch.link(V.tensor_tensor(sq, cv, cv, ALU.mult))
                ch.link(V.tensor_reduce(cmst[:, 1, 0:G], sq, AX_X, ALU.add))
                V.tensor_scalar(cmst[:, 1, 0:G], cmst[:, 1, 0:G], 1.0 / HD, EPS, ALU.mult, ALU.add).then_inc(sem("cm_var"), 1)
                dve.wait_ge(sem("cm_std"), l + 1)
                ch.link(V.reciprocal(cmst[:, 1, 0:G], cmst[:, 1, 0:G]))
                V.tensor_tensor(cv, cv, wide(1), ALU.mult).then_inc(sem("cm_vn"), 1)
                dve.wait_ge(sem("cm_mm"), l + 1)
                e = 0
                for c0, c1, s in parts(l == 0):
                    n = c1 - c0
                    for r in range(2):
                        src = ps[:, 5 + r, :] if s == 0 else ps[:, 7, SC * r:SC * r + SC]
                        dst = cmf[:, e % 2, 0:n]
                        g = vcol[:, R_CN + 2 * l + r:R_CN + 2 * l + r + 1]
                        bias = bsb[:, l, r, :].unsqueeze(1).to_broadcast([P, n // P, P])
                        ch.link(V.scalar_tensor_tensor(dst.rearrange("p (t q) -> p t q", q=P),
                                                       src.rearrange("p (t q) -> p t q", q=P), g, bias, ALU.mult, ALU.add))
                        V.tensor_tensor(dst, dst, cu[:, r, c0:c1], ALU.mult).then_inc(sem(f"cm_f{l}"), 1)
                        dve.wait_ge(sem(f"cm_hi{l}"), e + 1)
                        V.tensor_tensor(zl[:, 6 + r, c0:c1], dst, zh[:, 6 + r, c0:c1].bitcast(F32), ALU.subtract
                                        ).then_inc(sem(f"cm_lo{l}"), 1)
                        e += 1
                        dve.wait_ge(sem(f"cm_lo{l}"), e)

                def table(h):
                    i, b = l * 4 + h, h % 2
                    ch.link(V.tensor_scalar(T[:, b, :], dist, lg[:, i:i + 1], None, ALU.mult))
                    V.scalar_tensor_tensor(T[:, b, :], dist, nlg[:, 8 + i:9 + i], T[:, b, :], ALU.mult, ALU.min
                                           ).then_inc(sem(f"T_arg{l}"), 1)

                def table_end(h):
                    b = h % 2
                    dve.wait_ge(sem(f"T_exp{l}"), h + 1)
                    ch.link(V.tensor_tensor(T[:, b, 384:512], T[:, b, 384:512], eye, ALU.add))
                    V.tensor_tensor(TC[:, b, :], TC[:, b, :], TD[:, :], ALU.add).then_inc(sem(f"T_done{l}"), 1)
                    dve.wait_ge(sem(f"T_done{l}"), h + 1)

                jobs = [(c, 0) for c in range(6)] + ([(c, 1) for c in (4, 5)] if l == 0 else [])
                table(0)
                j = 0
                for h in range(4):
                    table_end(h)
                    if h < 3:
                        table(h + 1)
                    for c, s in jobs:
                        n = (SX, SC)[s]
                        if s == 0 and c >= 4:
                            tab = TC[:, h % 2, P - P * (c - 4):P - P * (c - 4) + SX]
                        else:
                            off = 384 - P * (c - 4 * s)
                            tab = T[:, h % 2, off:off + n]
                        dve.wait_ge(sem(f"ret_sc{l}"), j + 1)
                        if j >= 3:
                            dve.wait_ge(sem(f"ret_pv{l}"), j - 2)
                        V.scalar_tensor_tensor(Pm[:, j % 3, 0:n], ps[:, j % 3, 0:n], SCALE, tab, ALU.mult, ALU.mult
                                               ).then_inc(sem(f"ret_p{l}"), 1)
                        j += 1
                for r in range(2):
                    dve.wait_ge(sem(f"gmean_mm{l}"), r + 1)
                    for c0, c1, s in parts(l == 0):
                        last = V.tensor_tensor(oc[:, c0:c1], osb[:, r, c0:c1], ps[:, (7, 4)[s], 0:c1 - c0], ALU.subtract)
                    last.then_inc(sem(f"oc_rdy{l}"), 1)
                    dve.wait_ge(sem(f"gvar_mm{l}"), r + 1)
                    for c0, c1, s in parts(l == 0):
                        last = V.tensor_scalar(gsq[:, c0:c1], ps[:, (7, 4)[s], 0:c1 - c0], EPS, None, ALU.add)
                    last.then_inc(sem(f"gvar_rdy{l}"), 1)
                    dve.wait_ge(sem(f"gstd_rdy{l}"), r + 1)
                    ch.link(V.reciprocal(gsq[:, 0:W], gsq[:, 0:W]))
                    ch.link(V.tensor_tensor(oc[:, 0:W], oc[:, 0:W], gsq[:, 0:W], ALU.mult))
                    g = vcol[:, R_RN + 2 * l + r:R_RN + 2 * l + r + 1]
                    V.scalar_tensor_tensor(oc[:, 0:W], oc[:, 0:W], g, rg[:, r, 0:W], ALU.mult, ALU.mult
                                           ).then_inc(sem(f"ret_f{l}"), 1)
                    dve.wait_ge(sem(f"ret_hi{l}"), r + 1)
                    V.tensor_tensor(zl[:, r, 0:W], oc[:, 0:W], zh[:, r, 0:W].bitcast(F32), ALU.subtract
                                    ).then_inc(sem(f"ret_lo{l}"), 1)
                    dve.wait_ge(sem(f"ret_lo{l}"), r + 1)

                blocks = list(range(4)) + ([4, 5] if l == 0 else [])
                units = [(i, kv) for i in blocks for kv in range(2)]

                def local(i):
                    return list(range(max(i - 1, 0), min(i + 1, 3) + 1)) if i < 4 else []

                def scores(u):
                    i, kv = units[u]
                    nl = P * len(local(i))
                    wd = nl + SC
                    mask = {0: K_MASK + P, 3: K_MASK3}.get(i, K_MASK if i < 4 else K_MASK + 384)
                    if u >= 2:
                        dve.wait_ge(sem(f"at_tr{l}"), sum(len(local(i2)) + 2 for i2, _ in units[:u - 1]))
                    for c in range(4):
                        hd = 4 * kv + c
                        dve.wait_ge(sem(f"at_sc{l}"), 4 * u + c + 1)
                        pair = ps[:, 2 * (c % 2):2 * (c % 2) + 2, :].rearrange("p b n -> p (b n)")
                        V.tensor_tensor_reduce(s_at[:, u % 2, c, 0:wd], pair[:, SX - nl:SX + SC], K[:, mask:mask + wd], SCALE,
                                               sinkb[:, 8 * l + hd:8 * l + hd + 1], ALU.add, ALU.max,
                                               stats[:, u % 2, c:c + 1]).then_inc(sem(f"at_max{l}"), 1)
                    dve.wait_ge(sem(f"at_max{l}"), 4 * u + 4)
                    ch.link(V.tensor_scalar(stats[:, u % 2, 4:8], stats[:, u % 2, 0:4], -1.0, None, ALU.mult))
                    V.tensor_tensor(stats[:, u % 2, 8:12], sinkb[:, 8 * l + 4 * kv:8 * l + 4 * kv + 4], stats[:, u % 2, 4:8],
                                    ALU.add).then_inc(sem(f"at_nb{l}"), 1)

                def weights(u):
                    i, kv = units[u]
                    wd = P * len(local(i)) + SC
                    dve.wait_ge(sem(f"at_exp{l}"), u + 1)
                    ch.link(V.tensor_tensor(stats[:, u % 2, 16:20], stats[:, u % 2, 16:20], stats[:, u % 2, 12:16], ALU.add))
                    ch.link(V.reciprocal(stats[:, u % 2, 16:20], stats[:, u % 2, 16:20]))
                    for c in range(4):
                        last = V.tensor_scalar(s_at[:, u % 2, c, 0:wd], s_at[:, u % 2, c, 0:wd],
                                               stats[:, u % 2, 16 + c:17 + c], None, ALU.mult)
                    last.then_inc(sem(f"at_p{l}"), 1)

                def rest(u):
                    i, kv = units[u]
                    if kv:
                        dve.wait_ge(sem(f"at_hi{l}"), u // 2 + 1)
                        q = slice(P * i, P * i + P)
                        V.tensor_tensor(zl[:, 2:6, q], ps[:, 7, :].rearrange("p (c q) -> p c q", c=4),
                                        zh[:, 2:6, q].bitcast(F32), ALU.subtract).then_inc(sem(f"at_lo{l}"), 1)

                for u in range(len(units)):
                    scores(u)
                    weights(u)
                    if u:
                        rest(u - 1)
                rest(len(units) - 1)

                for p in range(4):
                    for h in range(2):
                        n = 2 * p + h
                        dve.wait_ge(sem("use_a"), 2 * (A_OUT[l] + p) + h + 1)
                        for c0, c1, s in parts(l == 0):
                            last = V.scalar_tensor_tensor(xT[:, n, c0:c1], ps[:, h + 2 * s, 0:c1 - c0],
                                                          modcol[:, 48 * l + 16 + n, s:s + 1], xT[:, n, c0:c1], ALU.mult, ALU.add)
                        last.then_inc(sem(f"ev_out{l}"), 1)
                dve.wait_ge(sem(f"ev_out{l}"), 8)
                V.memset(stats[:, 0, 0:1], 0.0).then_inc(sem("x_done"), 1)
                norm(2 * l + 1, W)

                V.memset(stats[:, 0, 1:2], 0.0).then_inc(sem(f"ev_h{l}"), 1)
                V.memset(stats[:, 0, 2:3], 0.0).then_inc(sem(f"ev_d{l}"), 1)

                def chunk(s, h, par):
                    n = 2 * s + h
                    per = 2 if l == 0 else 1
                    for c0, c1, sc in parts(l == 0):
                        dve.wait_ge(sem(f"gs_rdy{l}"), per * n + sc + 1)
                        up = ps[:, 3 * h + 1, :] if sc == 0 else ps[:, 3 * h + 2, SC:2 * SC]
                        last = V.tensor_tensor(hf[:, c0:c1], gs[:, c0:c1], up, ALU.mult)
                    last.then_inc(sem(f"ev_h{l}"), 1)
                    dve.wait_ge(sem(f"hh_rdy{l}"), n + 1)
                    V.tensor_tensor(hl[:, par, h, 0:W], hf[:, 0:W], hh[:, par, h, 0:W].bitcast(F32), ALU.subtract
                                    ).then_inc(sem(f"h_rdy{l}"), 1)
                    dve.wait_ge(sem(f"h_rdy{l}"), n + 1)

                def down(s):
                    dve.wait_ge(sem(f"ev_d{l}"), KC * s + 1)
                    for n in range(KC):
                        for c0, c1, sc in parts(l == 0):
                            dve.wait_ge(sem(f"dn{sc}_mm{l}"), KC * s + n + 1)
                            src = ps[:, 6, :] if sc == 0 else ps[:, 7, SC * (n % 2):SC * (n % 2) + SC]
                            last = V.scalar_tensor_tensor(xT[:, n, c0:c1], src, modcol[:, 48 * l + 40 + n, sc:sc + 1],
                                                          xT[:, n, c0:c1], ALU.mult, ALU.add)
                            if sc == 0:
                                last.then_inc(sem(f"ev_d{l}"), 1)
                            else:
                                last.then_inc(sem(f"ev_dc{l}"), 1)

                MODBANK[0] = 6

                def ffn_step(s, par, first=False):
                    chunk(s, 0, par)
                    if l == 0:
                        mod_copy("use_m", 4 * s + 4)
                    chunk(s, 1, par)
                    if l == 0:
                        mod_add(J_FFN + s)
                    if not first:
                        down(s - 1)

                ffn_step(0, 0, first=True)
                ffn_step(1, 1)
                with dve.Fori(0, 4) as i:
                    ffn_step(2 * i + 2, 0)
                    ffn_step(2 * i + 3, 1)
                ffn_step(FSTEPS - 1, 0)
                down(FSTEPS - 1)
                dve.wait_ge(sem(f"ev_d{l}"), KC * FSTEPS + 1)
                if l == 0:
                    dve.wait_ge(sem("ev_dc0"), KC * FSTEPS)
                V.memset(stats[:, 0, 0:1], 0.0).then_inc(sem("x_done"), 1)
                MODBANK[0] = 4
            norm(4, SX)

        @block.tensor
        def _(pe):
            MM, TR = nc.tensor.matmul, nc.tensor.transpose
            MODBANK = [4]

            def mod_half(m, w_hi, w_lo):
                for jj in range(2):
                    j = 2 * m + jj
                    for w in (w_hi, w_lo):
                        last = MM(ps[:, MODBANK[0], :], c4[:, 4 * j:4 * j + P], w[:, 512 * jj:512 * jj + 512],
                                  start=(j == 0 and w is w_hi), stop=(j == 7 and w is w_lo))
                return last

            def mod_finish(J):
                pe.wait_ge(sem("modrow_rdy"), J + 1)
                for i in range(4):
                    last = MM(ps[:, 7, 256 + 2 * i:258 + 2 * i], modrow[0:4, P * i:P * i + P], sel, start=True, stop=True)
                last.then_inc(sem("mod_fin"), 1)

            pe.wait_ge(sem("ld_k"), 16)
            pe.wait_ge(sem("ld_x"), 16)
            pe.wait_ge(sem("ld_ctx"), 16)
            for k in range(KC):
                if k >= 2:
                    pe.wait_ge(sem("xt_evac"), k - 1)
                for t in range(6):
                    dst = ps[:, k % 2, P * t:P * t + P] if t < 4 else ps[:, 2 + k % 2, P * (t - 4):P * (t - 4) + P]
                    last = TR(dst, xin[:, t, P * k:P * k + P], eye)
                last.then_inc(sem("xt_mm"), 1)
            pe.wait_ge(sem("ld_small"), 16 * 18)
            TR(ps[:, 7, 0:N_ROWS], rows_a[:, :], eye[0:N_ROWS, 0:N_ROWS])
            TR(ps[:, 7, N_ROWS:N_ROWS + N_BROWS], rows_b[:, :], eye[0:N_BROWS, 0:N_BROWS]).then_inc(sem("vc_mm"), 1)
            for i in range(8):
                last = TR(ps[:, 5 + i // 4, P * (i % 4):P * (i % 4) + P], cws[:, i, :], eye)
            last.then_inc(sem("ws_mm"), 1)
            pe.wait_ge(sem("c4_rdy"), 1)
            pe.wait_ge(sem("vc_evac"), 1)
            for q in range(8):
                J = q // 2
                pe.wait_ge(sem("st_lo"), q + 1)
                wh_q, wl_q = [(wh[0], wl[0]), (wh[1], wl[1]), (wh_s, wl_s)][q % 3]
                if q % 2 == 0 and J:
                    mod_finish(J - 1)
                for hh_ in range(2):
                    last = mod_half(2 * (q % 2) + hh_, wh_q[:, hh_, :], wl_q[:, hh_, :])
                last.then_inc(sem("st_use"), 1)
            mod_finish(3)

            def norm(u, W):
                pe.wait_ge(sem("nacc_rdy"), 8 * u + 8)
                for c0, c1, s in ([(0, SX, 0)] + ([(SX, NT, 1)] if W == NT else [])):
                    last = MM(ps[:, s, 0:c1 - c0], ones, nacc[:, c0:c1], start=True, stop=True)
                last.then_inc(sem("nst_mm"), 1)
                if u < 4:
                    pe.wait_ge(sem("z_rdy"), 8 * u + 8)

            def panel_half(a, h, ctx):
                pe.wait_ge(sem("loA"), 2 * a + h + 1)
                for c0, c1, s in parts(ctx):
                    for k in range(KC):
                        w = slice(P * k, P * k + P)
                        dst = ps[:, h + 2 * s, 0:c1 - c0]
                        MM(dst, wh[0][:, h, w], zh[:, k, c0:c1], start=(k == 0), stop=False)
                        MM(dst, wh[0][:, h, w], zl[:, k, c0:c1], start=False, stop=False)
                        last = MM(dst, wl[0][:, h, w], zh[:, k, c0:c1], start=False, stop=(k == KC - 1))
                last.then_inc(sem("use_a"), 1)

            for l in range(DEPTH):
                W = NT if l == 0 else SX
                norm(2 * l, NT)

                def in_step(p, ctx, first=False):
                    for h in range(2):
                        if not first:
                            pe.wait_ge(sem(f"ev_in{l}"), 2 * p + h - 1)
                        panel_half(A_IN[l] + p, h, ctx)
                        if l == 0:
                            if h == 0 and not first:
                                mod_finish(J_IN + p - 1)
                            b = 2 * p + h
                            for hh_ in range(2):
                                pe.wait_ge(sem("loB"), 2 * b + hh_ + 1)
                                last = mod_half(2 * h + hh_, wh[1][:, hh_, :], wl[1][:, hh_, :])
                                last.then_inc(sem("use_b"), 1)

                in_step(0, True, first=True)
                with pe.Fori(1, NP_CTX) as p:
                    in_step(p, True)

                def to_tokens(v, slot, ctx, order):
                    pe.wait_ge(sem(f"ev_in{l}"), order)
                    if v:
                        pe.wait_ge(sem(f"vtr_ev{l}"), v)
                    if l == 0:
                        pe.wait_ge(sem("modcol_rdy"), J_IN + (NP_CTX - 1 if v < 3 else NP_IN))
                    for t in range(6 if ctx else 4):
                        dst = ps[:, 5 + (v % 3) % 2, P * t:P * t + P] if t < 4 else ps[:, 7, P * (t - 4):P * (t - 4) + P]
                        last = TR(dst, vT[:, slot, P * t:P * t + P], eye)
                    last.then_inc(sem(f"vtr_mm{l}"), 1)

                for v in range(3):
                    to_tokens(v, v, True, 6)
                pe.wait_ge(sem(f"vtr_ev{l}"), 3)
                with pe.Fori(NP_CTX, NP_IN) as p:
                    in_step(p, l == 0)
                if l == 0:
                    mod_finish(J_IN + NP_IN - 1)
                for v in range(2):
                    to_tokens(3 + v, v, l == 0, 18)

                pe.wait_ge(sem("cm_vn"), l + 1)
                for s in range(2 if l == 0 else 1):
                    for r in range(2):
                        for t in range((4, 2)[s]):
                            for g2 in range(2):
                                cols = (0, SC * r)[s] + P * t
                                last = MM(ps[64 * g2:64 * g2 + 64, (5 + r, 7)[s], cols:cols + P],
                                          cvt[:, 4 * s + t, P * r + HD * g2:P * r + HD * g2 + HD],
                                          wsT[:, l, P * (2 * r + g2):P * (2 * r + g2) + P], start=True, stop=True)
                last.then_inc(sem("cm_mm"), 1)

                jobs = [(h, c, s) for h in range(4) for c, s in
                        [(c, 0) for c in range(6)] + ([(c, 1) for c in (4, 5)] if l == 0 else [])]
                pe.wait_ge(sem(f"rope_done{l}"), 9)
                pe.wait_ge(sem(f"cm_lo{l}"), 4 if l == 0 else 2)

                def score(j):
                    h, c, s = jobs[j]
                    b, r = 64 * (h % 2), h // 2
                    q = slice(0, SX) if s == 0 else slice(SX, NT)
                    if j >= 3:
                        pe.wait_ge(sem(f"ret_p{l}"), j - 2)
                    MM(ps[:, j % 3, 0:q.stop - q.start], rk[b:b + 64, r, P * c:P * c + P], rq[b:b + 64, r, q],
                       start=True, stop=True).then_inc(sem(f"ret_sc{l}"), 1)

                def value(j):
                    h, c, s = jobs[j]
                    b = 64 * (h % 2)
                    n = (SX, SC)[s]
                    first = c == (0, 4)[s]
                    if h == 2 and first and s == 0:
                        pe.wait_ge(sem(f"osb_rdy{l}"), 1)
                    pe.wait_ge(sem(f"ret_p{l}"), j + 1)
                    last = MM(ps[b:b + 64, 5 + s, 0:n], vtok[:, c, HD * h:HD * h + HD], Pm[:, j % 3, 0:n],
                              start=first, stop=(c == 5))
                    last.then_inc(sem(f"ret_pv{l}"), 1)

                for j in range(len(jobs)):
                    score(j)
                    if j >= 2:
                        value(j - 2)
                value(len(jobs) - 2)
                value(len(jobs) - 1)
                for r in range(2):
                    pe.wait_ge(sem(f"osb_rdy{l}"), r + 1)
                    if r:
                        pe.wait_ge(sem(f"gvar_rdy{l}"), r)
                    for c0, c1, s in parts(l == 0):
                        last = MM(ps[:, (7, 4)[s], 0:c1 - c0], blk, osb[:, r, c0:c1], start=True, stop=True)
                    last.then_inc(sem(f"gmean_mm{l}"), 1)
                    pe.wait_ge(sem(f"gsq_rdy{l}"), r + 1)
                    for c0, c1, s in parts(l == 0):
                        last = MM(ps[:, (7, 4)[s], 0:c1 - c0], blk, gsq[:, c0:c1], start=True, stop=True)
                    last.then_inc(sem(f"gvar_mm{l}"), 1)

                blocks = list(range(4)) + ([4, 5] if l == 0 else [])
                units = [(i, kv) for i in blocks for kv in range(2)]
                pe.wait_ge(sem(f"ret_lo{l}"), 2)

                def local(i):
                    return list(range(max(i - 1, 0), min(i + 1, 3) + 1)) if i < 4 else []

                def scores(u):
                    i, kv = units[u]
                    b = 64 * kv
                    loc = local(i)
                    nl = P * len(loc)
                    for c in range(4):
                        if 4 * u + c >= 2:
                            pe.wait_ge(sem(f"at_max{l}"), 4 * u + c - 1)
                        q = aq[b:b + 64, c, P * i:P * i + P]
                        if loc:
                            MM(ps[:, 2 * (c % 2), SX - nl:SX], q, ak[b:b + 64, P * loc[0]:P * loc[0] + nl], start=True, stop=True)
                        MM(ps[:, 2 * (c % 2) + 1, 0:SC], q, ak[b:b + 64, SX:NT], start=True, stop=True).then_inc(sem(f"at_sc{l}"), 1)

                g = 0

                def values(u):
                    nonlocal g
                    i, kv = units[u]
                    chunks = local(i) + [4, 5]
                    pe.wait_ge(sem(f"at_p{l}"), u + 1)
                    g0 = g
                    for kk in range(len(chunks)):
                        if g >= 2:
                            pe.wait_ge(sem(f"at_pt{l}"), g - 1)
                        for c in range(4):
                            last = TR(ps[:, 5 + g % 2, P * c:P * c + P], s_at[:, u % 2, c, P * kk:P * kk + P], eye)
                        last.then_inc(sem(f"at_tr{l}"), 1)
                        g += 1
                    if kv == 0 and i:
                        pe.wait_ge(sem(f"at_lo{l}"), i)
                    for kk, tile in enumerate(chunks):
                        pe.wait_ge(sem(f"at_pt{l}"), g0 + kk + 1)
                        last = MM(ps[64 * kv:64 * kv + 64, 7, :], vtok[:, tile, 256 + HD * kv:256 + HD * kv + HD], pT[:, kk, :],
                                  start=(kk == 0), stop=(kk == len(chunks) - 1))
                    last.then_inc(sem(f"at_o{l}"), 1)

                for u in range(len(units)):
                    scores(u)
                    if u:
                        values(u - 1)
                values(len(units) - 1)

                pe.wait_ge(sem(f"at_lo{l}"), len(blocks))

                def out_step(p, first=False):
                    for h in range(2):
                        if not first:
                            pe.wait_ge(sem(f"ev_out{l}"), 2 * p + h - 1)
                        panel_half(A_OUT[l] + p, h, l == 0)

                out_step(0, first=True)
                with pe.Fori(1, 4) as p:
                    out_step(p)

                norm(2 * l + 1, W)

                MODBANK[0] = 6

                def up_gate(wt_h, wt_l, h, banks):
                    for c0, c1, s in parts(l == 0):
                        dst = banks[s]
                        for k in range(KC):
                            w = slice(P * k, P * k + P)
                            MM(dst, wt_h[:, h, w], zh[:, k, c0:c1], start=(k == 0), stop=False)
                            MM(dst, wt_h[:, h, w], zl[:, k, c0:c1], start=False, stop=False)
                            last = MM(dst, wt_l[:, h, w], zh[:, k, c0:c1], start=False, stop=(k == KC - 1))
                    return last

                def ffn_mod(s, h):
                    for hh_ in range(2):
                        pe.wait_ge(sem("loM"), 4 * s + 2 * h + hh_ + 1)
                        last = mod_half(2 * h + hh_, wh_m[:, hh_, :], wl_m[:, hh_, :])
                        last.then_inc(sem("use_m"), 1)

                def down(s, par):
                    pe.wait_ge(sem(f"loD{l}"), 2 * s + 2)
                    pe.wait_ge(sem(f"h_rdy{l}"), 2 * s + 2)
                    for n in range(KC):
                        w = slice(P * n, P * n + P)
                        for c0, c1, sc in parts(l == 0):
                            if sc == 0:
                                pe.wait_ge(sem(f"ev_d{l}"), KC * s + n + 1)
                            elif n:
                                pe.wait_ge(sem(f"ev_dc{l}"), KC * s + n)
                            dst = ps[:, 6, :] if sc == 0 else ps[:, 7, SC * (n % 2):SC * (n % 2) + SC]
                            for k in range(2):
                                MM(dst, wh_d[:, k, w], hh[:, par, k, c0:c1], start=(k == 0), stop=False)
                                MM(dst, wh_d[:, k, w], hl[:, par, k, c0:c1], start=False, stop=False)
                                last = MM(dst, wl_d[:, k, w], hh[:, par, k, c0:c1], start=False, stop=(k == 1))
                            last.then_inc(sem(f"dn{sc}_mm{l}"), 1)

                def ffn_step(s, par, first=False):
                    a, b = A_GATE[l] + s, B_UP[l] + s
                    for h in range(2):
                        pe.wait_ge(sem("loA"), 2 * a + h + 1)
                        pe.wait_ge(sem(f"ev_h{l}"), 2 * s + h) if not first else None
                        last = up_gate(wh[0], wl[0], h, (ps[:, 3 * h, :], ps[:, 3 * h + 2, 0:SC]))
                        last.then_inc(sem("use_a"), 1)
                        if l == 0 and h:
                            ffn_mod(s, 1)
                        pe.wait_ge(sem("loB"), 2 * b + h + 1)
                        last = up_gate(wh[1], wl[1], h, (ps[:, 3 * h + 1, :], ps[:, 3 * h + 2, SC:2 * SC]))
                        last.then_inc(sem("use_b"), 1)
                        if l == 0 and h == 0:
                            if not first:
                                pe.wait_ge(sem("ev_d0"), KC * (s - 1) + 1)
                            ffn_mod(s, 0)
                    if l == 0:
                        mod_finish(J_FFN + s)
                        pe.wait_ge(sem("modcol_rdy"), J_FFN + s + 1)
                    if not first:
                        down(s - 1, 1 - par)

                ffn_step(0, 0, first=True)
                ffn_step(1, 1)
                with pe.Fori(0, 4) as i:
                    ffn_step(2 * i + 2, 0)
                    ffn_step(2 * i + 3, 1)
                ffn_step(FSTEPS - 1, 0)
                if l == 0:
                    pe.wait_ge(sem("ev_dc0"), KC * (FSTEPS - 1))
                down(FSTEPS - 1, 0)
                MODBANK[0] = 4

            norm(4, SX)
            pe.wait_ge(sem("fz_rdy"), 8)
            for t in range(4):
                for half in range(2):
                    g = 2 * t + half
                    if g >= 2:
                        pe.wait_ge(sem("fin_evac"), g - 1)
                    for i in range(4):
                        last = TR(ps[:, 2 + g % 2, P * i:P * i + P], fz[:, 4 * half + i, P * t:P * t + P], eye)
                    last.then_inc(sem("fin_mm"), 1)


_INS = ['x', 'c', 'ctx', 'c_ctx', 'w_mod', 'b_mod', 'norm1_g', 'norm2_g', 'w_in', 'ret_decay_f', 'ret_decay_b',
        'ret_norm_g', 'attn_sink', 'cm_norm_g', 'cm_w_s', 'cm_b_s', 'w_out', 'w_gate', 'w_up', 'w_down', 'final_norm_g']


def shape_constants():
    import numpy as np
    k = np.zeros((P, K_ALL), np.float32)
    k[:, K_EYE:K_EYE + P] = np.eye(P)
    k[:, K_ONES:K_ONES + P] = 1.0
    for g in range(2):
        k[64 * g:64 * g + 64, K_BLK + 64 * g:K_BLK + 64 * g + 64] = 1.0 / HD
    k[[0, 2], K_SEL] = 1.0
    k[[1, 3], K_SEL + 1] = 1.0
    q, kk = np.arange(P)[:, None], np.arange(384)[None, :]
    band = np.where(np.abs(kk - P - q) <= P, 0.0, MASKED)
    k[:, K_MASK:K_MASK + 384] = band
    k[:, K_MASK3:K_MASK3 + 256] = band[:, 0:256]
    k[:, K_DIST:K_DIST + DIST_W] = np.arange(DIST_W)[None, :] - 384 - q
    pos = np.arange(SX)
    inv = (1.0 / np.float32(10000.0) ** (np.arange(16, dtype=np.float32) / np.float32(16))).astype(np.float32)
    for r in range(P):
        d = r % HD
        at = (pos // 64 if d < 32 else pos % 64).astype(np.float32)
        ang = at * inv[d % 16]
        k[r, K_RC:K_RC + SX] = np.cos(ang)
        k[r, K_RS:K_RS + SX] = np.sin(ang) * (-1.0 if d % 32 < 16 else 1.0)
    return k


def kernel(**inputs):
    import numpy as _np
    import concourse.bacc as _bacc
    from concourse.bass_utils import run_bass_kernel_spmd as _run

    nc = _bacc.Bacc("TRN2", target_bir_lowering=False, num_devices=1, dynamic_dma_scratch_size=1024)
    arrays, args = {}, []
    for name in _INS:
        a = _np.ascontiguousarray(inputs[name])
        arrays[f"in_{name}_dram"] = a
        args.append(nc.dram_tensor(f"in_{name}_dram", a.shape, F32, kind="ExternalInput").ap())
    arrays["consts_dram"] = shape_constants()
    args.append(nc.dram_tensor("consts_dram", (P, K_ALL), F32, kind="ExternalInput").ap())
    args.append(nc.dram_tensor("out_0_dram", (1, SX, D), F32, kind="ExternalOutput").ap())
    trunk(nc, *args)
    r = _run(nc, [arrays], core_ids=[0])
    return r.results[0]["out_0_dram"]
```

```python
from contextlib import ExitStack

import concourse.bass as bass
from concourse import mybir

F32 = mybir.dt.float32
F32R = mybir.dt.float32r
ALU = mybir.AluOpType
ACT = mybir.ActivationFunctionType
AX_X = mybir.AxisListType.X

P = 128
D = 1024
KC = D // P
DEPTH = 2
SX = 512
SC = 256
NT = SX + SC
HD = 64
EPS = 1e-6
SCALE = HD ** -0.5
FFN = 2816
FSTEPS = FFN // 256
IN_W = 2304
MASKED = -1e30

C_RQ, C_RK, C_RV, C_RG, C_AQ, C_AK, C_CU, C_CV = 0, 256, 512, 768, 1024, 1536, 1792, 2048
PANELS = ["rv", "rk", "akav", "rq", "cv", "cu", "aq0", "aq1", "rg"]
PANEL_COL = {"rv": C_RV, "rk": C_RK, "akav": C_AK, "rq": C_RQ, "cv": C_CV, "cu": C_CU, "rg": C_RG}
NP_IN = len(PANELS)
NP_CTX = 3

R_N1, R_N2, R_NF, R_RN, R_CN, N_ROWS = 0, 16, 32, 40, 44, 48
N_BROWS = DEPTH * 48

K_EYE, K_ONES, K_BLK, K_SEL, K_MASK, K_MASK3, K_DIST, K_RC, K_RS = 0, 128, 256, 384, 386, 1026, 1538, 2434, 2946
K_ALL = 3458
DIST_W = 896


class Chain:

    def __init__(self, eng, sem):
        self.eng, self.sem, self.n, self.shift = eng, sem, 0, 0

    def then(self, ins):
        ins.then_inc(self.sem, 1)
        self.n += 1
        return ins

    def wait(self):
        self.eng.wait_ge(self.sem, self.n + self.shift)

    def link(self, ins):
        self.then(ins)
        self.wait()
        return ins


def trunk(nc, x, c, ctx_in, c_ctx, w_mod, b_mod, norm1_g, norm2_g, w_in, ret_decay_f, ret_decay_b, ret_norm_g,
          attn_sink, cm_norm_g, cm_w_s, cm_b_s, w_out, w_gate, w_up, w_down, final_norm_g, consts, out):
    stack = ExitStack()
    with stack:
        def sb(name, shape, dt=F32):
            return stack.enter_context(nc.sbuf_tensor(name, shape, dt))

        sems = {}

        def sem(name):
            if name not in sems:
                sems[name] = stack.enter_context(nc.semaphore(name))
            return sems[name]

        def overlay(specs, under=()):
            with ExitStack() as phase:
                for name, shape, dt in list(under) + list(specs):
                    t = phase.enter_context(nc.sbuf_tensor(name, shape, dt))
                    made[name] = t
            return [made[s[0]] for s in specs if not s[0].startswith("n")]

        made = {}

        K = sb("consts_sb", [P, K_ALL])
        xT = sb("xT", [P, KC, NT])
        zh = sb("zh", [P, KC, NT], F32R)
        zl = sb("zl", [P, KC, NT], F32R)
        raw = [sb(f"raw{i}", [P, 2048]) for i in range(2)]
        wh = [sb(f"wh{i}", [P, 2, 1024], F32R) for i in range(2)]
        wl = [sb(f"wl{i}", [P, 2, 1024], F32R) for i in range(2)]
        wsT = sb("wsT", [P, DEPTH, 512])
        bsb = sb("bsb", [P, DEPTH, 2, P])
        vcol = sb("vcol", [P, N_ROWS + N_BROWS])
        modcol = sb("modcol", [P, DEPTH * 48, 2])
        acol = sb("acol", [P, KC, 2])
        modrow = sb("modrow", [4, 512])
        c4 = sb("c4", [P, 4 * KC + P], F32R)
        c4j = c4[:, 0:4 * KC].rearrange("p (j s) -> p j s", s=4)
        lg = sb("lg", [P, 16])
        nlg = sb("nlg", [P, 16])
        blg = sb("blg", [P, 16])
        sinkb = sb("sinkb", [P, DEPTH * 8])
        stats = sb("stats", [P, 2, 20])

        eye = K[:, K_EYE:K_EYE + P]
        ones = K[:, K_ONES:K_ONES + P]
        blk = K[:, K_BLK:K_BLK + P]
        sel = K[0:4, K_SEL:K_SEL + 2]
        dist = K[:, K_DIST:K_DIST + DIST_W]
        ropeC = K[:, K_RC:K_RC + SX]
        ropeS = K[:, K_RS:K_RS + SX]

        xin, raw_s, wh_s, wl_s, crow, cws, rows_a, rows_b, csil, dec, lt1, lt2, lt3 = overlay([
            ("xin", [P, 6, D], F32), ("raw_s", [P, 2048], F32), ("wh_s", [P, 2, 1024], F32R),
            ("wl_s", [P, 2, 1024], F32R), ("crow", [P, 2, KC], F32), ("cws", [P, DEPTH * 4, P], F32),
            ("rows_a", [N_ROWS, P], F32), ("rows_b", [N_BROWS, P], F32), ("csil", [P, KC, 2], F32),
            ("dec", [P, 16], F32), ("lt1", [P, 16], F32), ("lt2", [P, 16], F32), ("lt3", [P, 16], F32),
            ("nsq_s", [P, 2, NT], F32), ("nacc_s", [P, NT], F32), ("nrb_s", [P, NT], F32), ("nxz_s", [P, 3, NT], F32)])
        xr_start = xin[:, :, :].rearrange("p t d -> p (t d)").rearrange("p (k n) -> p k n", k=KC)
        norm_start = tuple(made[n] for n in ("nsq_s", "nacc_s", "nrb_s", "nxz_s"))
        norm_bufs = [("pad_a", [P, 2, NT], F32), ("nsq", [P, 2, NT], F32), ("nrb", [P, NT], F32), ("pad_b", [P, NT], F32),
                     ("nacc", [P, NT], F32), ("nxz", [P, 3, NT], F32)]
        overlay(norm_bufs)
        norm_later = tuple(made[n] for n in ("nsq", "nacc", "nrb", "nxz"))
        Z_DVE = (0, 4)
        Z_POOL = tuple(k for k in range(KC) if k not in Z_DVE)
        attn_base = [("aq", [P, 4, NT], F32), ("ak", [P, NT], F32), ("vtok", [P, 6, 384], F32)]
        mix_base = attn_base + [("rq", [P, 2, NT], F32), ("rk", [P, 2, NT], F32), ("rg", [P, 2, NT], F32),
                                ("cu", [P, 2, NT], F32)]
        mixers = mix_base + [("cvt", [P, 6, 256], F32), ("vT", [P, 3, NT], F32), ("rtmp", [P, 2, SX], F32),
                             ("shuf", [P, SX], F32), ("cmst", [P, 2, 24], F32)]
        aq, ak, vtok, rq, rk, rg, cu, cvt, vT, rtmp, shuf, cmst = overlay(mixers)
        cmf = rtmp
        cmsq = vT[:, 0:2, :].rearrange("p a (t n) -> p (a t) n", n=256)
        T, TC, TD, Pm, osb = overlay([
            ("T", [P, 2, DIST_W], F32), ("TC", [P, 2, 640], F32), ("TD", [P, 640], F32), ("Pm", [P, 3, SX], F32),
            ("osb", [P, 2, NT], F32)],
            under=[(n + "_r", s, d) for n, s, d in mix_base])
        oc, gsq = T[:, 0, 0:NT], T[:, 1, 0:NT]
        s_at, pT = overlay([("s_at", [P, 2, 4, 640], F32), ("pT", [P, 5, SX], F32)],
                           under=[(n + "_a", s, d) for n, s, d in attn_base])
        hh, hl, gs, hf, raw_d, raw_m, wh_d, wl_d, wh_m, wl_m = overlay([
            ("hh", [P, 2, 2, NT], F32R), ("hl", [P, 2, 2, NT], F32R), ("gs", [P, NT], F32), ("hf", [P, NT], F32),
            ("raw_d", [P, 2048], F32), ("raw_m", [P, 2048], F32), ("wh_d", [P, 2, 1024], F32R),
            ("wl_d", [P, 2, 1024], F32R), ("wh_m", [P, 2, 1024], F32R), ("wl_m", [P, 2, 1024], F32R)])
        fz, = overlay([("fz", [P, KC, SX], F32)], under=[(n + "_f", s, d) for n, s, d in norm_bufs])
        otok, = overlay([("otok", [P, 4, D], F32)],
                        under=[(n + "_g", s, d) for n, s, d in norm_bufs] + [("fz_g", [P, KC, SX], F32)])

        ps = stack.enter_context(nc.psum_tensor("ps", [P, 8, 512], F32))

        def parts(l_or_w):
            return [(0, SX, 0)] + ([(SX, NT, 1)] if l_or_w else [])

        mod_v = [w_mod[l].rearrange("(p j) n -> p j n", j=KC) for l in range(DEPTH)]
        win_v = [w_in[l].rearrange("(k p) n -> p k n", p=P) for l in range(DEPTH)]
        wout_v = [w_out[l].rearrange("(k p) n -> p k n", p=P) for l in range(DEPTH)]
        gate_v = [w_gate[l].rearrange("(k p) n -> p k n", p=P) for l in range(DEPTH)]
        up_v = [w_up[l].rearrange("(k p) n -> p k n", p=P) for l in range(DEPTH)]
        down_v = [w_down[l].rearrange("(k p) n -> p k n", p=P) for l in range(DEPTH)]

        A_IN = [0, NP_IN + 4 + FSTEPS]
        A_OUT = [a + NP_IN for a in A_IN]
        A_GATE = [a + 4 for a in A_OUT]
        N_MODB = 2 * NP_IN
        B_UP = [N_MODB, N_MODB + FSTEPS]
        J_IN, J_FFN = 4, 4 + NP_IN

        def z_wait(eng, u, k):
            if k in Z_DVE:
                eng.wait_ge(sem("z_dve"), len(Z_DVE) * u + Z_DVE.index(k) + 1)
            else:
                eng.wait_ge(sem("z_pool"), len(Z_POOL) * u + Z_POOL.index(k) + 1)

        block = stack.enter_context(nc.Block())

        @block.sync
        def _(sp):
            def startup_panel(q):
                dst = [raw[0], raw[1], raw_s][q % 3]
                J, half = q // 2, q % 2
                sp.dma_start(dst[:, :].rearrange("p (j n) -> p j n", j=4),
                             mod_v[0][:, 4 * half:4 * half + 4, 512 * J:512 * J + 512]).then_inc(sem(f"st_ld{q % 3}"), 16)

            sp.dma_start(crow[:, 0, :], c[0].rearrange("(p j) -> p j", j=KC)).then_inc(sem("ld_c"), 16)
            sp.dma_start(crow[:, 1, :], c_ctx.rearrange("(p j) -> p j", j=KC)).then_inc(sem("ld_c"), 16)
            sp.dma_start(K[:, :], consts).then_inc(sem("ld_k"), 16)
            sp.dma_start(xin[:, 0:4, :], x[0].rearrange("(t p) d -> p t d", p=P)).then_inc(sem("ld_x"), 16)
            for q in range(3):
                startup_panel(q)
            sp.dma_start(xin[:, 4:6, :], ctx_in[0].rearrange("(t p) d -> p t d", p=P)).then_inc(sem("ld_ctx"), 16)
            rows = 0
            for v, n in ((norm1_g.rearrange("l (k p) -> (l k) p", p=P), 16), (norm2_g.rearrange("l (k p) -> (l k) p", p=P), 16),
                         (final_norm_g.rearrange("(k p) -> k p", p=P), 8), (ret_norm_g.rearrange("l (k p) -> (l k) p", p=P), 4),
                         (cm_norm_g.rearrange("l (k p) -> (l k) p", p=P), 4)):
                sp.dma_start(rows_a[rows:rows + n, :], v).then_inc(sem("ld_small"), 16)
                rows += n
            sp.dma_start(rows_b[:, :], b_mod.rearrange("l (k p) -> (l k) p", p=P)).then_inc(sem("ld_small"), 16)
            sp.dma_start(dec[:, 0:8], ret_decay_f.rearrange("l h -> (l h)").partition_broadcast(P)).then_inc(sem("ld_small"), 16)
            sp.dma_start(dec[:, 8:16], ret_decay_b.rearrange("l h -> (l h)").partition_broadcast(P)).then_inc(sem("ld_small"), 16)
            sp.dma_start(sinkb[:, :], attn_sink.rearrange("l h -> (l h)").partition_broadcast(P)).then_inc(sem("ld_small"), 16)
            sp.dma_start(cws[:, :, :], cm_w_s.rearrange("l g p q -> p (l g) q")).then_inc(sem("ld_small"), 16)
            for l in range(DEPTH):
                for g in range(4):
                    sp.dma_start(bsb[64 * (g % 2):64 * (g % 2) + 64, l, g // 2, :],
                                 cm_b_s[l, g].partition_broadcast(64)).then_inc(sem("ld_small"), 16)
            for q in range(3, 8):
                sp.wait_ge(sem("st_hi"), q - 2)
                sp.wait_ge(sem("st_lo"), q - 2)
                startup_panel(q)

            def a_free(a, first=False):
                sp.wait_ge(sem("st_hi" if first else "hiA"), 7 if first else 2 * a)
                sp.wait_ge(sem("st_lo" if first else "loA"), 7 if first else 2 * a)

            def b_free(b, first=False):
                if first:
                    sp.wait_ge(sem("st_hi"), 8)
                    sp.wait_ge(sem("st_lo"), 8)
                else:
                    sp.wait_ge(sem("hiB"), 2 * b)
                    sp.wait_ge(sem("lo_modb"), 2 * b)

            def load_in(l, p):
                a_free(A_IN[l] + p, first=(l == 0 and p == 0))
                dst = raw[0][:, :].rearrange("p (k n) -> p k n", k=KC)
                name = PANELS[p]
                if name.startswith("aq"):
                    for h in range(2):
                        q = 2 * int(name[2]) + h
                        for part in range(2):
                            col = C_AQ + HD * (q + 4 * part)
                            at = P * h + HD * part
                            sp.dma_start(dst[:, :, at:at + HD], win_v[l][:, :, col:col + HD]).then_inc(sem(f"ld_in{l}"), 16)
                else:
                    sp.dma_start(dst, win_v[l][:, :, PANEL_COL[name]:PANEL_COL[name] + 256]).then_inc(sem(f"ld_in{l}"), 16)

            def load_modb(b):
                b_free(b, first=(b == 0))
                J, half = J_IN + b // 2, b % 2
                l, Jl = J // 12, J % 12
                sp.dma_start(raw[1][:, :].rearrange("p (j n) -> p j n", j=4),
                             mod_v[l][:, 4 * half:4 * half + 4, 512 * Jl:512 * Jl + 512]).then_inc(sem("ld_modb"), 16)

            def load_out(l, p):
                a_free(A_OUT[l] + p)
                dst = raw[0][:, :].rearrange("p (k n) -> p k n", k=KC)
                cols = slice(256 * p, 256 * p + 256)
                sp.dma_start(dst[:, 0:2, :], wout_v[l][:, 0:2, cols]).then_inc(sem(f"ld_out{l}"), 16)
                for part in range(2):
                    rows = w_out[l, 256 + 256 * part:512 + 256 * part, cols].rearrange("(k p) n -> p k n", p=HD)
                    sp.dma_start(dst[64 * part:64 * part + 64, 2:6, :], rows).then_inc(sem(f"ld_out{l}"), 16)
                sp.dma_start(dst[:, 6:8, :], wout_v[l][:, 6:8, cols]).then_inc(sem(f"ld_out{l}"), 16)

            def load_ffn(l, s):
                a_free(A_GATE[l] + s)
                sp.dma_start(raw[0][:, :].rearrange("p (k n) -> p k n", k=KC),
                             gate_v[l][:, :, bass.ds(256 * s, 256)]).then_inc(sem(f"ld_gate{l}"), 16)
                up = FSTEPS * l + s
                if type(up) is int and up == 0:
                    sp.wait_ge(sem("lo_modb"), 2 * N_MODB)
                else:
                    sp.wait_ge(sem("loB"), 2 * up)
                sp.dma_start(raw[1][:, :].rearrange("p (k n) -> p k n", k=KC),
                             up_v[l][:, :, bass.ds(256 * s, 256)]).then_inc(sem(f"ld_up{l}"), 16)

            def load_down(l, s, first=False):
                if not first:
                    sp.wait_ge(sem(f"hiD{l}"), 2 * s)
                    sp.wait_ge(sem(f"loD{l}"), 2 * s)
                sp.dma_start(raw_d[:, :].rearrange("p (k n) -> p k n", k=2),
                             down_v[l][:, bass.ds(2 * s, 2), :]).then_inc(sem(f"ld_down{l}"), 16)

            def load_modm(s, half, first=False):
                if not first:
                    sp.wait_ge(sem("hiM"), 4 * s + 2 * half)
                    sp.wait_ge(sem("loM"), 4 * s + 2 * half)
                sp.dma_start(raw_m[:, :].rearrange("p (j n) -> p j n", j=4),
                             mod_v[1][:, 4 * half:4 * half + 4, bass.ds(512 * (s + 1), 512)]).then_inc(sem("ld_modm"), 16)

            load_in(0, 0)
            load_modb(0)
            for p in range(NP_IN):
                load_modb(2 * p + 1)
                if p + 1 < NP_IN:
                    load_in(0, p + 1)
                    load_modb(2 * p + 2)
            for l in range(DEPTH):
                if l:
                    for p in range(NP_IN):
                        load_in(l, p)
                for p in range(4):
                    load_out(l, p)
                load_ffn(l, 0)
                sp.wait_ge(sem("use_a"), 2 * A_GATE[l])
                load_down(l, 0, first=True)
                if l == 0:
                    load_modm(0, 0, first=True)
                    load_modm(0, 1)
                with sp.Fori(1, FSTEPS) as s:
                    load_ffn(l, s)
                    if l == 0:
                        load_modm(s, 0)
                        load_modm(s, 1)
                    load_down(l, s)

            for g in range(8):
                half, t = g // 4, g % 4
                sp.wait_ge(sem("fin_evac"), g + 1)
                sp.dma_start(out[0, P * t:P * t + P, 512 * half:512 * half + 512],
                             otok[:, t, 512 * half:512 * half + 512]).then_inc(sem("stored"), 16)
            sp.wait_ge(sem("stored"), 16 * 8)

        @block.gpsimd
        def _(pool):
            def lo(dst, src, hi, done):
                nc.gpsimd.tensor_tensor(dst, src, hi.bitcast(F32), ALU.subtract).then_inc(sem(done), 1)

            def raw_half(buf, h):
                return buf[:, :].rearrange("p (k j n) -> p j k n", k=KC, j=2)[:, h]

            def slot_half(t, h):
                return t[:, h, :].rearrange("p (k n) -> p k n", k=KC)

            def lo_a(a, h):
                pool.wait_ge(sem("hiA"), 2 * a + h + 1)
                lo(slot_half(wl[0], h), raw_half(raw[0], h), slot_half(wh[0], h), "loA")

            def lo_b(b, h):
                pool.wait_ge(sem("hiB"), 2 * b + h + 1)
                lo(slot_half(wl[1], h), raw_half(raw[1], h), slot_half(wh[1], h), "loB")

            def lo_modm(m, h):
                pool.wait_ge(sem("hiM"), m + 1)
                lo(wl_m[:, h, :], raw_m[:, 1024 * h:1024 * h + 1024], wh_m[:, h, :], "loM")

            def lo_down(l, s):
                for h in range(2):
                    pool.wait_ge(sem(f"hiD{l}"), 2 * s + h + 1)
                    lo(wl_d[:, h, :], raw_d[:, 1024 * h:1024 * h + 1024], wh_d[:, h, :], f"loD{l}")

            def norm(u, W):
                nxz = (norm_later if u else norm_start)[3]
                for k in Z_POOL:
                    pool.wait_ge(sem("nzf_rdy"), 8 * u + k + 1)
                    pool.wait_ge(sem("zh_rdy"), 8 * u + k + 1)
                    lo(zl[:, k, 0:W], nxz[:, k % 3, 0:W], zh[:, k, 0:W], "z_pool")

            lo_a(0, 0)
            lo_a(0, 1)
            norm(0, NT)
            with pool.Fori(1, NP_IN + 1) as a:
                lo_a(a, 0)
                lo_a(a, 1)
            for l in range(DEPTH):
                if l:
                    norm(2, NT)
                    with pool.Fori(A_IN[l] + 1, A_OUT[l] + 1) as a:
                        lo_a(a, 0)
                        lo_a(a, 1)
                with pool.Fori(A_OUT[l] + 1, A_GATE[l] + 1) as a:
                    lo_a(a, 0)
                    lo_a(a, 1)
                lo_b(B_UP[l], 0)
                lo_b(B_UP[l], 1)
                norm(2 * l + 1, NT if l == 0 else SX)
                if l == 0:
                    lo_modm(0, 0)
                    lo_modm(1, 1)

                def ffn_step(s, first=False, last=False):
                    if not first:
                        lo_down(l, s - 1)
                    for h in range(2):
                        if not (last and l):
                            lo_a(A_GATE[l] + s + 1, h)
                        if not last:
                            lo_b(B_UP[l] + s + 1, h)
                        if l == 0 and not (last and h):
                            lo_modm(4 * s + 2 * h + 2, 0)
                            lo_modm(4 * s + 2 * h + 3, 1)

                ffn_step(0, first=True)
                with pool.Fori(1, FSTEPS - 1) as s:
                    ffn_step(s)
                ffn_step(FSTEPS - 1, last=True)
                lo_down(l, FSTEPS - 1)

        @block.scalar
        def _(act):
            ch = Chain(act, sem("act_chain"))

            def copy(dst, src):
                return nc.scalar.activation(dst, src, ACT.Copy)

            def raw_half(buf, h):
                return buf[:, :].rearrange("p (k j n) -> p j k n", k=KC, j=2)[:, h]

            def slot_half(t, h):
                return t[:, h, :].rearrange("p (k n) -> p k n", k=KC)

            def hi_a(a, h, loaded, value, first=False):
                act.wait_ge(sem(loaded), value)
                if first:
                    act.wait_ge(sem("st_use"), 7)
                else:
                    act.wait_ge(sem("use_a"), 2 * a + h - 1)
                copy(slot_half(wh[0], h), raw_half(raw[0], h)).then_inc(sem("hiA"), 1)

            def hi_modb(b, h, first=False):
                act.wait_ge(sem("ld_modb"), 16 * (b + 1))
                if first:
                    act.wait_ge(sem("st_use"), 8)
                else:
                    act.wait_ge(sem("use_b"), 2 * b + h - 1)
                copy(wh[1][:, h, :], raw[1][:, 1024 * h:1024 * h + 1024]).then_inc(sem("hiB"), 1)

            def hi_b(l, s, h):
                act.wait_ge(sem(f"ld_up{l}"), 16 * (s + 1))
                act.wait_ge(sem("use_b"), 2 * (B_UP[l] + s) + h - 1)
                copy(slot_half(wh[1], h), raw_half(raw[1], h)).then_inc(sem("hiB"), 1)

            def hi_modm(m, h, first=False, panel=None):
                act.wait_ge(sem("ld_modm"), 16 * (panel + 1))
                if not first:
                    act.wait_ge(sem("use_m"), m - 1)
                copy(wh_m[:, h, :], raw_m[:, 1024 * h:1024 * h + 1024]).then_inc(sem("hiM"), 1)

            def hi_down(l, s, first=False):
                act.wait_ge(sem(f"ld_down{l}"), 16 * (s + 1))
                if not first:
                    act.wait_ge(sem("dn1_mm0" if l == 0 else "dn0_mm1"), KC * s)
                elif l:
                    act.wait_ge(sem("dn1_mm0"), KC * FSTEPS)
                for h in range(2):
                    copy(wh_d[:, h, :], raw_d[:, 1024 * h:1024 * h + 1024]).then_inc(sem(f"hiD{l}"), 1)

            def square(u, k, W):
                nsq = (norm_later if u else norm_start)[0]
                if k >= 2:
                    act.wait_ge(sem("nacc_rdy"), 8 * u + k - 1)
                nc.scalar.activation(nsq[:, k % 2, 0:W], xT[:, k, 0:W], ACT.Square).then_inc(sem("nsq_rdy"), 1)

            def norm_root(u, W):
                nrb = (norm_later if u else norm_start)[2]
                act.wait_ge(sem("nvar_rdy"), u + 1)
                nc.scalar.activation(nrb[:, 0:W], nrb[:, 0:W], ACT.Sqrt).then_inc(sem("nrms_rdy"), 1)

            def norm_hi(u, W):
                nxz = (norm_later if u else norm_start)[3]
                for k in range(KC):
                    act.wait_ge(sem("nzf_rdy"), 8 * u + k + 1)
                    copy(zh[:, k, 0:W], nxz[:, k % 3, 0:W]).then_inc(sem("zh_rdy"), 1)

            act.wait_ge(sem("ld_c"), 32)
            ch.link(nc.scalar.activation(csil[:, :, 0], crow[:, 0, :], ACT.Silu))
            nc.scalar.activation(csil[:, :, 1], crow[:, 1, :], ACT.Silu).then_inc(sem("csil_rdy"), 1)
            for q in range(3):
                act.wait_ge(sem(f"st_ld{q}"), 16)
                copy([wh[0], wh[1], wh_s][q][:, :, :].rearrange("p h n -> p (h n)"),
                     [raw[0], raw[1], raw_s][q][:, :]).then_inc(sem("st_hi"), 1)
            for k in range(KC):
                act.wait_ge(sem("xt_mm"), k + 1)
                copy(xT[:, k, 0:SX], ps[:, k % 2, :])
                copy(xT[:, k, SX:NT], ps[:, 2 + k % 2, 0:SC]).then_inc(sem("xt_evac"), 1)
                if k:
                    act.wait_ge(sem("xt_evac"), k)
                    square(0, k - 1, NT)
            act.wait_ge(sem("xt_evac"), KC)
            square(0, KC - 1, NT)
            act.wait_ge(sem("ws_mm"), 1)
            for l in range(DEPTH):
                copy(wsT[:, l, :], ps[:, 5 + l, :]).then_inc(sem("ws_evac"), 1)
            for q in range(3, 8):
                act.wait_ge(sem(f"st_ld{q % 3}"), 16 * (q // 3 + 1))
                act.wait_ge(sem("st_use"), q - 2)
                copy([wh[0], wh[1], wh_s][q % 3][:, :, :].rearrange("p h n -> p (h n)"),
                     [raw[0], raw[1], raw_s][q % 3][:, :]).then_inc(sem("st_hi"), 1)
                if q == 3:
                    norm_root(0, NT)
                if q == 4:
                    act.wait_ge(sem("lg_ax"), 1)
                    nc.scalar.activation(lt2[:, :], lt1[:, :], ACT.Exp, scale=-1.0).then_inc(sem("lg_e"), 1)

            for l in range(DEPTH):
                W = NT if l == 0 else SX

                ld = [0]
                for name in PANELS:
                    ld.append(ld[-1] + (64 if name.startswith("aq") else 16))
                if l == 0:
                    hi_a(0, 0, "ld_in0", ld[1], first=True)
                    hi_a(0, 1, "ld_in0", ld[1], first=True)
                    norm_hi(0, NT)
                    hi_modb(0, 0, first=True)
                    hi_modb(0, 1, first=True)
                else:
                    norm_hi(2, NT)
                a0 = A_IN[l]
                rope_n = 0
                for p, name in enumerate(PANELS):
                    for h in range(2):
                        n = 2 * p + h
                        act.wait_ge(sem("use_a"), 2 * (a0 + p) + h + 1)
                        if p + 1 < NP_IN:
                            hi_a(a0 + p + 1, h, f"ld_in{l}", ld[p + 2])
                        else:
                            hi_a(a0 + p + 1, h, f"ld_out{l}", 64)
                        ctx = l == 0 or p < NP_CTX
                        px, pc = ps[:, h, :], ps[:, 2 + h, 0:SC]
                        is_rope = name in ("rk", "rq", "aq0", "aq1") or (name == "akav" and h == 0)
                        if is_rope:
                            dst = {"rk": rk[:, h], "rq": rq[:, h], "akav": ak, "aq0": aq[:, h], "aq1": aq[:, 2 + h]}[name]
                            if ctx:
                                copy(dst[:, SX:NT], pc)
                            if rope_n >= 2:
                                act.wait_ge(sem(f"rope_done{l}"), rope_n - 1)
                            copy(rtmp[:, rope_n % 2, :], px).then_inc(sem(f"ev_in{l}"), 1)
                            rope_n += 1
                        else:
                            func = {"cv": ACT.Gelu_apprx_tanh, "cu": ACT.Gelu_apprx_tanh, "rg": ACT.Silu}.get(name, ACT.Copy)
                            dst = {"rv": vT[:, h], "akav": vT[:, 2], "cv": vT[:, h], "cu": cu[:, h], "rg": rg[:, h]}[name]
                            if name == "cv" and h == 0:
                                act.wait_ge(sem(f"vtr_mm{l}"), 3)
                            if ctx:
                                nc.scalar.activation(dst[:, SX:NT], pc, func)
                            nc.scalar.activation(dst[:, 0:SX], px, func).then_inc(sem(f"ev_in{l}"), 1)
                        if l == 0 and h == 0:
                            hi_modb(2 * p + 1, 0)
                            hi_modb(2 * p + 1, 1)
                        if l == 0 and h == 1 and p + 1 < NP_IN:
                            hi_modb(2 * p + 2, 0)
                            hi_modb(2 * p + 2, 1)
                    if p == NP_CTX - 1:
                        for v in range(3):
                            act.wait_ge(sem(f"vtr_mm{l}"), v + 1)
                            cols = slice(P * v, P * v + P)
                            copy(vtok[:, 4:6, cols], ps[:, 7, 0:SC].rearrange("p (t n) -> p t n", t=2))
                            copy(vtok[:, 0:4, cols], ps[:, 5 + v % 2, :].rearrange("p (t n) -> p t n", t=4)).then_inc(sem(f"vtr_ev{l}"), 1)
                for v in range(2):
                    act.wait_ge(sem(f"vtr_mm{l}"), 4 + v)
                    cols = slice(P * v, P * v + P)
                    if l == 0:
                        copy(cvt[:, 4:6, cols], ps[:, 7, 0:SC].rearrange("p (t n) -> p t n", t=2))
                    copy(cvt[:, 0:4, cols], ps[:, 5 + v % 2, :].rearrange("p (t n) -> p t n", t=4)).then_inc(sem(f"vtr_ev{l}"), 1)

                nt = W // P
                act.wait_ge(sem("cm_var"), l + 1)
                nc.scalar.activation(cmst[:, 1, 0:4 * nt], cmst[:, 1, 0:4 * nt], ACT.Sqrt).then_inc(sem("cm_std"), 1)
                e = 0
                for c0, c1, s in parts(l == 0):
                    for r in range(2):
                        act.wait_ge(sem(f"cm_f{l}"), e + 1)
                        copy(zh[:, 6 + r, c0:c1], cmf[:, e % 2, 0:c1 - c0]).then_inc(sem(f"cm_hi{l}"), 1)
                        e += 1

                for h in range(4):
                    act.wait_ge(sem(f"T_arg{l}"), h + 1)
                    i, b = l * 4 + h, h % 2
                    nc.scalar.activation(T[:, b, :], T[:, b, :], ACT.Exp)
                    nc.scalar.activation(TC[:, b, :], dist[:, 0:640], ACT.Exp, bias=blg[:, i:i + 1], scale=lg[:, i:i + 1])
                    if h:
                        act.wait_ge(sem(f"T_done{l}"), h)
                    nc.scalar.activation(TD[:, :], dist[:, 0:640], ACT.Exp, bias=blg[:, 8 + i:9 + i],
                                         scale=nlg[:, 8 + i:9 + i]).then_inc(sem(f"T_exp{l}"), 1)
                    if h % 2:
                        r = h // 2
                        act.wait_ge(sem(f"ret_pv{l}"), (r + 1) * (16 if l == 0 else 12))
                        if l == 0:
                            copy(osb[:, r, SX:NT], ps[:, 6, 0:SC])
                        copy(osb[:, r, 0:SX], ps[:, 5, :]).then_inc(sem(f"osb_rdy{l}"), 1)
                for r in range(2):
                    act.wait_ge(sem(f"oc_rdy{l}"), r + 1)
                    nc.scalar.activation(gsq[:, 0:W], oc[:, 0:W], ACT.Square).then_inc(sem(f"gsq_rdy{l}"), 1)
                    act.wait_ge(sem(f"gvar_rdy{l}"), r + 1)
                    nc.scalar.activation(gsq[:, 0:W], gsq[:, 0:W], ACT.Sqrt).then_inc(sem(f"gstd_rdy{l}"), 1)
                    act.wait_ge(sem(f"ret_f{l}"), r + 1)
                    copy(zh[:, r, 0:W], oc[:, 0:W]).then_inc(sem(f"ret_hi{l}"), 1)

                blocks = list(range(4)) + ([4, 5] if l == 0 else [])
                units = [(i, kv) for i in blocks for kv in range(2)]
                g = 0

                def softmax(u):
                    i, kv = units[u]
                    wd = len(local(i)) * P + SC
                    act.wait_ge(sem(f"at_nb{l}"), u + 1)
                    nc.scalar.activation(stats[:, u % 2, 12:16], stats[:, u % 2, 8:12], ACT.Exp)
                    for c in range(4):
                        last = nc.scalar.activation(s_at[:, u % 2, c, 0:wd], s_at[:, u % 2, c, 0:wd], ACT.Exp,
                                                    bias=stats[:, u % 2, 4 + c:5 + c],
                                                    accum_out=stats[:, u % 2, 16 + c:17 + c])
                    last.then_inc(sem(f"at_exp{l}"), 1)

                def local(i):
                    return list(range(max(i - 1, 0), min(i + 1, 3) + 1)) if i < 4 else []

                def after(u):
                    nonlocal g
                    i, kv = units[u]
                    for kk in range(len(local(i)) + 2):
                        act.wait_ge(sem(f"at_tr{l}"), g + 1)
                        if kk == 0 and u:
                            act.wait_ge(sem(f"at_o{l}"), u)
                        copy(pT[:, kk, :], ps[:, 5 + g % 2, :]).then_inc(sem(f"at_pt{l}"), 1)
                        g += 1
                    if kv == 1:
                        act.wait_ge(sem(f"at_o{l}"), u + 1)
                        copy(zh[:, 2:6, P * i:P * i + P], ps[:, 7, :].rearrange("p (c q) -> p c q", c=4)).then_inc(sem(f"at_hi{l}"), 1)

                for u in range(len(units)):
                    softmax(u)
                    if u:
                        after(u - 1)
                after(len(units) - 1)

                for p in range(4):
                    for h in range(2):
                        a = A_OUT[l] + p + 1
                        if p < 3:
                            hi_a(a, h, f"ld_out{l}", 64 * (p + 2))
                        else:
                            hi_a(a, h, f"ld_gate{l}", 16)
                        if p or h:
                            act.wait_ge(sem(f"ev_out{l}"), 2 * p + h)
                            square(2 * l + 1, 2 * p + h - 1, W)
                act.wait_ge(sem(f"ev_out{l}"), KC)
                square(2 * l + 1, KC - 1, W)
                norm_root(2 * l + 1, W)
                for h in range(2):
                    hi_b(l, 0, h)
                norm_hi(2 * l + 1, W)
                if l == 0:
                    hi_modm(0, 0, first=True, panel=0)
                    hi_modm(1, 1, first=True, panel=0)

                def chunk(s, h, par):
                    n = 2 * s + h
                    act.wait_ge(sem("use_b"), 2 * (B_UP[l] + s) + h + 1)
                    act.wait_ge(sem(f"ev_h{l}"), n + 1)
                    nc.scalar.activation(gs[:, 0:SX], ps[:, 3 * h, :], ACT.Silu).then_inc(sem(f"gs_rdy{l}"), 1)
                    if l == 0:
                        nc.scalar.activation(gs[:, SX:NT], ps[:, 3 * h + 2, 0:SC], ACT.Silu).then_inc(sem(f"gs_rdy{l}"), 1)
                    return n

                def chunk_hi(s, h, par):
                    n = 2 * s + h
                    act.wait_ge(sem(f"ev_h{l}"), n + 2)
                    copy(hh[:, par, h, 0:W], hf[:, 0:W]).then_inc(sem(f"hh_rdy{l}"), 1)

                def ffn_step(s, par, first=False, last=False, first_down=False):
                    if not first:
                        hi_down(l, s - 1, first=first_down)
                    for h in range(2):
                        chunk(s, h, par)
                        if not last:
                            hi_a(A_GATE[l] + s + 1, h, f"ld_gate{l}", 16 * (s + 2))
                            hi_b(l, s + 1, h)
                        elif l == 0:
                            hi_a(A_IN[1], h, "ld_in1", 16)
                        if l == 0 and not (last and h):
                            nxt = 2 * s + h + 1
                            hi_modm(4 * s + 2 * h + 2, 0, panel=nxt)
                            hi_modm(4 * s + 2 * h + 3, 1, panel=nxt)
                        chunk_hi(s, h, par)

                ffn_step(0, 0, first=True)
                ffn_step(1, 1, first_down=True)
                with act.Fori(0, 4) as i:
                    ffn_step(2 * i + 2, 0)
                    ffn_step(2 * i + 3, 1)
                ffn_step(FSTEPS - 1, 0, last=True)
                hi_down(l, FSTEPS - 1)
                W = NT if l == 0 else SX
                for k in range(KC):
                    act.wait_ge(sem(f"ev_d{l}"), KC * (FSTEPS - 1) + k + 2)
                    if l == 0:
                        act.wait_ge(sem("ev_dc0"), KC * (FSTEPS - 1) + k + 1)
                    square(2 * l + 2, k, W)
                norm_root(2 * l + 2, W)

            for half in range(2):
                for t in range(4):
                    g = 4 * half + t
                    act.wait_ge(sem("fin_mm"), g + 1)
                    copy(otok[:, t, 512 * half:512 * half + 512], ps[:, 2 + g % 2, :]).then_inc(sem("fin_evac"), 1)

        @block.vector
        def _(dve):
            ch = Chain(dve, sem("dve_chain"))
            V = nc.vector

            def mod_copy(*done):
                dve.wait_ge(sem(done[0]), done[1])
                V.tensor_copy(modrow[:, :], ps[0:4, MODBANK[0], :]).then_inc(sem("modrow_rdy"), 1)

            MODBANK, MODCOLS = [4], [7]

            def mod_add(J):
                dve.wait_ge(sem("mod_fin"), J + 1)
                b = vcol[:, bass.ds(N_ROWS + 4 * J, 4)].unsqueeze(2).to_broadcast([P, 4, 2])
                V.tensor_tensor(modcol[:, bass.ds(4 * J, 4), :],
                                ps[:, MODCOLS[0], 256:264].rearrange("p (i s) -> p i s", i=4), b, ALU.add).then_inc(sem("modcol_rdy"), 1)

            ch.link(V.memset(c4[:, :].bitcast(F32), 0.0))
            dve.wait_ge(sem("csil_rdy"), 1)
            ch.link(V.tensor_copy(c4j[:, :, 0:2], csil[:, :, :]))
            V.tensor_tensor(c4j[:, :, 2:4], csil[:, :, :], c4j[:, :, 0:2].bitcast(F32), ALU.subtract).then_inc(sem("c4_rdy"), 1)

            def lo_start(q):
                dve.wait_ge(sem("st_hi"), q + 1)
                wl_q, wh_q, raw_q = [(wl[0], wh[0], raw[0]), (wl[1], wh[1], raw[1]), (wl_s, wh_s, raw_s)][q % 3]
                V.tensor_tensor(wl_q[:, :, :].rearrange("p h n -> p (h n)"), raw_q[:, :],
                                wh_q[:, :, :].rearrange("p h n -> p (h n)").bitcast(F32), ALU.subtract).then_inc(sem("st_lo"), 1)

            def add_square(u, k, W):
                nsq, nacc = (norm_later if u else norm_start)[0:2]
                dve.wait_ge(sem("nsq_rdy"), 8 * u + k + 1)
                if k:
                    dve.wait_ge(sem("nacc_rdy"), 8 * u + k)
                    ins = V.tensor_tensor(nacc[:, 0:W], nacc[:, 0:W], nsq[:, k % 2, 0:W], ALU.add)
                else:
                    ins = V.tensor_copy(nacc[:, 0:W], nsq[:, 0, 0:W])
                ins.then_inc(sem("nacc_rdy"), 1)

            def norm_parts(W):
                return [(0, SX, 0)] + ([(SX, NT, 1)] if W == NT else [])

            def norm_mean(u, W):
                nrb = (norm_later if u else norm_start)[2]
                dve.wait_ge(sem("nst_mm"), u + 1)
                for c0, c1, s in norm_parts(W):
                    last = V.tensor_scalar(nrb[:, c0:c1], ps[:, s, 0:c1 - c0], 1.0 / D, EPS, ALU.mult, ALU.add)
                last.then_inc(sem("nvar_rdy"), 1)

            def norm_recip(u, W):
                nrb = (norm_later if u else norm_start)[2]
                dve.wait_ge(sem("nrms_rdy"), u + 1)
                ch.link(V.reciprocal(nrb[:, 0:W], nrb[:, 0:W]))

            def start_scaled(k):
                ch.then(V.tensor_tensor(xr_start[:, k, :], xT[:, k, :], norm_start[2][:, :], ALU.mult))

            def log_decay_a():
                dve.wait_ge(sem("ld_small"), 16 * 18)
                ch.link(V.tensor_scalar(lt3[:, :], dec[:, :], -1.0, None, ALU.mult))
                V.tensor_tensor(lt1[:, :], dec[:, :], lt3[:, :], ALU.max).then_inc(sem("lg_ax"), 1)

            def log_decay_b():
                dve.wait_ge(sem("lg_e"), 1)
                ch.link(V.tensor_scalar(lt1[:, :], lt2[:, :], 2.0, None, ALU.add))
                ch.link(V.reciprocal(lt3[:, :], lt1[:, :]))
                ch.link(V.tensor_tensor(lt2[:, :], lt2[:, :], lt3[:, :], ALU.mult))
                ch.link(V.tensor_tensor(lt3[:, :], lt2[:, :], lt2[:, :], ALU.mult))
                ch.link(V.tensor_scalar(lt1[:, :], lt3[:, :], 1.0 / 15, 1.0 / 13, ALU.mult, ALU.add))
                for m in (11, 9, 7, 5, 3, 1):
                    ch.link(V.tensor_tensor(lt1[:, :], lt1[:, :], lt3[:, :], ALU.mult))
                    ch.link(V.tensor_scalar(lt1[:, :], lt1[:, :], 1.0 / m, None, ALU.add))
                ch.link(V.tensor_tensor(lt1[:, :], lt1[:, :], lt2[:, :], ALU.mult))
                ch.link(V.tensor_scalar(lt1[:, :], lt1[:, :], 2.0, None, ALU.mult))
                ch.link(V.tensor_scalar(lt3[:, :], dec[:, :], 0.0, None, ALU.min))
                ch.link(V.tensor_tensor(lg[:, :], lt3[:, :], lt1[:, :], ALU.subtract))
                ch.link(V.tensor_scalar(nlg[:, :], lg[:, :], -1.0, None, ALU.mult))
                ch.link(V.tensor_scalar(blg[:, 0:8], lg[:, 0:8], float(SX), None, ALU.mult))
                ch.link(V.tensor_scalar(blg[:, 8:16], lg[:, 8:16], float(SC), None, ALU.mult))

            for q in range(3):
                lo_start(q)
            for k in range(KC):
                add_square(0, k, NT)
            dve.wait_ge(sem("vc_mm"), 1)
            V.tensor_copy(vcol[:, :], ps[:, 7, 0:N_ROWS + N_BROWS]).then_inc(sem("vc_evac"), 1)
            for q in range(3, 8):
                lo_start(q)
                if q == 3:
                    norm_mean(0, NT)
                    log_decay_a()
                if q == 4:
                    norm_recip(0, NT)
                if q == 5:
                    log_decay_b()
                if q >= 4:
                    for k in range(2 * q - 8, 2 * q - 6):
                        start_scaled(k)
                if q % 2 == 1:
                    if q > 3:
                        mod_add(q // 2 - 2)
                    else:
                        mod_copy("st_use", 2)
                        continue
                    mod_copy("st_use", 2 * (q // 2))
            mod_add(2)
            mod_copy("st_use", 8)
            mod_add(3)
            def norm(u, W):
                l, second = u // 2, u % 2
                nrb, nxz = (norm_later if u else norm_start)[2:4]
                if u:
                    add_square(u, KC - 1, W)
                if u < 4:
                    dve.wait_ge(sem("modcol_rdy"), (J_IN, J_FFN, 24, 24)[u])
                    g0 = (R_N2 if second else R_N1) + KC * l
                    v = 4 if second else 1
                    gb = vcol[:, g0:g0 + KC].unsqueeze(2).to_broadcast([P, KC, 2])
                    ch.link(V.scalar_tensor_tensor(acol[:, :, :], modcol[:, 48 * l + KC * v:48 * l + KC * v + KC, :], 1.0,
                                                   gb, ALU.add, ALU.mult))
                if u:
                    norm_mean(u, W)
                    norm_recip(u, W)
                if u == 4:
                    for k in range(KC):
                        V.scalar_tensor_tensor(fz[:, k, :], xT[:, k, 0:SX], vcol[:, R_NF + k:R_NF + k + 1], nrb[:, 0:SX],
                                               ALU.mult, ALU.mult).then_inc(sem("fz_rdy"), 1)
                    return
                sh = 48 * l + KC * (3 if second else 0)

                def lo(k):
                    if k in Z_DVE:
                        dve.wait_ge(sem("nzf_rdy"), 8 * u + k + 1)
                        dve.wait_ge(sem("zh_rdy"), 8 * u + k + 1)
                        V.tensor_tensor(zl[:, k, 0:W], nxz[:, k % 3, 0:W], zh[:, k, 0:W].bitcast(F32), ALU.subtract
                                        ).then_inc(sem("z_dve"), 1)

                if u == 0:
                    ch.wait()
                for k in range(KC):
                    if k >= 3:
                        z_wait(dve, u, k - 3)
                    if u:
                        src = nxz[:, k % 3, 0:W]
                        ch.link(V.tensor_tensor(src, xT[:, k, 0:W], nrb[:, 0:W], ALU.mult))
                    else:
                        src = xr_start[:, k, :]
                    for c0, c1, s in norm_parts(W):
                        last = V.tensor_scalar(nxz[:, k % 3, c0:c1], src[:, c0:c1], acol[:, k, s:s + 1],
                                               modcol[:, sh + k, s:s + 1], ALU.mult, ALU.add)
                    last.then_inc(sem("nzf_rdy"), 1)
                    if k:
                        lo(k - 1)
                lo(KC - 1)

            for l in range(DEPTH):
                W = NT if l == 0 else SX
                norm(2 * l, NT)

                def lo_modb(b):
                    for h in range(2):
                        dve.wait_ge(sem("hiB"), 2 * b + h + 1)
                        V.tensor_tensor(wl[1][:, h, :], raw[1][:, 1024 * h:1024 * h + 1024], wh[1][:, h, :].bitcast(F32),
                                        ALU.subtract).then_inc(sem("lo_modb"), 1)

                if l == 0:
                    lo_modb(0)
                rope_n = 0
                for p, name in enumerate(PANELS):
                    for h in range(2):
                        if name in ("rk", "rq", "aq0", "aq1") or (name == "akav" and h == 0):
                            dst = {"rk": rk[:, h], "rq": rq[:, h], "akav": ak, "aq0": aq[:, h], "aq1": aq[:, 2 + h]}[name]
                            dve.wait_ge(sem(f"ev_in{l}"), 2 * p + h + 1)
                            src = rtmp[:, rope_n % 2, :]
                            ch.then(V.stream_shuffle(shuf[:, :], src, [(j + 16) % 32 for j in range(32)]))
                            ch.link(V.tensor_tensor(dst[:, 0:SX], src, ropeC, ALU.mult))
                            ch.link(V.tensor_tensor(shuf[:, :], shuf[:, :], ropeS, ALU.mult))
                            V.tensor_tensor(dst[:, 0:SX], dst[:, 0:SX], shuf[:, :], ALU.add).then_inc(sem(f"rope_done{l}"), 1)
                            rope_n += 1
                            dve.wait_ge(sem(f"rope_done{l}"), rope_n)
                        if l == 0 and 2 * p + h + 1 < N_MODB:
                            lo_modb(2 * p + h + 1)
                        if l == 0 and h == 0 and p:
                            mod_add(J_IN + p - 1)
                    if l == 0:
                        mod_copy("use_b", 4 * p + 4)
                if l == 0:
                    mod_add(J_IN + NP_IN - 1)

                nt = W // P
                G = 4 * nt
                dve.wait_ge(sem(f"vtr_ev{l}"), 5)
                cv = cvt[:, 0:nt, :].rearrange("p t (g d) -> p (t g) d", d=HD)
                sq = cmsq[:, 0:nt, :].rearrange("p t (g d) -> p (t g) d", d=HD)

                def wide(i):
                    return cmst[:, i, 0:G].unsqueeze(2).to_broadcast([P, G, HD])

                ch.link(V.tensor_reduce(cmst[:, 0, 0:G], cv, AX_X, ALU.add))
                ch.link(V.tensor_scalar(cmst[:, 0, 0:G], cmst[:, 0, 0:G], 1.0 / HD, None, ALU.mult))
                ch.link(V.tensor_tensor(cv, cv, wide(0), ALU.subtract))
                ch.link(V.tensor_tensor(sq, cv, cv, ALU.mult))
                ch.link(V.tensor_reduce(cmst[:, 1, 0:G], sq, AX_X, ALU.add))
                V.tensor_scalar(cmst[:, 1, 0:G], cmst[:, 1, 0:G], 1.0 / HD, EPS, ALU.mult, ALU.add).then_inc(sem("cm_var"), 1)
                dve.wait_ge(sem("cm_std"), l + 1)
                ch.link(V.reciprocal(cmst[:, 1, 0:G], cmst[:, 1, 0:G]))
                V.tensor_tensor(cv, cv, wide(1), ALU.mult).then_inc(sem("cm_vn"), 1)
                dve.wait_ge(sem("cm_mm"), l + 1)
                e = 0
                for c0, c1, s in parts(l == 0):
                    n = c1 - c0
                    for r in range(2):
                        src = ps[:, 5 + r, :] if s == 0 else ps[:, 7, SC * r:SC * r + SC]
                        dst = cmf[:, e % 2, 0:n]
                        g = vcol[:, R_CN + 2 * l + r:R_CN + 2 * l + r + 1]
                        bias = bsb[:, l, r, :].unsqueeze(1).to_broadcast([P, n // P, P])
                        ch.link(V.scalar_tensor_tensor(dst.rearrange("p (t q) -> p t q", q=P),
                                                       src.rearrange("p (t q) -> p t q", q=P), g, bias, ALU.mult, ALU.add))
                        V.tensor_tensor(dst, dst, cu[:, r, c0:c1], ALU.mult).then_inc(sem(f"cm_f{l}"), 1)
                        dve.wait_ge(sem(f"cm_hi{l}"), e + 1)
                        V.tensor_tensor(zl[:, 6 + r, c0:c1], dst, zh[:, 6 + r, c0:c1].bitcast(F32), ALU.subtract
                                        ).then_inc(sem(f"cm_lo{l}"), 1)
                        e += 1
                        dve.wait_ge(sem(f"cm_lo{l}"), e)

                def table(h):
                    i, b = l * 4 + h, h % 2
                    ch.link(V.tensor_scalar(T[:, b, :], dist, lg[:, i:i + 1], None, ALU.mult))
                    V.scalar_tensor_tensor(T[:, b, :], dist, nlg[:, 8 + i:9 + i], T[:, b, :], ALU.mult, ALU.min
                                           ).then_inc(sem(f"T_arg{l}"), 1)

                def table_end(h):
                    b = h % 2
                    dve.wait_ge(sem(f"T_exp{l}"), h + 1)
                    ch.link(V.tensor_tensor(T[:, b, 384:512], T[:, b, 384:512], eye, ALU.add))
                    V.tensor_tensor(TC[:, b, :], TC[:, b, :], TD[:, :], ALU.add).then_inc(sem(f"T_done{l}"), 1)
                    dve.wait_ge(sem(f"T_done{l}"), h + 1)

                jobs = [(c, 0) for c in range(6)] + ([(c, 1) for c in (4, 5)] if l == 0 else [])
                table(0)
                j = 0
                for h in range(4):
                    table_end(h)
                    if h < 3:
                        table(h + 1)
                    for c, s in jobs:
                        n = (SX, SC)[s]
                        if s == 0 and c >= 4:
                            tab = TC[:, h % 2, P - P * (c - 4):P - P * (c - 4) + SX]
                        else:
                            off = 384 - P * (c - 4 * s)
                            tab = T[:, h % 2, off:off + n]
                        dve.wait_ge(sem(f"ret_sc{l}"), j + 1)
                        if j >= 3:
                            dve.wait_ge(sem(f"ret_pv{l}"), j - 2)
                        V.scalar_tensor_tensor(Pm[:, j % 3, 0:n], ps[:, j % 3, 0:n], SCALE, tab, ALU.mult, ALU.mult
                                               ).then_inc(sem(f"ret_p{l}"), 1)
                        j += 1
                for r in range(2):
                    dve.wait_ge(sem(f"gmean_mm{l}"), r + 1)
                    for c0, c1, s in parts(l == 0):
                        last = V.tensor_tensor(oc[:, c0:c1], osb[:, r, c0:c1], ps[:, (7, 4)[s], 0:c1 - c0], ALU.subtract)
                    last.then_inc(sem(f"oc_rdy{l}"), 1)
                    dve.wait_ge(sem(f"gvar_mm{l}"), r + 1)
                    for c0, c1, s in parts(l == 0):
                        last = V.tensor_scalar(gsq[:, c0:c1], ps[:, (7, 4)[s], 0:c1 - c0], EPS, None, ALU.add)
                    last.then_inc(sem(f"gvar_rdy{l}"), 1)
                    dve.wait_ge(sem(f"gstd_rdy{l}"), r + 1)
                    ch.link(V.reciprocal(gsq[:, 0:W], gsq[:, 0:W]))
                    ch.link(V.tensor_tensor(oc[:, 0:W], oc[:, 0:W], gsq[:, 0:W], ALU.mult))
                    g = vcol[:, R_RN + 2 * l + r:R_RN + 2 * l + r + 1]
                    V.scalar_tensor_tensor(oc[:, 0:W], oc[:, 0:W], g, rg[:, r, 0:W], ALU.mult, ALU.mult
                                           ).then_inc(sem(f"ret_f{l}"), 1)
                    dve.wait_ge(sem(f"ret_hi{l}"), r + 1)
                    V.tensor_tensor(zl[:, r, 0:W], oc[:, 0:W], zh[:, r, 0:W].bitcast(F32), ALU.subtract
                                    ).then_inc(sem(f"ret_lo{l}"), 1)
                    dve.wait_ge(sem(f"ret_lo{l}"), r + 1)

                blocks = list(range(4)) + ([4, 5] if l == 0 else [])
                units = [(i, kv) for i in blocks for kv in range(2)]

                def local(i):
                    return list(range(max(i - 1, 0), min(i + 1, 3) + 1)) if i < 4 else []

                def scores(u):
                    i, kv = units[u]
                    nl = P * len(local(i))
                    wd = nl + SC
                    mask = {0: K_MASK + P, 3: K_MASK3}.get(i, K_MASK if i < 4 else K_MASK + 384)
                    if u >= 2:
                        dve.wait_ge(sem(f"at_tr{l}"), sum(len(local(i2)) + 2 for i2, _ in units[:u - 1]))
                    for c in range(4):
                        hd = 4 * kv + c
                        dve.wait_ge(sem(f"at_sc{l}"), 4 * u + c + 1)
                        pair = ps[:, 2 * (c % 2):2 * (c % 2) + 2, :].rearrange("p b n -> p (b n)")
                        V.tensor_tensor_reduce(s_at[:, u % 2, c, 0:wd], pair[:, SX - nl:SX + SC], K[:, mask:mask + wd], SCALE,
                                               sinkb[:, 8 * l + hd:8 * l + hd + 1], ALU.add, ALU.max,
                                               stats[:, u % 2, c:c + 1]).then_inc(sem(f"at_max{l}"), 1)
                    dve.wait_ge(sem(f"at_max{l}"), 4 * u + 4)
                    ch.link(V.tensor_scalar(stats[:, u % 2, 4:8], stats[:, u % 2, 0:4], -1.0, None, ALU.mult))
                    V.tensor_tensor(stats[:, u % 2, 8:12], sinkb[:, 8 * l + 4 * kv:8 * l + 4 * kv + 4], stats[:, u % 2, 4:8],
                                    ALU.add).then_inc(sem(f"at_nb{l}"), 1)

                def weights(u):
                    i, kv = units[u]
                    wd = P * len(local(i)) + SC
                    dve.wait_ge(sem(f"at_exp{l}"), u + 1)
                    ch.link(V.tensor_tensor(stats[:, u % 2, 16:20], stats[:, u % 2, 16:20], stats[:, u % 2, 12:16], ALU.add))
                    ch.link(V.reciprocal(stats[:, u % 2, 16:20], stats[:, u % 2, 16:20]))
                    for c in range(4):
                        last = V.tensor_scalar(s_at[:, u % 2, c, 0:wd], s_at[:, u % 2, c, 0:wd],
                                               stats[:, u % 2, 16 + c:17 + c], None, ALU.mult)
                    last.then_inc(sem(f"at_p{l}"), 1)

                def rest(u):
                    i, kv = units[u]
                    if kv:
                        dve.wait_ge(sem(f"at_hi{l}"), u // 2 + 1)
                        q = slice(P * i, P * i + P)
                        V.tensor_tensor(zl[:, 2:6, q], ps[:, 7, :].rearrange("p (c q) -> p c q", c=4),
                                        zh[:, 2:6, q].bitcast(F32), ALU.subtract).then_inc(sem(f"at_lo{l}"), 1)

                for u in range(len(units)):
                    scores(u)
                    weights(u)
                    if u:
                        rest(u - 1)
                rest(len(units) - 1)

                for p in range(4):
                    for h in range(2):
                        n = 2 * p + h
                        dve.wait_ge(sem("use_a"), 2 * (A_OUT[l] + p) + h + 1)
                        for c0, c1, s in parts(l == 0):
                            last = V.scalar_tensor_tensor(xT[:, n, c0:c1], ps[:, h + 2 * s, 0:c1 - c0],
                                                          modcol[:, 48 * l + 16 + n, s:s + 1], xT[:, n, c0:c1], ALU.mult, ALU.add)
                        last.then_inc(sem(f"ev_out{l}"), 1)
                        if n:
                            add_square(2 * l + 1, n - 1, W)
                dve.wait_ge(sem(f"ev_out{l}"), 8)
                norm(2 * l + 1, W)

                V.memset(stats[:, 0, 1:2], 0.0).then_inc(sem(f"ev_h{l}"), 1)
                V.memset(stats[:, 0, 2:3], 0.0).then_inc(sem(f"ev_d{l}"), 1)

                def chunk(s, h, par):
                    n = 2 * s + h
                    per = 2 if l == 0 else 1
                    for c0, c1, sc in parts(l == 0):
                        dve.wait_ge(sem(f"gs_rdy{l}"), per * n + sc + 1)
                        up = ps[:, 3 * h + 1, :] if sc == 0 else ps[:, 3 * h + 2, SC:2 * SC]
                        last = V.tensor_tensor(hf[:, c0:c1], gs[:, c0:c1], up, ALU.mult)
                    last.then_inc(sem(f"ev_h{l}"), 1)

                def chunk_lo(s, h, par):
                    n = 2 * s + h
                    dve.wait_ge(sem(f"hh_rdy{l}"), n + 1)
                    V.tensor_tensor(hl[:, par, h, 0:W], hf[:, 0:W], hh[:, par, h, 0:W].bitcast(F32), ALU.subtract
                                    ).then_inc(sem(f"h_rdy{l}"), 1)
                    dve.wait_ge(sem(f"h_rdy{l}"), n + 1)

                def down(s, chunks=range(KC), last_step=False):
                    if chunks[0] == 0:
                        dve.wait_ge(sem(f"ev_d{l}"), KC * s + 1)
                    for n in chunks:
                        for c0, c1, sc in parts(l == 0):
                            dve.wait_ge(sem(f"dn{sc}_mm{l}"), KC * s + n + 1)
                            src = ps[:, (0, 6)[n % 2], :] if sc == 0 else ps[:, (2, 7)[n % 2], 0:SC]
                            last = V.scalar_tensor_tensor(xT[:, n, c0:c1], src, modcol[:, 48 * l + 40 + n, sc:sc + 1],
                                                          xT[:, n, c0:c1], ALU.mult, ALU.add)
                            if sc == 0:
                                last.then_inc(sem(f"ev_d{l}"), 1)
                            else:
                                last.then_inc(sem(f"ev_dc{l}"), 1)
                        if last_step and n:
                            add_square(2 * l + 2, n - 1, W)

                MODBANK[0], MODCOLS[0] = 6, 1

                def ffn_step(s, par, first=False):
                    chunk(s, 0, par)
                    chunk_lo(s, 0, par)
                    if l == 0:
                        mod_copy("use_m", 4 * s + 4)
                    chunk(s, 1, par)
                    if l == 0:
                        mod_add(J_FFN + s)
                    if not first:
                        down(s - 1, range(0, 3))
                    chunk_lo(s, 1, par)
                    if not first:
                        down(s - 1, range(3, KC))

                ffn_step(0, 0, first=True)
                ffn_step(1, 1)
                with dve.Fori(0, 4) as i:
                    ffn_step(2 * i + 2, 0)
                    ffn_step(2 * i + 3, 1)
                ffn_step(FSTEPS - 1, 0)
                down(FSTEPS - 1, last_step=True)
                dve.wait_ge(sem(f"ev_d{l}"), KC * FSTEPS + 1)
                if l == 0:
                    dve.wait_ge(sem("ev_dc0"), KC * FSTEPS)
                MODBANK[0], MODCOLS[0] = 4, 7
            norm(4, SX)

        @block.tensor
        def _(pe):
            MM, TR = nc.tensor.matmul, nc.tensor.transpose
            MODBANK, MODCOLS = [4], [7]

            def mod_half(m, w_hi, w_lo):
                for jj in range(2):
                    j = 2 * m + jj
                    for w in (w_hi, w_lo):
                        last = MM(ps[:, MODBANK[0], :], c4[:, 4 * j:4 * j + P], w[:, 512 * jj:512 * jj + 512],
                                  start=(j == 0 and w is w_hi), stop=(j == 7 and w is w_lo))
                return last

            def mod_finish(J):
                pe.wait_ge(sem("modrow_rdy"), J + 1)
                for i in range(4):
                    last = MM(ps[:, MODCOLS[0], 256 + 2 * i:258 + 2 * i], modrow[0:4, P * i:P * i + P], sel, start=True, stop=True)
                last.then_inc(sem("mod_fin"), 1)

            def norm(u, W):
                nacc = (norm_later if u else norm_start)[1]
                pe.wait_ge(sem("nacc_rdy"), 8 * u + 8)
                for c0, c1, s in ([(0, SX, 0)] + ([(SX, NT, 1)] if W == NT else [])):
                    last = MM(ps[:, s, 0:c1 - c0], ones, nacc[:, c0:c1], start=True, stop=True)
                last.then_inc(sem("nst_mm"), 1)

            pe.wait_ge(sem("ld_k"), 16)
            pe.wait_ge(sem("ld_x"), 16)
            pe.wait_ge(sem("ld_ctx"), 16)
            for k in range(KC):
                if k >= 2:
                    pe.wait_ge(sem("xt_evac"), k - 1)
                for t in range(6):
                    dst = ps[:, k % 2, P * t:P * t + P] if t < 4 else ps[:, 2 + k % 2, P * (t - 4):P * (t - 4) + P]
                    last = TR(dst, xin[:, t, P * k:P * k + P], eye)
                last.then_inc(sem("xt_mm"), 1)
            pe.wait_ge(sem("ld_small"), 16 * 18)
            TR(ps[:, 7, 0:N_ROWS], rows_a[:, :], eye[0:N_ROWS, 0:N_ROWS])
            TR(ps[:, 7, N_ROWS:N_ROWS + N_BROWS], rows_b[:, :], eye[0:N_BROWS, 0:N_BROWS]).then_inc(sem("vc_mm"), 1)
            for i in range(8):
                last = TR(ps[:, 5 + i // 4, P * (i % 4):P * (i % 4) + P], cws[:, i, :], eye)
            last.then_inc(sem("ws_mm"), 1)
            pe.wait_ge(sem("c4_rdy"), 1)
            pe.wait_ge(sem("vc_evac"), 1)
            norm(0, NT)
            for q in range(8):
                J = q // 2
                pe.wait_ge(sem("st_lo"), q + 1)
                wh_q, wl_q = [(wh[0], wl[0]), (wh[1], wl[1]), (wh_s, wl_s)][q % 3]
                if q % 2 == 0 and J:
                    mod_finish(J - 1)
                for hh_ in range(2):
                    last = mod_half(2 * (q % 2) + hh_, wh_q[:, hh_, :], wl_q[:, hh_, :])
                last.then_inc(sem("st_use"), 1)
            mod_finish(3)

            def three_pass(wt_h, wt_l, h, dsts, ctx, norm_u=None):
                for k in range(KC):
                    w = slice(P * k, P * k + P)
                    if norm_u is not None:
                        z_wait(pe, norm_u, k)
                    for c0, c1, s in parts(ctx):
                        dst = dsts[s]
                        MM(dst, wt_h[:, h, w], zh[:, k, c0:c1], start=(k == 0), stop=False)
                        MM(dst, wt_h[:, h, w], zl[:, k, c0:c1], start=False, stop=False)
                        last = MM(dst, wt_l[:, h, w], zh[:, k, c0:c1], start=False, stop=(k == KC - 1))
                return last

            def panel_half(a, h, ctx, norm_u=None):
                pe.wait_ge(sem("loA"), 2 * a + h + 1)
                three_pass(wh[0], wl[0], h, (ps[:, h, :], ps[:, h + 2, 0:SC]), ctx, norm_u).then_inc(sem("use_a"), 1)

            for l in range(DEPTH):
                W = NT if l == 0 else SX
                if l:
                    norm(2 * l, NT)

                def in_step(p, ctx, first=False):
                    for h in range(2):
                        if not first:
                            pe.wait_ge(sem(f"ev_in{l}"), 2 * p + h - 1)
                        panel_half(A_IN[l] + p, h, ctx, 2 * l if first and h == 0 else None)
                        if l == 0:
                            if h == 0 and not first:
                                mod_finish(J_IN + p - 1)
                            b = 2 * p + h
                            for hh_ in range(2):
                                pe.wait_ge(sem("lo_modb"), 2 * b + hh_ + 1)
                                last = mod_half(2 * h + hh_, wh[1][:, hh_, :], wl[1][:, hh_, :])
                                last.then_inc(sem("use_b"), 1)

                in_step(0, True, first=True)
                with pe.Fori(1, NP_CTX) as p:
                    in_step(p, True)

                def to_tokens(v, slot, ctx, order):
                    pe.wait_ge(sem(f"ev_in{l}"), order)
                    if v:
                        pe.wait_ge(sem(f"vtr_ev{l}"), v)
                    if l == 0:
                        pe.wait_ge(sem("modcol_rdy"), J_IN + (NP_CTX - 1 if v < 3 else NP_IN))
                    for t in range(6 if ctx else 4):
                        dst = ps[:, 5 + (v % 3) % 2, P * t:P * t + P] if t < 4 else ps[:, 7, P * (t - 4):P * (t - 4) + P]
                        last = TR(dst, vT[:, slot, P * t:P * t + P], eye)
                    last.then_inc(sem(f"vtr_mm{l}"), 1)

                for v in range(3):
                    to_tokens(v, v, True, 6)
                pe.wait_ge(sem(f"vtr_ev{l}"), 3)
                with pe.Fori(NP_CTX, NP_IN) as p:
                    in_step(p, l == 0)
                if l == 0:
                    mod_finish(J_IN + NP_IN - 1)
                for v in range(2):
                    to_tokens(3 + v, v, l == 0, 18)

                pe.wait_ge(sem("cm_vn"), l + 1)
                for s in range(2 if l == 0 else 1):
                    for r in range(2):
                        for t in range((4, 2)[s]):
                            for g2 in range(2):
                                cols = (0, SC * r)[s] + P * t
                                last = MM(ps[64 * g2:64 * g2 + 64, (5 + r, 7)[s], cols:cols + P],
                                          cvt[:, 4 * s + t, P * r + HD * g2:P * r + HD * g2 + HD],
                                          wsT[:, l, P * (2 * r + g2):P * (2 * r + g2) + P], start=True, stop=True)
                last.then_inc(sem("cm_mm"), 1)

                jobs = [(h, c, s) for h in range(4) for c, s in
                        [(c, 0) for c in range(6)] + ([(c, 1) for c in (4, 5)] if l == 0 else [])]
                pe.wait_ge(sem(f"rope_done{l}"), 9)
                pe.wait_ge(sem(f"cm_lo{l}"), 4 if l == 0 else 2)

                def score(j):
                    h, c, s = jobs[j]
                    b, r = 64 * (h % 2), h // 2
                    q = slice(0, SX) if s == 0 else slice(SX, NT)
                    if j >= 3:
                        pe.wait_ge(sem(f"ret_p{l}"), j - 2)
                    MM(ps[:, j % 3, 0:q.stop - q.start], rk[b:b + 64, r, P * c:P * c + P], rq[b:b + 64, r, q],
                       start=True, stop=True).then_inc(sem(f"ret_sc{l}"), 1)

                def value(j):
                    h, c, s = jobs[j]
                    b = 64 * (h % 2)
                    n = (SX, SC)[s]
                    first = c == (0, 4)[s]
                    if h == 2 and first and s == 0:
                        pe.wait_ge(sem(f"osb_rdy{l}"), 1)
                    pe.wait_ge(sem(f"ret_p{l}"), j + 1)
                    last = MM(ps[b:b + 64, 5 + s, 0:n], vtok[:, c, HD * h:HD * h + HD], Pm[:, j % 3, 0:n],
                              start=first, stop=(c == 5))
                    last.then_inc(sem(f"ret_pv{l}"), 1)

                for j in range(len(jobs)):
                    score(j)
                    if j >= 2:
                        value(j - 2)
                value(len(jobs) - 2)
                value(len(jobs) - 1)
                for r in range(2):
                    pe.wait_ge(sem(f"osb_rdy{l}"), r + 1)
                    if r:
                        pe.wait_ge(sem(f"gvar_rdy{l}"), r)
                    for c0, c1, s in parts(l == 0):
                        last = MM(ps[:, (7, 4)[s], 0:c1 - c0], blk, osb[:, r, c0:c1], start=True, stop=True)
                    last.then_inc(sem(f"gmean_mm{l}"), 1)
                    pe.wait_ge(sem(f"gsq_rdy{l}"), r + 1)
                    for c0, c1, s in parts(l == 0):
                        last = MM(ps[:, (7, 4)[s], 0:c1 - c0], blk, gsq[:, c0:c1], start=True, stop=True)
                    last.then_inc(sem(f"gvar_mm{l}"), 1)

                blocks = list(range(4)) + ([4, 5] if l == 0 else [])
                units = [(i, kv) for i in blocks for kv in range(2)]
                pe.wait_ge(sem(f"ret_lo{l}"), 2)

                def local(i):
                    return list(range(max(i - 1, 0), min(i + 1, 3) + 1)) if i < 4 else []

                def scores(u):
                    i, kv = units[u]
                    b = 64 * kv
                    loc = local(i)
                    nl = P * len(loc)
                    for c in range(4):
                        if 4 * u + c >= 2:
                            pe.wait_ge(sem(f"at_max{l}"), 4 * u + c - 1)
                        q = aq[b:b + 64, c, P * i:P * i + P]
                        if loc:
                            MM(ps[:, 2 * (c % 2), SX - nl:SX], q, ak[b:b + 64, P * loc[0]:P * loc[0] + nl], start=True, stop=True)
                        MM(ps[:, 2 * (c % 2) + 1, 0:SC], q, ak[b:b + 64, SX:NT], start=True, stop=True).then_inc(sem(f"at_sc{l}"), 1)

                g = 0

                def values(u):
                    nonlocal g
                    i, kv = units[u]
                    chunks = local(i) + [4, 5]
                    pe.wait_ge(sem(f"at_p{l}"), u + 1)
                    g0 = g
                    for kk in range(len(chunks)):
                        if g >= 2:
                            pe.wait_ge(sem(f"at_pt{l}"), g - 1)
                        for c in range(4):
                            last = TR(ps[:, 5 + g % 2, P * c:P * c + P], s_at[:, u % 2, c, P * kk:P * kk + P], eye)
                        last.then_inc(sem(f"at_tr{l}"), 1)
                        g += 1
                    if kv == 0 and i:
                        pe.wait_ge(sem(f"at_lo{l}"), i)
                    for kk, tile in enumerate(chunks):
                        pe.wait_ge(sem(f"at_pt{l}"), g0 + kk + 1)
                        last = MM(ps[64 * kv:64 * kv + 64, 7, :], vtok[:, tile, 256 + HD * kv:256 + HD * kv + HD], pT[:, kk, :],
                                  start=(kk == 0), stop=(kk == len(chunks) - 1))
                    last.then_inc(sem(f"at_o{l}"), 1)

                for u in range(len(units)):
                    scores(u)
                    if u:
                        values(u - 1)
                values(len(units) - 1)

                pe.wait_ge(sem(f"at_lo{l}"), len(blocks))

                def out_step(p, first=False):
                    for h in range(2):
                        if not first:
                            pe.wait_ge(sem(f"ev_out{l}"), 2 * p + h - 1)
                        panel_half(A_OUT[l] + p, h, l == 0)

                out_step(0, first=True)
                with pe.Fori(1, 4) as p:
                    out_step(p)

                norm(2 * l + 1, W)

                MODBANK[0], MODCOLS[0] = 6, 1

                def ffn_mod(s, h):
                    for hh_ in range(2):
                        pe.wait_ge(sem("loM"), 4 * s + 2 * h + hh_ + 1)
                        last = mod_half(2 * h + hh_, wh_m[:, hh_, :], wl_m[:, hh_, :])
                        last.then_inc(sem("use_m"), 1)

                def down(s, par):
                    pe.wait_ge(sem(f"loD{l}"), 2 * s + 2)
                    pe.wait_ge(sem(f"h_rdy{l}"), 2 * s + 2)
                    start = type(s) is int and s == 0
                    for n in range(KC):
                        w = slice(P * n, P * n + P)
                        for c0, c1, sc in parts(l == 0):
                            if sc == 0 and not (start and n == 0):
                                pe.wait_ge(sem(f"ev_d{l}"), KC * s + n)
                            if sc == 1 and not (start and n < 2):
                                pe.wait_ge(sem(f"ev_dc{l}"), KC * s + n - 1)
                            dst = ps[:, (0, 6)[n % 2], :] if sc == 0 else ps[:, (2, 7)[n % 2], 0:SC]
                            for k in range(2):
                                MM(dst, wh_d[:, k, w], hh[:, par, k, c0:c1], start=(k == 0), stop=False)
                                MM(dst, wh_d[:, k, w], hl[:, par, k, c0:c1], start=False, stop=False)
                                last = MM(dst, wl_d[:, k, w], hh[:, par, k, c0:c1], start=False, stop=(k == 1))
                            last.then_inc(sem(f"dn{sc}_mm{l}"), 1)

                def ffn_step(s, par, first=False):
                    a, b = A_GATE[l] + s, B_UP[l] + s
                    if not (type(s) is int and s < 2):
                        pe.wait_ge(sem(f"ev_d{l}"), KC * (s - 1))
                        if l == 0:
                            pe.wait_ge(sem("ev_dc0"), KC * (s - 1) - 1)
                    for h in range(2):
                        pe.wait_ge(sem("loA"), 2 * a + h + 1)
                        pe.wait_ge(sem(f"ev_h{l}"), 2 * s + h) if not first else None
                        last = three_pass(wh[0], wl[0], h, (ps[:, 3 * h, :], ps[:, 3 * h + 2, 0:SC]), l == 0,
                                          2 * l + 1 if first and h == 0 else None)
                        last.then_inc(sem("use_a"), 1)
                        if l == 0 and h:
                            ffn_mod(s, 1)
                        pe.wait_ge(sem("loB"), 2 * (b - N_MODB) + h + 1)
                        if l == 0 and h == 0 and not first:
                            pe.wait_ge(sem("modcol_rdy"), J_FFN + s)
                        last = three_pass(wh[1], wl[1], h, (ps[:, 3 * h + 1, :], ps[:, 3 * h + 2, SC:2 * SC]), l == 0)
                        last.then_inc(sem("use_b"), 1)
                        if l == 0 and h == 0:
                            if not first:
                                pe.wait_ge(sem("ev_d0"), KC * (s - 1) + 1)
                            ffn_mod(s, 0)
                    pe.wait_ge(sem(f"ev_h{l}"), 2 * s + 2)
                    if l == 0:
                        mod_finish(J_FFN + s)
                    if not first:
                        down(s - 1, 1 - par)

                ffn_step(0, 0, first=True)
                ffn_step(1, 1)
                with pe.Fori(0, 4) as i:
                    ffn_step(2 * i + 2, 0)
                    ffn_step(2 * i + 3, 1)
                ffn_step(FSTEPS - 1, 0)
                down(FSTEPS - 1, 0)
                MODBANK[0], MODCOLS[0] = 4, 7

            norm(4, SX)
            for half in range(2):
                pe.wait_ge(sem("fz_rdy"), 4 * half + 4)
                for t in range(4):
                    g = 4 * half + t
                    if g >= 2:
                        pe.wait_ge(sem("fin_evac"), g - 1)
                    for i in range(4):
                        last = TR(ps[:, 2 + g % 2, P * i:P * i + P], fz[:, 4 * half + i, P * t:P * t + P], eye)
                    last.then_inc(sem("fin_mm"), 1)


_INS = ['x', 'c', 'ctx', 'c_ctx', 'w_mod', 'b_mod', 'norm1_g', 'norm2_g', 'w_in', 'ret_decay_f', 'ret_decay_b',
        'ret_norm_g', 'attn_sink', 'cm_norm_g', 'cm_w_s', 'cm_b_s', 'w_out', 'w_gate', 'w_up', 'w_down', 'final_norm_g']


def shape_constants():
    import numpy as np
    k = np.zeros((P, K_ALL), np.float32)
    k[:, K_EYE:K_EYE + P] = np.eye(P)
    k[:, K_ONES:K_ONES + P] = 1.0
    for g in range(2):
        k[64 * g:64 * g + 64, K_BLK + 64 * g:K_BLK + 64 * g + 64] = 1.0 / HD
    k[[0, 2], K_SEL] = 1.0
    k[[1, 3], K_SEL + 1] = 1.0
    q, kk = np.arange(P)[:, None], np.arange(384)[None, :]
    band = np.where(np.abs(kk - P - q) <= P, 0.0, MASKED)
    k[:, K_MASK:K_MASK + 384] = band
    k[:, K_MASK3:K_MASK3 + 256] = band[:, 0:256]
    k[:, K_DIST:K_DIST + DIST_W] = np.arange(DIST_W)[None, :] - 384 - q
    pos = np.arange(SX)
    inv = (1.0 / np.float32(10000.0) ** (np.arange(16, dtype=np.float32) / np.float32(16))).astype(np.float32)
    for r in range(P):
        d = r % HD
        at = (pos // 64 if d < 32 else pos % 64).astype(np.float32)
        ang = at * inv[d % 16]
        k[r, K_RC:K_RC + SX] = np.cos(ang)
        k[r, K_RS:K_RS + SX] = np.sin(ang) * (-1.0 if d % 32 < 16 else 1.0)
    return k


def kernel(**inputs):
    import numpy as _np
    import concourse.bacc as _bacc
    from concourse.bass_utils import run_bass_kernel_spmd as _run

    nc = _bacc.Bacc("TRN2", target_bir_lowering=False, num_devices=1, dynamic_dma_scratch_size=1024)
    arrays, args = {}, []
    for name in _INS:
        a = _np.ascontiguousarray(inputs[name])
        arrays[f"in_{name}_dram"] = a
        args.append(nc.dram_tensor(f"in_{name}_dram", a.shape, F32, kind="ExternalInput").ap())
    arrays["consts_dram"] = shape_constants()
    args.append(nc.dram_tensor("consts_dram", (P, K_ALL), F32, kind="ExternalInput").ap())
    args.append(nc.dram_tensor("out_0_dram", (1, SX, D), F32, kind="ExternalOutput").ap())
    trunk(nc, *args)
    r = _run(nc, [arrays], core_ids=[0])
    return r.results[0]["out_0_dram"]
```

```python
from contextlib import ExitStack

import concourse.bass as bass
from concourse import mybir

F32 = mybir.dt.float32
F32R = mybir.dt.float32r
ALU = mybir.AluOpType
ACT = mybir.ActivationFunctionType
AX_X = mybir.AxisListType.X

P = 128
D = 1024
KC = D // P
DEPTH = 2
SX = 512
SC = 256
NT = SX + SC
HD = 64
EPS = 1e-6
SCALE = HD ** -0.5
FFN = 2816
FSTEPS = FFN // 256
IN_W = 2304
MASKED = -1e30

C_RQ, C_RK, C_RV, C_RG, C_AQ, C_AK, C_CU, C_CV = 0, 256, 512, 768, 1024, 1536, 1792, 2048
PANELS = ["rv", "rk", "akav", "rq", "cv", "cu", "aq0", "aq1", "rg"]
PANEL_COL = {"rv": C_RV, "rk": C_RK, "akav": C_AK, "rq": C_RQ, "cv": C_CV, "cu": C_CU, "rg": C_RG}
NP_IN = len(PANELS)
NP_CTX = 3
V_AT, CV_AT = 3, 6

R_N1, R_N2, R_NF, R_RN, R_CN, N_ROWS = 0, 16, 32, 40, 44, 48
N_BROWS = DEPTH * 48

K_EYE, K_ONES, K_BLK, K_SEL, K_MASK, K_MASK3, K_DIST, K_RC, K_RS = 0, 128, 256, 384, 386, 1026, 1538, 2434, 2946
K_ALL = 3458
DIST_W = 896


class Chain:

    def __init__(self, eng, sem):
        self.eng, self.sem, self.n = eng, sem, 0

    def then(self, ins):
        ins.then_inc(self.sem, 1)
        self.n += 1
        return ins

    def wait(self):
        self.eng.wait_ge(self.sem, self.n)

    def link(self, ins):
        self.then(ins)
        self.wait()
        return ins


def trunk(nc, x, c, ctx_in, c_ctx, w_mod, b_mod, norm1_g, norm2_g, w_in, ret_decay_f, ret_decay_b, ret_norm_g,
          attn_sink, cm_norm_g, cm_w_s, cm_b_s, w_out, w_gate, w_up, w_down, final_norm_g, consts, out):
    stack = ExitStack()
    with stack:
        def sb(name, shape, dt=F32):
            return stack.enter_context(nc.sbuf_tensor(name, shape, dt))

        sems = {}

        def sem(name):
            if name not in sems:
                sems[name] = stack.enter_context(nc.semaphore(name))
            return sems[name]

        def overlay(specs, under=()):
            with ExitStack() as phase:
                for name, shape, dt in list(under) + list(specs):
                    t = phase.enter_context(nc.sbuf_tensor(name, shape, dt))
                    made[name] = t
            return [made[s[0]] for s in specs]

        made = {}

        K = sb("consts_sb", [P, K_ALL])
        xT = sb("xT", [P, KC, NT])
        zh = sb("zh", [P, KC, NT], F32R)
        zl = sb("zl", [P, KC, NT], F32R)
        raw = [sb(f"raw{i}", [P, 2048]) for i in range(2)]
        wh = [sb(f"wh{i}", [P, 2, 1024], F32R) for i in range(2)]
        wl = [sb(f"wl{i}", [P, 2, 1024], F32R) for i in range(2)]
        wsT = sb("wsT", [P, DEPTH, 512])
        bsb = sb("bsb", [P, DEPTH, 2, P])
        vcol = sb("vcol", [P, N_ROWS + N_BROWS])
        modcol = sb("modcol", [P, DEPTH * 48, 2])
        acol = sb("acol", [P, KC, 2])
        modrow = sb("modrow", [4, 512])
        epsc = sb("epsc", [P, 1])
        c4 = sb("c4", [P, 4 * KC + P], F32R)
        c4j = c4[:, 0:4 * KC].rearrange("p (j s) -> p j s", s=4)
        lg = sb("lg", [P, 16])
        nlg = sb("nlg", [P, 16])
        blg = sb("blg", [P, 16])
        sinkb = sb("sinkb", [P, DEPTH * 8])
        stats = sb("stats", [P, 2, 20])

        eye = K[:, K_EYE:K_EYE + P]
        ones = K[:, K_ONES:K_ONES + P]
        blk = K[:, K_BLK:K_BLK + P]
        sel = K[0:4, K_SEL:K_SEL + 2]
        dist = K[:, K_DIST:K_DIST + DIST_W]
        ropeC = K[:, K_RC:K_RC + SX]
        ropeS = K[:, K_RS:K_RS + SX]

        xin, raw_s, wh_s, wl_s, crow, cws, rows_a, rows_b, csil, dec, lt1, lt2, lt3, *norm_start = overlay([
            ("xin", [P, 6, D], F32), ("raw_s", [P, 2048], F32), ("wh_s", [P, 2, 1024], F32R),
            ("wl_s", [P, 2, 1024], F32R), ("crow", [P, 2, KC], F32), ("cws", [P, DEPTH * 4, P], F32),
            ("rows_a", [N_ROWS, P], F32), ("rows_b", [N_BROWS, P], F32), ("csil", [P, KC, 2], F32),
            ("dec", [P, 16], F32), ("lt1", [P, 16], F32), ("lt2", [P, 16], F32), ("lt3", [P, 16], F32),
            ("nsq_s", [P, 2, NT], F32), ("nacc_s", [P, NT], F32), ("nrb_s", [P, NT], F32), ("nxz_s", [P, 3, NT], F32)])
        xr_start = xin[:, :, :].rearrange("p t d -> p (t d)").rearrange("p (k n) -> p k n", k=KC)
        norm_bufs = [("pad_a", [P, 2, NT], F32), ("nsq", [P, 2, NT], F32), ("nrb", [P, NT], F32), ("pad_b", [P, NT], F32),
                     ("nacc", [P, NT], F32), ("nxz", [P, 3, NT], F32)]
        overlay(norm_bufs)
        norm_later = tuple(made[n] for n in ("nsq", "nacc", "nrb", "nxz"))
        Z_DVE = (0,)
        Z_POOL = tuple(k for k in range(KC) if k not in Z_DVE)
        attn_base = [("aq", [P, 4, NT], F32), ("ak", [P, NT], F32), ("vtok", [P, 6, 384], F32)]
        attn_base += [("rg", [P, 2, NT], F32)]
        mix_base = attn_base + [("rq", [P, 2, NT], F32), ("rk", [P, 2, NT], F32), ("cu", [P, 2, NT], F32)]
        mixers = mix_base + [("cvt", [P, 6, 256], F32), ("vT", [P, 3, NT], F32), ("rtmp", [P, 2, SX], F32),
                             ("shuf", [P, SX], F32), ("cmst", [P, 2, 24], F32)]
        aq, ak, vtok, rg, rq, rk, cu, cvt, vT, rtmp, shuf, cmst = overlay(mixers)
        cmf = rtmp
        cmsq = vT[:, 0:2, :].rearrange("p a (t n) -> p (a t) n", n=256)
        T, TC, TD, osb, Pm = overlay([
            ("T", [P, 2, DIST_W], F32), ("TC", [P, 2, 640], F32), ("TD", [P, 640], F32), ("osb", [P, 2, NT], F32),
            ("Pm", [P, 3, SX], F32)],
            under=[(n + "_r", s, d) for n, s, d in mix_base])
        gn = Pm[:, :, :].rearrange("p a n -> p (a n)").rearrange("p (a n) -> p a n", a=2)
        oc, gsq = gn[:, 0, :], gn[:, 1, :]
        aqh, aql = zh[:, 2:6, :], zl[:, 2:6, :]
        akh, akl = (t[1][:, :, :].rearrange("p h n -> p (h n)")[:, 0:2 * NT].rearrange("p (g n) -> p g n", g=2)
                    for t in (wh, wl))
        s_at, pT = overlay([("s_at", [P, 2, 4, 640], F32), ("pT", [P, 5, SX], F32)],
                           under=[(n + "_a", s, d) for n, s, d in attn_base])
        hh, hl, gs, hf, raw_d, raw_m, wh_d, wl_d, wh_m, wl_m = overlay([
            ("hh", [P, 2, 2, NT], F32R), ("hl", [P, 2, 2, NT], F32R), ("gs", [P, NT], F32), ("hf", [P, NT], F32),
            ("raw_d", [P, 2048], F32), ("raw_m", [P, 2048], F32), ("wh_d", [P, 2, 1024], F32R),
            ("wl_d", [P, 2, 1024], F32R), ("wh_m", [P, 2, 1024], F32R), ("wl_m", [P, 2, 1024], F32R)])
        fz, = overlay([("fz", [P, KC, SX], F32)], under=[(n + "_f", s, d) for n, s, d in norm_bufs])
        otok, = overlay([("otok", [P, 4, D], F32)],
                        under=[(n + "_g", s, d) for n, s, d in norm_bufs] + [("fz_g", [P, KC, SX], F32)])

        ps = stack.enter_context(nc.psum_tensor("ps", [P, 8, 512], F32))

        def parts(l_or_w):
            return [(0, SX, 0)] + ([(SX, NT, 1)] if l_or_w else [])

        mod_v = [w_mod[l].rearrange("(p j) n -> p j n", j=KC) for l in range(DEPTH)]
        win_v = [w_in[l].rearrange("(k p) n -> p k n", p=P) for l in range(DEPTH)]
        wout_v = [w_out[l].rearrange("(k p) n -> p k n", p=P) for l in range(DEPTH)]
        gate_v = [w_gate[l].rearrange("(k p) n -> p k n", p=P) for l in range(DEPTH)]
        up_v = [w_up[l].rearrange("(k p) n -> p k n", p=P) for l in range(DEPTH)]
        down_v = [w_down[l].rearrange("(k p) n -> p k n", p=P) for l in range(DEPTH)]

        A_IN = [0, NP_IN + 4 + FSTEPS]
        A_OUT = [a + NP_IN for a in A_IN]
        A_GATE = [a + 4 for a in A_OUT]
        N_MODB = 2 * NP_IN
        B_UP = [N_MODB, N_MODB + FSTEPS]
        J_IN, J_FFN = 4, 4 + NP_IN

        def z_wait(eng, u, k):
            if k in Z_DVE:
                eng.wait_ge(sem("z_dve"), len(Z_DVE) * u + Z_DVE.index(k) + 1)
            else:
                eng.wait_ge(sem("z_pool"), len(Z_POOL) * u + Z_POOL.index(k) + 1)

        block = stack.enter_context(nc.Block())

        @block.sync
        def _(sp):
            def startup_panel(q):
                dst = [raw[0], raw[1], raw_s][q % 3]
                J, half = q // 2, q % 2
                sp.dma_start(dst[:, :].rearrange("p (j n) -> p j n", j=4),
                             mod_v[0][:, 4 * half:4 * half + 4, 512 * J:512 * J + 512]).then_inc(sem(f"st_ld{q % 3}"), 16)

            sp.dma_start(crow[:, 0, :], c[0].rearrange("(p j) -> p j", j=KC)).then_inc(sem("ld_c"), 16)
            sp.dma_start(crow[:, 1, :], c_ctx.rearrange("(p j) -> p j", j=KC)).then_inc(sem("ld_c"), 16)
            sp.dma_start(K[:, 0:K_MASK], consts[:, 0:K_MASK]).then_inc(sem("ld_x"), 16)
            sp.dma_start(xin[:, 0:4, :], x[0].rearrange("(t p) d -> p t d", p=P)).then_inc(sem("ld_x"), 16)
            sp.dma_start(xin[:, 4:6, :], ctx_in[0].rearrange("(t p) d -> p t d", p=P)).then_inc(sem("ld_x"), 16)
            for q in range(3):
                startup_panel(q)
            rows = 0
            for v, n in ((norm1_g.rearrange("l (k p) -> (l k) p", p=P), 16), (norm2_g.rearrange("l (k p) -> (l k) p", p=P), 16),
                         (final_norm_g.rearrange("(k p) -> k p", p=P), 8), (ret_norm_g.rearrange("l (k p) -> (l k) p", p=P), 4),
                         (cm_norm_g.rearrange("l (k p) -> (l k) p", p=P), 4)):
                sp.dma_start(rows_a[rows:rows + n, :], v).then_inc(sem("ld_small"), 16)
                rows += n
            sp.dma_start(rows_b[:, :], b_mod.rearrange("l (k p) -> (l k) p", p=P)).then_inc(sem("ld_small"), 16)
            sp.dma_start(dec[:, 0:8], ret_decay_f.rearrange("l h -> (l h)").partition_broadcast(P)).then_inc(sem("ld_small"), 16)
            sp.dma_start(dec[:, 8:16], ret_decay_b.rearrange("l h -> (l h)").partition_broadcast(P)).then_inc(sem("ld_small"), 16)
            sp.dma_start(sinkb[:, :], attn_sink.rearrange("l h -> (l h)").partition_broadcast(P)).then_inc(sem("ld_small"), 16)
            sp.dma_start(cws[:, :, :], cm_w_s.rearrange("l g p q -> p (l g) q")).then_inc(sem("ld_small"), 16)
            for l in range(DEPTH):
                for g in range(4):
                    sp.dma_start(bsb[64 * (g % 2):64 * (g % 2) + 64, l, g // 2, :],
                                 cm_b_s[l, g].partition_broadcast(64)).then_inc(sem("ld_small"), 16)
            for q in range(3, 8):
                sp.wait_ge(sem("st_hi"), q - 2)
                sp.wait_ge(sem("st_lo"), q - 2)
                startup_panel(q)
            sp.dma_start(K[:, K_MASK:K_ALL], consts[:, K_MASK:K_ALL]).then_inc(sem("ld_tables"), 16)

            def a_free(a, first=False):
                sp.wait_ge(sem("st_hi" if first else "hiA"), 7 if first else 2 * a)
                sp.wait_ge(sem("st_lo" if first else "loA"), 7 if first else 2 * a)

            def b_free(b, first=False):
                if first:
                    sp.wait_ge(sem("st_hi"), 8)
                    sp.wait_ge(sem("st_lo"), 8)
                else:
                    sp.wait_ge(sem("hiB"), 2 * b)
                    sp.wait_ge(sem("lo_modb"), 2 * b)

            def load_in(l, p):
                a_free(A_IN[l] + p, first=(l == 0 and p == 0))
                dst = raw[0][:, :].rearrange("p (k n) -> p k n", k=KC)
                name = PANELS[p]
                if name.startswith("aq"):
                    for h in range(2):
                        q = 2 * int(name[2]) + h
                        for part in range(2):
                            col = C_AQ + HD * (q + 4 * part)
                            at = P * h + HD * part
                            sp.dma_start(dst[:, :, at:at + HD], win_v[l][:, :, col:col + HD]).then_inc(sem(f"ld_in{l}"), 16)
                else:
                    sp.dma_start(dst, win_v[l][:, :, PANEL_COL[name]:PANEL_COL[name] + 256]).then_inc(sem(f"ld_in{l}"), 16)

            def load_modb(b):
                b_free(b, first=(b == 0))
                J, half = J_IN + b // 2, b % 2
                l, Jl = J // 12, J % 12
                sp.dma_start(raw[1][:, :].rearrange("p (j n) -> p j n", j=4),
                             mod_v[l][:, 4 * half:4 * half + 4, 512 * Jl:512 * Jl + 512]).then_inc(sem("ld_modb"), 16)

            def load_out(l, p):
                a_free(A_OUT[l] + p)
                dst = raw[0][:, :].rearrange("p (k n) -> p k n", k=KC)
                cols = slice(256 * p, 256 * p + 256)
                sp.dma_start(dst[:, 0:2, :], wout_v[l][:, 0:2, cols]).then_inc(sem(f"ld_out{l}"), 16)
                for part in range(2):
                    rows = w_out[l, 256 + 256 * part:512 + 256 * part, cols].rearrange("(k p) n -> p k n", p=HD)
                    sp.dma_start(dst[64 * part:64 * part + 64, 2:6, :], rows).then_inc(sem(f"ld_out{l}"), 16)
                sp.dma_start(dst[:, 6:8, :], wout_v[l][:, 6:8, cols]).then_inc(sem(f"ld_out{l}"), 16)

            def load_ffn(l, s):
                a_free(A_GATE[l] + s)
                sp.dma_start(raw[0][:, :].rearrange("p (k n) -> p k n", k=KC),
                             gate_v[l][:, :, bass.ds(256 * s, 256)]).then_inc(sem(f"ld_gate{l}"), 16)
                up = FSTEPS * l + s
                if l and type(s) is int and s == 0:
                    sp.wait_ge(sem("loD0"), 2 * FSTEPS)
                if type(up) is int and up == 0:
                    sp.wait_ge(sem("lo_modb"), 2 * N_MODB)
                else:
                    sp.wait_ge(sem("loB"), 2 * up)
                sp.dma_start(raw[1][:, :].rearrange("p (k n) -> p k n", k=KC),
                             up_v[l][:, :, bass.ds(256 * s, 256)]).then_inc(sem(f"ld_up{l}"), 16)

            def load_down(l, s, first=False):
                if not first:
                    sp.wait_ge(sem(f"hiD{l}"), 2 * s)
                    sp.wait_ge(sem(f"loD{l}"), 2 * s)
                sp.dma_start(raw_d[:, :].rearrange("p (k n) -> p k n", k=2),
                             down_v[l][:, bass.ds(2 * s, 2), :]).then_inc(sem(f"ld_down{l}"), 16)

            def load_modm(s, half, first=False):
                if not first:
                    sp.wait_ge(sem("hiM"), 4 * s + 2 * half)
                    sp.wait_ge(sem("loM"), 4 * s + 2 * half)
                sp.dma_start(raw_m[:, :].rearrange("p (j n) -> p j n", j=4),
                             mod_v[1][:, 4 * half:4 * half + 4, bass.ds(512 * (s + 1), 512)]).then_inc(sem("ld_modm"), 16)

            load_in(0, 0)
            load_modb(0)
            for p in range(NP_IN):
                load_modb(2 * p + 1)
                if p + 1 < NP_IN:
                    load_in(0, p + 1)
                    load_modb(2 * p + 2)
            for l in range(DEPTH):
                if l:
                    for p in range(NP_IN):
                        load_in(l, p)
                for p in range(4):
                    load_out(l, p)
                load_ffn(l, 0)
                sp.wait_ge(sem("use_a"), 2 * A_GATE[l])
                load_down(l, 0, first=True)
                if l == 0:
                    load_modm(0, 0, first=True)
                    load_modm(0, 1)
                with sp.Fori(1, FSTEPS - 1) as s:
                    load_ffn(l, s)
                    if l == 0:
                        load_modm(s, 0)
                        load_modm(s, 1)
                    load_down(l, s)
                load_ffn(l, FSTEPS - 1)
                if l == 0:
                    load_modm(FSTEPS - 1, 0)
                    load_modm(FSTEPS - 1, 1)
                sp.wait_ge(sem("loB"), 2 * FSTEPS * (l + 1))
                sp.dma_start(raw[1][:, :].rearrange("p (k n) -> p k n", k=2),
                             down_v[l][:, 2 * FSTEPS - 2:2 * FSTEPS, :]).then_inc(sem("ld_down_last"), 16)

            for g in range(8):
                half, t = g // 4, g % 4
                sp.wait_ge(sem("fin_evac"), g + 1)
                sp.dma_start(out[0, P * t:P * t + P, 512 * half:512 * half + 512],
                             otok[:, t, 512 * half:512 * half + 512]).then_inc(sem("stored"), 16)
            sp.wait_ge(sem("stored"), 16 * 8)

        @block.gpsimd
        def _(pool):
            ch = Chain(pool, sem("pool_chain"))

            def lo(dst, src, hi, done):
                nc.gpsimd.tensor_tensor(dst, src, hi.bitcast(F32), ALU.subtract).then_inc(sem(done), 1)

            def raw_half(buf, h):
                return buf[:, :].rearrange("p (k j n) -> p j k n", k=KC, j=2)[:, h]

            def slot_half(t, h):
                return t[:, h, :].rearrange("p (k n) -> p k n", k=KC)

            def lo_a(a, h):
                pool.wait_ge(sem("hiA"), 2 * a + h + 1)
                lo(slot_half(wl[0], h), raw_half(raw[0], h), slot_half(wh[0], h), "loA")

            def lo_b(b, h):
                pool.wait_ge(sem("hiB"), 2 * b + h + 1)
                lo(slot_half(wl[1], h), raw_half(raw[1], h), slot_half(wh[1], h), "loB")

            def lo_modm(m, h):
                pool.wait_ge(sem("hiM"), m + 1)
                lo(wl_m[:, h, :], raw_m[:, 1024 * h:1024 * h + 1024], wh_m[:, h, :], "loM")

            def lo_down(l, s):
                for h in range(2):
                    pool.wait_ge(sem(f"hiD{l}"), 2 * s + h + 1)
                    lo(wl_d[:, h, :], raw_d[:, 1024 * h:1024 * h + 1024], wh_d[:, h, :], f"loD{l}")

            def norm(u, W):
                nxz = (norm_later if u else norm_start)[3]
                for k in Z_POOL:
                    pool.wait_ge(sem("nzf_rdy"), 8 * u + k + 1)
                    pool.wait_ge(sem("zh_rdy"), 8 * u + k + 1)
                    lo(zl[:, k, 0:W], nxz[:, k % 3, 0:W], zh[:, k, 0:W], "z_pool")

            pool.wait_ge(sem("nrms_inv"), 1)
            for k in range(KC):
                ch.then(nc.gpsimd.tensor_tensor(xr_start[:, k, :], xT[:, k, :], norm_start[2][:, :], ALU.mult))
            lo_a(0, 0)
            lo_a(0, 1)
            norm(0, NT)
            with pool.Fori(1, NP_IN + 1) as a:
                lo_a(a, 0)
                lo_a(a, 1)
            for l in range(DEPTH):
                if l:
                    norm(2, NT)
                    with pool.Fori(A_IN[l] + 1, A_OUT[l] + 1) as a:
                        lo_a(a, 0)
                        lo_a(a, 1)

                pool.wait_ge(sem("loA"), 2 * A_OUT[l] + 2)
                for kv in range(2):
                    pool.wait_ge(sem(f"qk_hi{l}"), kv + 1)
                    rows, rest = slice(HD * kv, HD * kv + HD), slice(HD - HD * kv, P - HD * kv)
                    zeros = blk[rest, HD * kv:HD * kv + HD].unsqueeze(1).to_broadcast([HD, NT // HD, HD])
                    for t in (akh, akl):
                        ch.link(nc.gpsimd.tensor_tensor(t[rest, kv, :].rearrange("p (a n) -> p a n", n=HD), zeros, zeros,
                                                        ALU.subtract))
                    lo(akl[rows, kv, :], ak[rows, :], akh[rows, kv, :], f"qk_lo{l}")
                    pool.wait_ge(sem(f"qk_lo{l}"), kv + 1)
                for q in range(4):
                    W = NT if l == 0 else SX
                    pool.wait_ge(sem(f"qk_hi{l}"), 3 + q)
                    lo(aql[:, q, 0:W], aq[:, q, 0:W], aqh[:, q, 0:W], f"qk_lo{l}")
                with pool.Fori(A_OUT[l] + 1, A_GATE[l] + 1) as a:
                    lo_a(a, 0)
                    lo_a(a, 1)
                lo_b(B_UP[l], 0)
                lo_b(B_UP[l], 1)
                norm(2 * l + 1, NT if l == 0 else SX)
                if l == 0:
                    lo_modm(0, 0)
                    lo_modm(1, 1)

                def ffn_step(s, first=False, last=False):
                    if not first:
                        lo_down(l, s - 1)
                    for h in range(2):
                        if not (last and l):
                            lo_a(A_GATE[l] + s + 1, h)
                        if not last:
                            lo_b(B_UP[l] + s + 1, h)
                        if l == 0 and not (last and h):
                            lo_modm(4 * s + 2 * h + 2, 0)
                            lo_modm(4 * s + 2 * h + 3, 1)

                ffn_step(0, first=True)
                with pool.Fori(1, FSTEPS - 1) as s:
                    ffn_step(s)
                ffn_step(FSTEPS - 1, last=True)
                for h in range(2):
                    pool.wait_ge(sem(f"hiD{l}"), 2 * FSTEPS - 1 + h)
                    lo(wl[1][:, h, :], raw[1][:, 1024 * h:1024 * h + 1024], wh[1][:, h, :], f"loD{l}")

        @block.scalar
        def _(act):
            ch = Chain(act, sem("act_chain"))

            def copy(dst, src):
                return nc.scalar.activation(dst, src, ACT.Copy)

            def raw_half(buf, h):
                return buf[:, :].rearrange("p (k j n) -> p j k n", k=KC, j=2)[:, h]

            def slot_half(t, h):
                return t[:, h, :].rearrange("p (k n) -> p k n", k=KC)

            def hi_a(a, h, loaded, value, first=False):
                act.wait_ge(sem(loaded), value)
                if first:
                    act.wait_ge(sem("st_use"), 7)
                else:
                    act.wait_ge(sem("use_a"), 2 * a + h - 1)
                copy(slot_half(wh[0], h), raw_half(raw[0], h)).then_inc(sem("hiA"), 1)

            def hi_modb(b, h, first=False):
                act.wait_ge(sem("ld_modb"), 16 * (b + 1))
                if first:
                    act.wait_ge(sem("st_use"), 8)
                else:
                    act.wait_ge(sem("use_b"), 2 * b + h - 1)
                copy(wh[1][:, h, :], raw[1][:, 1024 * h:1024 * h + 1024]).then_inc(sem("hiB"), 1)

            def hi_b(l, s, h):
                act.wait_ge(sem(f"ld_up{l}"), 16 * (s + 1))
                act.wait_ge(sem("use_b"), 2 * (B_UP[l] + s) + h - 1)
                copy(slot_half(wh[1], h), raw_half(raw[1], h)).then_inc(sem("hiB"), 1)

            def hi_modm(m, h, first=False, panel=None):
                act.wait_ge(sem("ld_modm"), 16 * (panel + 1))
                if not first:
                    act.wait_ge(sem("use_m"), m - 1)
                copy(wh_m[:, h, :], raw_m[:, 1024 * h:1024 * h + 1024]).then_inc(sem("hiM"), 1)

            def hi_down(l, s, first=False):
                act.wait_ge(sem(f"ld_down{l}"), 16 * (s + 1))
                if not first:
                    act.wait_ge(sem("dn1_mm0" if l == 0 else "dn0_mm1"), KC * s)
                elif l:
                    act.wait_ge(sem("dn1_mm0"), KC * FSTEPS)
                for h in range(2):
                    copy(wh_d[:, h, :], raw_d[:, 1024 * h:1024 * h + 1024]).then_inc(sem(f"hiD{l}"), 1)

            def square(u, k, W):
                nsq = (norm_later if u else norm_start)[0]
                if k >= 2:
                    act.wait_ge(sem("nacc_rdy"), 8 * u + k - 1)
                nc.scalar.activation(nsq[:, k % 2, 0:W], xT[:, k, 0:W], ACT.Square).then_inc(sem("nsq_rdy"), 1)

            def norm_root(u, W):
                nrb = (norm_later if u else norm_start)[2]
                act.wait_ge(sem("nst_mm"), u + 1)
                for c0, c1, s in [(0, SX, 0)] + ([(SX, NT, 1)] if W == NT else []):
                    last = nc.scalar.activation(nrb[:, c0:c1], ps[:, s, 0:c1 - c0], ACT.Sqrt, bias=epsc[:, 0:1], scale=1.0 / D)
                last.then_inc(sem("nrms_rdy"), 1)

            def norm_hi(u, W):
                nxz = (norm_later if u else norm_start)[3]
                for k in range(KC):
                    act.wait_ge(sem("nzf_rdy"), 8 * u + k + 1)
                    copy(zh[:, k, 0:W], nxz[:, k % 3, 0:W]).then_inc(sem("zh_rdy"), 1)

            act.wait_ge(sem("ld_c"), 32)
            ch.link(nc.scalar.activation(csil[:, :, 0], crow[:, 0, :], ACT.Silu))
            nc.scalar.activation(csil[:, :, 1], crow[:, 1, :], ACT.Silu).then_inc(sem("csil_rdy"), 1)
            for k in range(KC):
                if k in (2, 4, 6):
                    q = k // 2 - 1
                    act.wait_ge(sem(f"st_ld{q}"), 16)
                    copy([wh[0], wh[1], wh_s][q][:, :, :].rearrange("p h n -> p (h n)"),
                         [raw[0], raw[1], raw_s][q][:, :]).then_inc(sem("st_hi"), 1)
                act.wait_ge(sem("xt_mm"), k + 1)
                copy(xT[:, k, 0:SX], ps[:, k % 2, :])
                copy(xT[:, k, SX:NT], ps[:, 2 + k % 2, 0:SC]).then_inc(sem("xt_evac"), 1)
                if k:
                    act.wait_ge(sem("xt_evac"), k)
                    square(0, k - 1, NT)
            act.wait_ge(sem("xt_evac"), KC)
            square(0, KC - 1, NT)
            act.wait_ge(sem("ws_mm"), 1)
            for l in range(DEPTH):
                copy(wsT[:, l, :], ps[:, 5 + l, :])
            for q in range(3, 8):
                act.wait_ge(sem(f"st_ld{q % 3}"), 16 * (q // 3 + 1))
                act.wait_ge(sem("st_use"), q - 2)
                copy([wh[0], wh[1], wh_s][q % 3][:, :, :].rearrange("p h n -> p (h n)"),
                     [raw[0], raw[1], raw_s][q % 3][:, :]).then_inc(sem("st_hi"), 1)
                if q == 3:
                    norm_root(0, NT)
                if q == 4:
                    act.wait_ge(sem("lg_ax"), 1)
                    nc.scalar.activation(lt2[:, :], lt1[:, :], ACT.Exp, scale=-1.0).then_inc(sem("lg_e"), 1)

            for l in range(DEPTH):
                W = NT if l == 0 else SX

                ld = [0]
                for name in PANELS:
                    ld.append(ld[-1] + (64 if name.startswith("aq") else 16))
                if l == 0:
                    hi_a(0, 0, "ld_in0", ld[1], first=True)
                    hi_a(0, 1, "ld_in0", ld[1], first=True)
                    norm_hi(0, NT)
                    hi_modb(0, 0, first=True)
                    hi_modb(0, 1, first=True)
                else:
                    norm_hi(2, NT)
                a0 = A_IN[l]
                rope_n = 0

                def to_tokens_out(p):
                    if p == V_AT:
                        for v in range(3):
                            act.wait_ge(sem(f"vtr_mm{l}"), v + 1)
                            cols = slice(P * v, P * v + P)
                            copy(vtok[:, 4:6, cols], ps[:, 7, 0:SC].rearrange("p (t n) -> p t n", t=2))
                            copy(vtok[:, 0:4, cols], ps[:, 5 + v % 2, :].rearrange("p (t n) -> p t n", t=4)).then_inc(sem(f"vtr_ev{l}"), 1)
                    if p == CV_AT:
                        for v in range(2):
                            act.wait_ge(sem(f"vtr_mm{l}"), 4 + v)
                            cols = slice(P * v, P * v + P)
                            if l == 0:
                                copy(cvt[:, 4:6, cols], ps[:, 7, 0:SC].rearrange("p (t n) -> p t n", t=2))
                            copy(cvt[:, 0:4, cols], ps[:, 5 + v % 2, :].rearrange("p (t n) -> p t n", t=4)).then_inc(sem(f"vtr_ev{l}"), 1)

                for p, name in enumerate(PANELS):
                    for h in range(2):
                        n = 2 * p + h
                        act.wait_ge(sem("use_a"), 2 * (a0 + p) + h + 1)
                        if p + 1 < NP_IN:
                            hi_a(a0 + p + 1, h, f"ld_in{l}", ld[p + 2])
                        else:
                            hi_a(a0 + p + 1, h, f"ld_out{l}", 64)
                        ctx = l == 0 or p < NP_CTX
                        px, pc = ps[:, h, :], ps[:, 2 + h, 0:SC]
                        is_rope = name in ("rk", "rq", "aq0", "aq1") or (name == "akav" and h == 0)
                        if is_rope:
                            dst = {"rk": rk[:, h], "rq": rq[:, h], "akav": ak, "aq0": aq[:, h], "aq1": aq[:, 2 + h]}[name]
                            if ctx:
                                copy(dst[:, SX:NT], pc)
                            if rope_n >= 2:
                                act.wait_ge(sem(f"rope_done{l}"), rope_n - 1)
                            copy(rtmp[:, rope_n % 2, :], px).then_inc(sem(f"ev_in{l}"), 1)
                            rope_n += 1
                        else:
                            func = {"cv": ACT.Gelu_apprx_tanh, "cu": ACT.Gelu_apprx_tanh, "rg": ACT.Silu}.get(name, ACT.Copy)
                            dst = {"rv": vT[:, h], "akav": vT[:, 2], "cv": vT[:, h], "cu": cu[:, h], "rg": rg[:, h]}[name]
                            if name == "cv" and h == 0:
                                act.wait_ge(sem(f"vtr_mm{l}"), 3)
                            if ctx:
                                nc.scalar.activation(dst[:, SX:NT], pc, func)
                            nc.scalar.activation(dst[:, 0:SX], px, func).then_inc(sem(f"ev_in{l}"), 1)
                        if l == 0 and h == 0:
                            hi_modb(2 * p + 1, 0)
                            hi_modb(2 * p + 1, 1)
                        if h == 1:
                            to_tokens_out(p)
                        if l == 0 and h == 1 and p + 1 < NP_IN:
                            hi_modb(2 * p + 2, 0)
                            hi_modb(2 * p + 2, 1)
                        if p == NP_IN - 1 and h == 0:
                            act.wait_ge(sem("cm_var"), l + 1)
                            nc.scalar.activation(cmst[:, 1, 0:4 * (W // P)], cmst[:, 1, 0:4 * (W // P)], ACT.Sqrt
                                                 ).then_inc(sem("cm_std"), 1)
                def tables(h):
                    act.wait_ge(sem(f"T_arg{l}"), h + 1)
                    i, b = l * 4 + h, h % 2
                    nc.scalar.activation(T[:, b, :], T[:, b, :], ACT.Exp)
                    nc.scalar.activation(TC[:, b, :], dist[:, 0:640], ACT.Exp, bias=blg[:, i:i + 1], scale=lg[:, i:i + 1])
                    if h:
                        act.wait_ge(sem(f"T_done{l}"), h)
                    nc.scalar.activation(TD[:, :], dist[:, 0:640], ACT.Exp, bias=blg[:, 8 + i:9 + i],
                                         scale=nlg[:, 8 + i:9 + i]).then_inc(sem(f"T_exp{l}"), 1)

                if l == 0:
                    act.wait_ge(sem("ld_tables"), 16)
                tables(0)
                def copy_out(r):
                    act.wait_ge(sem(f"ret_pv{l}"), (r + 1) * (16 if l == 0 else 12))
                    if l == 0:
                        copy(osb[:, r, SX:NT], ps[:, 6, 0:SC])
                    copy(osb[:, r, 0:SX], ps[:, 5, :]).then_inc(sem(f"osb_rdy{l}"), 1)

                tables(1)
                e = 0
                for c0, c1, s in parts(l == 0):
                    for r in range(2):
                        act.wait_ge(sem(f"cm_f{l}"), e + 1)
                        copy(zh[:, 6 + r, c0:c1], cmf[:, e % 2, 0:c1 - c0]).then_inc(sem(f"cm_hi{l}"), 1)
                        e += 1
                act.wait_ge(sem("use_a"), 2 * A_OUT[l])
                act.wait_ge(sem("use_b"), 2 * B_UP[l])
                act.wait_ge(sem(f"rope_done{l}"), 9)
                for kv in range(2):
                    rows = slice(HD * kv, HD * kv + HD)
                    copy(akh[rows, kv, :], ak[rows, :]).then_inc(sem(f"qk_hi{l}"), 1)
                for q in range(4):
                    copy(aqh[:, q, 0:W], aq[:, q, 0:W]).then_inc(sem(f"qk_hi{l}"), 1)
                tables(2)
                copy_out(0)
                tables(3)
                copy_out(1)
                gn_jobs = [(r, c0, c1) for r in range(2) for c0, c1, s in parts(l == 0)]

                def gn_square(j):
                    if j < len(gn_jobs):
                        n = gn_jobs[j][2] - gn_jobs[j][1]
                        act.wait_ge(sem(f"oc_rdy{l}"), j + 1)
                        nc.scalar.activation(gsq[:, 0:n], oc[:, 0:n], ACT.Square).then_inc(sem(f"gsq_rdy{l}"), 1)

                def gn_root(j):
                    if j < len(gn_jobs):
                        n = gn_jobs[j][2] - gn_jobs[j][1]
                        act.wait_ge(sem(f"gvar_mm{l}"), j + 1)
                        nc.scalar.activation(gsq[:, 0:n], ps[:, 4, 0:n], ACT.Sqrt, bias=epsc[:, 0:1], scale=1.0).then_inc(sem(f"gstd_rdy{l}"), 1)

                def gn_hi(j):
                    if j < len(gn_jobs):
                        r, c0, c1 = gn_jobs[j]
                        act.wait_ge(sem(f"ret_f{l}"), j + 1)
                        copy(zh[:, r, c0:c1], oc[:, 0:c1 - c0]).then_inc(sem(f"ret_hi{l}"), 1)

                blocks = list(range(4)) + ([4, 5] if l == 0 else [])
                units = [(i, kv) for i in blocks for kv in range(2)]
                g = 0

                def local(i):
                    return list(range(max(i - 1, 0), min(i + 1, 3) + 1)) if i < 4 else []

                def softmax_and_transposed(u):
                    nonlocal g
                    before = len(local(units[u - 1][0])) + 2 if u else 0
                    for step in range(max(before, 4)):
                        if step < before:
                            act.wait_ge(sem(f"at_tr{l}"), g + 1)
                            if step == 0 and u > 1:
                                act.wait_ge(sem(f"at_o{l}"), u - 1)
                            copy(pT[:, step, :], ps[:, 5 + g % 2, :]).then_inc(sem(f"at_pt{l}"), 1)
                            g += 1
                        if u < len(units) and step < 4:
                            wd = len(local(units[u][0])) * P + SC
                            if step == 0:
                                act.wait_ge(sem(f"at_nb{l}"), u + 1)
                                nc.scalar.activation(stats[:, u % 2, 12:16], stats[:, u % 2, 8:12], ACT.Exp)
                            last = nc.scalar.activation(s_at[:, u % 2, step, 0:wd], s_at[:, u % 2, step, 0:wd], ACT.Exp,
                                                        bias=stats[:, u % 2, 4 + step:5 + step],
                                                        accum_out=stats[:, u % 2, 16 + step:17 + step])
                            if step == 3:
                                last.then_inc(sem(f"at_exp{l}"), 1)
                    if u and units[u - 1][1] == 1:
                        i = units[u - 1][0]
                        act.wait_ge(sem(f"at_o{l}"), u)
                        copy(zh[:, 2:6, P * i:P * i + P], ps[:, 7, :].rearrange("p (c q) -> p c q", c=4)).then_inc(sem(f"at_hi{l}"), 1)

                for u in range(len(units) + 1):
                    softmax_and_transposed(u)
                    if u % 2 == 0:
                        gn_square(u // 2)
                        gn_root(u // 2)
                    else:
                        gn_hi(u // 2)

                for p in range(4):
                    for h in range(2):
                        a = A_OUT[l] + p + 1
                        if p < 3:
                            hi_a(a, h, f"ld_out{l}", 64 * (p + 2))
                        else:
                            hi_a(a, h, f"ld_gate{l}", 16)
                        if p or h:
                            act.wait_ge(sem(f"ev_out{l}"), 2 * p + h)
                            square(2 * l + 1, 2 * p + h - 1, W)
                act.wait_ge(sem(f"ev_out{l}"), KC)
                square(2 * l + 1, KC - 1, W)
                norm_root(2 * l + 1, W)
                for h in range(2):
                    hi_b(l, 0, h)
                norm_hi(2 * l + 1, W)
                if l == 0:
                    hi_modm(0, 0, first=True, panel=0)
                    hi_modm(1, 1, first=True, panel=0)

                def chunk(s, h, par):
                    n = 2 * s + h
                    act.wait_ge(sem("use_b"), 2 * (B_UP[l] + s) + h + 1)
                    act.wait_ge(sem(f"ev_h{l}"), n + 1)
                    nc.scalar.activation(gs[:, 0:SX], ps[:, 3 * h, :], ACT.Silu).then_inc(sem(f"gs_rdy{l}"), 1)
                    if l == 0:
                        nc.scalar.activation(gs[:, SX:NT], ps[:, 3 * h + 2, 0:SC], ACT.Silu).then_inc(sem(f"gs_rdy{l}"), 1)
                    return n

                def chunk_hi(s, h, par):
                    n = 2 * s + h
                    act.wait_ge(sem(f"ev_h{l}"), n + 2)
                    copy(hh[:, par, h, 0:W], hf[:, 0:W]).then_inc(sem(f"hh_rdy{l}"), 1)

                def ffn_step(s, par, first=False, last=False, first_down=False):
                    if not first:
                        hi_down(l, s - 1, first=first_down)
                    for h in range(2):
                        chunk(s, h, par)
                        if not last:
                            hi_a(A_GATE[l] + s + 1, h, f"ld_gate{l}", 16 * (s + 2))
                            hi_b(l, s + 1, h)
                        elif l == 0:
                            hi_a(A_IN[1], h, "ld_in1", 16)
                        if l == 0 and not (last and h):
                            nxt = 2 * s + h + 1
                            hi_modm(4 * s + 2 * h + 2, 0, panel=nxt)
                            hi_modm(4 * s + 2 * h + 3, 1, panel=nxt)
                        chunk_hi(s, h, par)

                ffn_step(0, 0, first=True)
                ffn_step(1, 1, first_down=True)
                with act.Fori(0, 4) as i:
                    ffn_step(2 * i + 2, 0)
                    ffn_step(2 * i + 3, 1)
                ffn_step(FSTEPS - 1, 0, last=True)
                act.wait_ge(sem("ld_down_last"), 16 * (l + 1))
                act.wait_ge(sem("use_b"), 2 * (B_UP[l] + FSTEPS))
                for h in range(2):
                    copy(wh[1][:, h, :], raw[1][:, 1024 * h:1024 * h + 1024]).then_inc(sem(f"hiD{l}"), 1)
                W = NT if l == 0 else SX
                for k in range(KC):
                    act.wait_ge(sem(f"ev_d{l}"), KC * (FSTEPS - 1) + k + 2)
                    if l == 0:
                        act.wait_ge(sem("ev_dc0"), KC * (FSTEPS - 1) + k + 1)
                    square(2 * l + 2, k, W)
                norm_root(2 * l + 2, W)

            for half in range(2):
                for t in range(4):
                    g = 4 * half + t
                    act.wait_ge(sem("fin_mm"), g + 1)
                    copy(otok[:, t, 512 * half:512 * half + 512], ps[:, 2 + g % 2, :]).then_inc(sem("fin_evac"), 1)

        @block.vector
        def _(dve):
            ch = Chain(dve, sem("dve_chain"))
            V = nc.vector

            def mod_copy(done, value):
                dve.wait_ge(sem(done), value)
                V.tensor_copy(modrow[:, :], ps[0:4, MODBANK[0], :]).then_inc(sem("modrow_rdy"), 1)

            MODBANK, MODCOLS = [4], [7]

            def mod_add(J):
                dve.wait_ge(sem("mod_fin"), J + 1)
                b = vcol[:, bass.ds(N_ROWS + 4 * J, 4)].unsqueeze(2).to_broadcast([P, 4, 2])
                V.tensor_tensor(modcol[:, bass.ds(4 * J, 4), :],
                                ps[:, MODCOLS[0], 256:264].rearrange("p (i s) -> p i s", i=4), b, ALU.add).then_inc(sem("modcol_rdy"), 1)

            ch.link(V.memset(epsc[:, :], EPS))
            ch.link(V.memset(c4[:, :].bitcast(F32), 0.0))
            dve.wait_ge(sem("csil_rdy"), 1)
            ch.link(V.tensor_copy(c4j[:, :, 0:2], csil[:, :, :]))
            V.tensor_tensor(c4j[:, :, 2:4], csil[:, :, :], c4j[:, :, 0:2].bitcast(F32), ALU.subtract).then_inc(sem("c4_rdy"), 1)

            def lo_start(q):
                dve.wait_ge(sem("st_hi"), q + 1)
                wl_q, wh_q, raw_q = [(wl[0], wh[0], raw[0]), (wl[1], wh[1], raw[1]), (wl_s, wh_s, raw_s)][q % 3]
                V.tensor_tensor(wl_q[:, :, :].rearrange("p h n -> p (h n)"), raw_q[:, :],
                                wh_q[:, :, :].rearrange("p h n -> p (h n)").bitcast(F32), ALU.subtract).then_inc(sem("st_lo"), 1)

            def add_square(u, k, W):
                nsq, nacc = (norm_later if u else norm_start)[0:2]
                dve.wait_ge(sem("nsq_rdy"), 8 * u + k + 1)
                if k:
                    dve.wait_ge(sem("nacc_rdy"), 8 * u + k)
                    ins = V.tensor_tensor(nacc[:, 0:W], nacc[:, 0:W], nsq[:, k % 2, 0:W], ALU.add)
                else:
                    ins = V.tensor_copy(nacc[:, 0:W], nsq[:, 0, 0:W])
                ins.then_inc(sem("nacc_rdy"), 1)

            def norm_parts(W):
                return [(0, SX, 0)] + ([(SX, NT, 1)] if W == NT else [])

            def norm_recip(u, W):
                nrb = (norm_later if u else norm_start)[2]
                dve.wait_ge(sem("nrms_rdy"), u + 1)
                V.reciprocal(nrb[:, 0:W], nrb[:, 0:W]).then_inc(sem("nrms_inv"), 1)
                dve.wait_ge(sem("nrms_inv"), u + 1)

            def log_decay_a():
                dve.wait_ge(sem("ld_small"), 16 * 18)
                ch.link(V.tensor_scalar(lt3[:, :], dec[:, :], -1.0, None, ALU.mult))
                V.tensor_tensor(lt1[:, :], dec[:, :], lt3[:, :], ALU.max).then_inc(sem("lg_ax"), 1)

            def log_decay_b():
                dve.wait_ge(sem("lg_e"), 1)
                ch.link(V.tensor_scalar(lt1[:, :], lt2[:, :], 2.0, None, ALU.add))
                ch.link(V.reciprocal(lt3[:, :], lt1[:, :]))
                ch.link(V.tensor_tensor(lt2[:, :], lt2[:, :], lt3[:, :], ALU.mult))
                ch.link(V.tensor_tensor(lt3[:, :], lt2[:, :], lt2[:, :], ALU.mult))
                ch.link(V.tensor_scalar(lt1[:, :], lt3[:, :], 1.0 / 15, 1.0 / 13, ALU.mult, ALU.add))
                for m in (11, 9, 7, 5, 3, 1):
                    ch.link(V.tensor_tensor(lt1[:, :], lt1[:, :], lt3[:, :], ALU.mult))
                    ch.link(V.tensor_scalar(lt1[:, :], lt1[:, :], 1.0 / m, None, ALU.add))
                ch.link(V.tensor_tensor(lt1[:, :], lt1[:, :], lt2[:, :], ALU.mult))
                ch.link(V.tensor_scalar(lt1[:, :], lt1[:, :], 2.0, None, ALU.mult))
                ch.link(V.tensor_scalar(lt3[:, :], dec[:, :], 0.0, None, ALU.min))
                ch.link(V.tensor_tensor(lg[:, :], lt3[:, :], lt1[:, :], ALU.subtract))
                ch.link(V.tensor_scalar(nlg[:, :], lg[:, :], -1.0, None, ALU.mult))
                ch.link(V.tensor_scalar(blg[:, 0:8], lg[:, 0:8], float(SX), None, ALU.mult))
                ch.link(V.tensor_scalar(blg[:, 8:16], lg[:, 8:16], float(SC), None, ALU.mult))

            for k in range(KC):
                add_square(0, k, NT)
                if k in (2, 4, 6):
                    lo_start(k // 2 - 1)
            dve.wait_ge(sem("vc_mm"), 1)
            V.tensor_copy(vcol[:, :], ps[:, 7, 0:N_ROWS + N_BROWS]).then_inc(sem("vc_evac"), 1)
            mod_copy("st_use", 2)
            for q in range(3, 8):
                lo_start(q)
                if q == 3:
                    log_decay_a()
                if q == 4:
                    norm_recip(0, NT)
                if q % 2 == 1 and q < 7:
                    mod_add(q // 2 - 1)
                    mod_copy("st_use", 2 * (q // 2) + 2)
            mod_add(2)
            mod_copy("st_use", 8)
            mod_add(3)
            def norm(u, W):
                l, second = u // 2, u % 2
                nrb, nxz = (norm_later if u else norm_start)[2:4]
                if u:
                    add_square(u, KC - 1, W)
                if u < 4:
                    dve.wait_ge(sem("modcol_rdy"), (J_IN, J_FFN, 24, 24)[u])
                    g0 = (R_N2 if second else R_N1) + KC * l
                    v = 4 if second else 1
                    gb = vcol[:, g0:g0 + KC].unsqueeze(2).to_broadcast([P, KC, 2])
                    ch.link(V.scalar_tensor_tensor(acol[:, :, :], modcol[:, 48 * l + KC * v:48 * l + KC * v + KC, :], 1.0,
                                                   gb, ALU.add, ALU.mult))
                if u:
                    norm_recip(u, W)
                if u == 4:
                    for k in range(KC):
                        V.scalar_tensor_tensor(fz[:, k, :], xT[:, k, 0:SX], vcol[:, R_NF + k:R_NF + k + 1], nrb[:, 0:SX],
                                               ALU.mult, ALU.mult).then_inc(sem("fz_rdy"), 1)
                    return
                sh = 48 * l + KC * (3 if second else 0)

                def lo(k):
                    if k in Z_DVE:
                        dve.wait_ge(sem("nzf_rdy"), 8 * u + k + 1)
                        dve.wait_ge(sem("zh_rdy"), 8 * u + k + 1)
                        V.tensor_tensor(zl[:, k, 0:W], nxz[:, k % 3, 0:W], zh[:, k, 0:W].bitcast(F32), ALU.subtract
                                        ).then_inc(sem("z_dve"), 1)

                for k in range(KC):
                    if k >= 3:
                        z_wait(dve, u, k - 3)
                    if u:
                        src = nxz[:, k % 3, 0:W]
                        ch.link(V.tensor_tensor(src, xT[:, k, 0:W], nrb[:, 0:W], ALU.mult))
                    else:
                        src = xr_start[:, k, :]
                        dve.wait_ge(sem("pool_chain"), k + 1)
                    for c0, c1, s in norm_parts(W):
                        last = V.tensor_scalar(nxz[:, k % 3, c0:c1], src[:, c0:c1], acol[:, k, s:s + 1],
                                               modcol[:, sh + k, s:s + 1], ALU.mult, ALU.add)
                    last.then_inc(sem("nzf_rdy"), 1)
                    if k:
                        lo(k - 1)
                lo(KC - 1)

            for l in range(DEPTH):
                W = NT if l == 0 else SX
                norm(2 * l, NT)

                def lo_modb(b):
                    for h in range(2):
                        dve.wait_ge(sem("hiB"), 2 * b + h + 1)
                        V.tensor_tensor(wl[1][:, h, :], raw[1][:, 1024 * h:1024 * h + 1024], wh[1][:, h, :].bitcast(F32),
                                        ALU.subtract).then_inc(sem("lo_modb"), 1)

                nt = W // P
                G = 4 * nt
                cv = cvt[:, 0:nt, :].rearrange("p t (g d) -> p (t g) d", d=HD)
                sq = cmsq[:, 0:nt, :].rearrange("p t (g d) -> p (t g) d", d=HD)

                def wide(i):
                    return cmst[:, i, 0:G].unsqueeze(2).to_broadcast([P, G, HD])

                def gate_norm(stage):
                    if stage == 0:
                        dve.wait_ge(sem(f"vtr_ev{l}"), 5)
                        ch.link(V.tensor_reduce(cmst[:, 0, 0:G], cv, AX_X, ALU.add))
                        ch.link(V.tensor_scalar(cmst[:, 0, 0:G], cmst[:, 0, 0:G], 1.0 / HD, None, ALU.mult))
                        ch.link(V.tensor_tensor(cv, cv, wide(0), ALU.subtract))
                    elif stage == 1:
                        ch.link(V.tensor_tensor(sq, cv, cv, ALU.mult))
                        ch.link(V.tensor_reduce(cmst[:, 1, 0:G], sq, AX_X, ALU.add))
                        V.tensor_scalar(cmst[:, 1, 0:G], cmst[:, 1, 0:G], 1.0 / HD, EPS, ALU.mult, ALU.add).then_inc(sem("cm_var"), 1)
                    elif stage == 3:
                        dve.wait_ge(sem("cm_std"), l + 1)
                        ch.link(V.reciprocal(cmst[:, 1, 0:G], cmst[:, 1, 0:G]))
                        V.tensor_tensor(cv, cv, wide(1), ALU.mult).then_inc(sem("cm_vn"), 1)

                if l == 0:
                    lo_modb(0)
                    dve.wait_ge(sem("ld_tables"), 16)
                rope_n = 0
                for p, name in enumerate(PANELS):
                    for h in range(2):
                        if name in ("rk", "rq", "aq0", "aq1") or (name == "akav" and h == 0):
                            dst = {"rk": rk[:, h], "rq": rq[:, h], "akav": ak, "aq0": aq[:, h], "aq1": aq[:, 2 + h]}[name]
                            dve.wait_ge(sem(f"ev_in{l}"), 2 * p + h + 1)
                            src = rtmp[:, rope_n % 2, :]
                            ch.then(V.stream_shuffle(shuf[:, :], src, [(j + 16) % 32 for j in range(32)]))
                            ch.link(V.tensor_tensor(dst[:, 0:SX], src, ropeC, ALU.mult))
                            ch.link(V.tensor_tensor(shuf[:, :], shuf[:, :], ropeS, ALU.mult))
                            V.tensor_tensor(dst[:, 0:SX], dst[:, 0:SX], shuf[:, :], ALU.add).then_inc(sem(f"rope_done{l}"), 1)
                            rope_n += 1
                            dve.wait_ge(sem(f"rope_done{l}"), rope_n)
                        if l == 0 and 2 * p + h + 1 < N_MODB:
                            lo_modb(2 * p + h + 1)
                        if l == 0 and p == 1 and h == 1:
                            log_decay_b()
                        if l == 0 and h == 0 and p:
                            mod_add(J_IN + p - 1)
                        if p > CV_AT:
                            gate_norm(2 * (p - CV_AT - 1) + h)
                    if l == 0:
                        mod_copy("use_b", 4 * p + 4)
                if l == 0:
                    mod_add(J_IN + NP_IN - 1)

                def table(h):
                    i, b = l * 4 + h, h % 2
                    ch.link(V.tensor_scalar(T[:, b, :], dist, lg[:, i:i + 1], None, ALU.mult))
                    V.scalar_tensor_tensor(T[:, b, :], dist, nlg[:, 8 + i:9 + i], T[:, b, :], ALU.mult, ALU.min
                                           ).then_inc(sem(f"T_arg{l}"), 1)

                dve.wait_ge(sem("cm_mm"), l + 1)
                table(0)
                cm_jobs = [(r, c0, c1, s) for c0, c1, s in parts(l == 0) for r in range(2)]

                def gate(e):
                    if e < len(cm_jobs):
                        r, c0, c1, s = cm_jobs[e]
                        n = c1 - c0
                        src = ps[:, 3 + r, :] if s == 0 else ps[:, 7, SC * r:SC * r + SC]
                        dst = cmf[:, e % 2, 0:n]
                        g = vcol[:, R_CN + 2 * l + r:R_CN + 2 * l + r + 1]
                        bias = bsb[:, l, r, :].unsqueeze(1).to_broadcast([P, n // P, P])
                        ch.link(V.scalar_tensor_tensor(dst.rearrange("p (t q) -> p t q", q=P),
                                                       src.rearrange("p (t q) -> p t q", q=P), g, bias, ALU.mult, ALU.add))
                        V.tensor_tensor(dst, dst, cu[:, r, c0:c1], ALU.mult).then_inc(sem(f"cm_f{l}"), 1)
                    if 0 < e <= len(cm_jobs):
                        r, c0, c1, s = cm_jobs[e - 1]
                        dve.wait_ge(sem(f"cm_f{l}"), e)
                        dve.wait_ge(sem(f"cm_hi{l}"), e)
                        V.tensor_tensor(zl[:, 6 + r, c0:c1], cmf[:, (e - 1) % 2, 0:c1 - c0],
                                        zh[:, 6 + r, c0:c1].bitcast(F32), ALU.subtract).then_inc(sem(f"cm_lo{l}"), 1)
                        dve.wait_ge(sem(f"cm_lo{l}"), e)

                def table_end(h):
                    b = h % 2
                    dve.wait_ge(sem(f"T_exp{l}"), h + 1)
                    ch.link(V.tensor_tensor(T[:, b, 384:512], T[:, b, 384:512], eye, ALU.add))
                    V.tensor_tensor(TC[:, b, :], TC[:, b, :], TD[:, :], ALU.add).then_inc(sem(f"T_done{l}"), 1)
                    dve.wait_ge(sem(f"T_done{l}"), h + 1)

                jobs = [(c, 0) for c in range(6)] + ([(c, 1) for c in (4, 5)] if l == 0 else [])
                j = 0
                for h in range(4):
                    table_end(h)
                    if h < 3:
                        table(h + 1)
                    for c, s in jobs:
                        n = (SX, SC)[s]
                        if s == 0 and c >= 4:
                            tab = TC[:, h % 2, P - P * (c - 4):P - P * (c - 4) + SX]
                        else:
                            off = 384 - P * (c - 4 * s)
                            tab = T[:, h % 2, off:off + n]
                        dve.wait_ge(sem(f"ret_sc{l}"), j + 1)
                        if j >= 3:
                            dve.wait_ge(sem(f"ret_pv{l}"), j - 2)
                        V.scalar_tensor_tensor(Pm[:, j % 3, 0:n], ps[:, j % 3, 0:n], SCALE, tab, ALU.mult, ALU.mult
                                               ).then_inc(sem(f"ret_p{l}"), 1)
                        if j % 2:
                            gate(j // 2)
                        j += 1
                gn_jobs = [(r, c0, c1) for r in range(2) for c0, c1, s in parts(l == 0)]

                def gn_centre(j):
                    if j < len(gn_jobs):
                        r, c0, c1 = gn_jobs[j]
                        dve.wait_ge(sem(f"gmean_mm{l}"), j + 1)
                        V.tensor_tensor(oc[:, 0:c1 - c0], osb[:, r, c0:c1], ps[:, 4, 0:c1 - c0], ALU.subtract
                                        ).then_inc(sem(f"oc_rdy{l}"), 1)

                def gn_scale(j):
                    if j < len(gn_jobs):
                        r, c0, c1 = gn_jobs[j]
                        n = c1 - c0
                        dve.wait_ge(sem(f"gstd_rdy{l}"), j + 1)
                        ch.link(V.reciprocal(gsq[:, 0:n], gsq[:, 0:n]))
                        ch.link(V.tensor_tensor(oc[:, 0:n], oc[:, 0:n], gsq[:, 0:n], ALU.mult))
                        g = vcol[:, R_RN + 2 * l + r:R_RN + 2 * l + r + 1]
                        V.scalar_tensor_tensor(oc[:, 0:n], oc[:, 0:n], g, rg[:, r, c0:c1], ALU.mult, ALU.mult
                                               ).then_inc(sem(f"ret_f{l}"), 1)

                def gn_lo(j):
                    if 0 <= j < len(gn_jobs):
                        r, c0, c1 = gn_jobs[j]
                        dve.wait_ge(sem(f"ret_f{l}"), j + 1)
                        dve.wait_ge(sem(f"ret_hi{l}"), j + 1)
                        V.tensor_tensor(zl[:, r, c0:c1], oc[:, 0:c1 - c0], zh[:, r, c0:c1].bitcast(F32), ALU.subtract
                                        ).then_inc(sem(f"ret_lo{l}"), 1)
                        dve.wait_ge(sem(f"ret_lo{l}"), j + 1)

                blocks = list(range(4)) + ([4, 5] if l == 0 else [])
                units = [(i, kv) for i in blocks for kv in range(2)]

                def local(i):
                    return list(range(max(i - 1, 0), min(i + 1, 3) + 1)) if i < 4 else []

                def scores(u):
                    i, kv = units[u]
                    nl = P * len(local(i))
                    wd = nl + SC
                    mask = {0: K_MASK + P, 3: K_MASK3}.get(i, K_MASK if i < 4 else K_MASK + 384)
                    if u >= 2:
                        dve.wait_ge(sem(f"at_tr{l}"), sum(len(local(i2)) + 2 for i2, _ in units[:u - 1]))
                    for c in range(4):
                        hd = 4 * kv + c
                        dve.wait_ge(sem(f"at_sc{l}"), 4 * u + c + 1)
                        pair = ps[:, 2 * (c % 2):2 * (c % 2) + 2, :].rearrange("p b n -> p (b n)")
                        V.tensor_tensor_reduce(s_at[:, u % 2, c, 0:wd], pair[:, SX - nl:SX + SC], K[:, mask:mask + wd], SCALE,
                                               sinkb[:, 8 * l + hd:8 * l + hd + 1], ALU.add, ALU.max,
                                               stats[:, u % 2, c:c + 1]).then_inc(sem(f"at_max{l}"), 1)
                    dve.wait_ge(sem(f"at_max{l}"), 4 * u + 4)
                    ch.link(V.tensor_scalar(stats[:, u % 2, 4:8], stats[:, u % 2, 0:4], -1.0, None, ALU.mult))
                    V.tensor_tensor(stats[:, u % 2, 8:12], sinkb[:, 8 * l + 4 * kv:8 * l + 4 * kv + 4], stats[:, u % 2, 4:8],
                                    ALU.add).then_inc(sem(f"at_nb{l}"), 1)

                def weights(u):
                    i, kv = units[u]
                    wd = P * len(local(i)) + SC
                    dve.wait_ge(sem(f"at_exp{l}"), u + 1)
                    ch.link(V.tensor_tensor(stats[:, u % 2, 16:20], stats[:, u % 2, 16:20], stats[:, u % 2, 12:16], ALU.add))
                    ch.link(V.reciprocal(stats[:, u % 2, 16:20], stats[:, u % 2, 16:20]))
                    for c in range(4):
                        last = V.tensor_scalar(s_at[:, u % 2, c, 0:wd], s_at[:, u % 2, c, 0:wd],
                                               stats[:, u % 2, 16 + c:17 + c], None, ALU.mult)
                    last.then_inc(sem(f"at_p{l}"), 1)

                def rest(u):
                    i, kv = units[u]
                    if kv:
                        dve.wait_ge(sem(f"at_hi{l}"), u // 2 + 1)
                        q = slice(P * i, P * i + P)
                        V.tensor_tensor(zl[:, 2:6, q], ps[:, 7, :].rearrange("p (c q) -> p c q", c=4),
                                        zh[:, 2:6, q].bitcast(F32), ALU.subtract).then_inc(sem(f"at_lo{l}"), 1)

                for u in range(len(units)):
                    scores(u)
                    if u % 2 == 0:
                        gn_lo(u // 2 - 1)
                        gn_centre(u // 2)
                    weights(u)
                    if u % 2:
                        gn_scale(u // 2)
                    if u:
                        rest(u - 1)
                rest(len(units) - 1)

                for p in range(4):
                    for h in range(2):
                        n = 2 * p + h
                        dve.wait_ge(sem("use_a"), 2 * (A_OUT[l] + p) + h + 1)
                        for c0, c1, s in parts(l == 0):
                            last = V.scalar_tensor_tensor(xT[:, n, c0:c1], ps[:, h + 2 * s, 0:c1 - c0],
                                                          modcol[:, 48 * l + 16 + n, s:s + 1], xT[:, n, c0:c1], ALU.mult, ALU.add)
                        last.then_inc(sem(f"ev_out{l}"), 1)
                        if n:
                            add_square(2 * l + 1, n - 1, W)
                dve.wait_ge(sem(f"ev_out{l}"), 8)
                norm(2 * l + 1, W)

                V.memset(stats[:, 0, 1:2], 0.0).then_inc(sem(f"ev_h{l}"), 1)
                V.memset(stats[:, 0, 2:3], 0.0).then_inc(sem(f"ev_d{l}"), 1)

                def chunk(s, h, par):
                    n = 2 * s + h
                    per = 2 if l == 0 else 1
                    for c0, c1, sc in parts(l == 0):
                        dve.wait_ge(sem(f"gs_rdy{l}"), per * n + sc + 1)
                        up = ps[:, 3 * h + 1, :] if sc == 0 else ps[:, 3 * h + 2, SC:2 * SC]
                        last = V.tensor_tensor(hf[:, c0:c1], gs[:, c0:c1], up, ALU.mult)
                    last.then_inc(sem(f"ev_h{l}"), 1)

                def chunk_lo(s, h, par):
                    n = 2 * s + h
                    dve.wait_ge(sem(f"hh_rdy{l}"), n + 1)
                    V.tensor_tensor(hl[:, par, h, 0:W], hf[:, 0:W], hh[:, par, h, 0:W].bitcast(F32), ALU.subtract
                                    ).then_inc(sem(f"h_rdy{l}"), 1)
                    dve.wait_ge(sem(f"h_rdy{l}"), n + 1)

                def down(s, chunks=range(KC), last_step=False):
                    if chunks[0] == 0:
                        dve.wait_ge(sem(f"ev_d{l}"), KC * s + 1)
                    for n in chunks:
                        for c0, c1, sc in parts(l == 0):
                            dve.wait_ge(sem(f"dn{sc}_mm{l}"), KC * s + n + 1)
                            src = ps[:, (0, 6)[n % 2], :] if sc == 0 else ps[:, (2, 7)[n % 2], 0:SC]
                            last = V.scalar_tensor_tensor(xT[:, n, c0:c1], src, modcol[:, 48 * l + 40 + n, sc:sc + 1],
                                                          xT[:, n, c0:c1], ALU.mult, ALU.add)
                            if sc == 0:
                                last.then_inc(sem(f"ev_d{l}"), 1)
                            else:
                                last.then_inc(sem(f"ev_dc{l}"), 1)
                        if last_step and n:
                            add_square(2 * l + 2, n - 1, W)

                MODBANK[0], MODCOLS[0] = 6, 1

                def ffn_step(s, par, first=False):
                    chunk(s, 0, par)
                    chunk_lo(s, 0, par)
                    if l == 0:
                        mod_copy("use_m", 4 * s + 4)
                    chunk(s, 1, par)
                    if l == 0:
                        mod_add(J_FFN + s)
                    if not first:
                        down(s - 1, range(0, 3))
                    chunk_lo(s, 1, par)
                    if not first:
                        down(s - 1, range(3, KC))

                ffn_step(0, 0, first=True)
                ffn_step(1, 1)
                with dve.Fori(0, 4) as i:
                    ffn_step(2 * i + 2, 0)
                    ffn_step(2 * i + 3, 1)
                ffn_step(FSTEPS - 1, 0)
                down(FSTEPS - 1, last_step=True)
                dve.wait_ge(sem(f"ev_d{l}"), KC * FSTEPS + 1)
                if l == 0:
                    dve.wait_ge(sem("ev_dc0"), KC * FSTEPS)
                MODBANK[0], MODCOLS[0] = 4, 7
            norm(4, SX)

        @block.tensor
        def _(pe):
            MM, TR = nc.tensor.matmul, nc.tensor.transpose
            MODBANK, MODCOLS = [4], [7]

            def mod_half(m, w_hi, w_lo):
                for jj in range(2):
                    j = 2 * m + jj
                    for w in (w_hi, w_lo):
                        last = MM(ps[:, MODBANK[0], :], c4[:, 4 * j:4 * j + P], w[:, 512 * jj:512 * jj + 512],
                                  start=(j == 0 and w is w_hi), stop=(j == 7 and w is w_lo))
                return last

            def mod_finish(J):
                pe.wait_ge(sem("modrow_rdy"), J + 1)
                for i in range(4):
                    last = MM(ps[:, MODCOLS[0], 256 + 2 * i:258 + 2 * i], modrow[0:4, P * i:P * i + P], sel, start=True, stop=True)
                last.then_inc(sem("mod_fin"), 1)

            def norm(u, W):
                nacc = (norm_later if u else norm_start)[1]
                pe.wait_ge(sem("nacc_rdy"), 8 * u + 8)
                for c0, c1, s in ([(0, SX, 0)] + ([(SX, NT, 1)] if W == NT else [])):
                    last = MM(ps[:, s, 0:c1 - c0], ones, nacc[:, c0:c1], start=True, stop=True)
                last.then_inc(sem("nst_mm"), 1)

            pe.wait_ge(sem("ld_x"), 48)
            for k in range(KC):
                if k >= 2:
                    pe.wait_ge(sem("xt_evac"), k - 1)
                for t in range(6):
                    dst = ps[:, k % 2, P * t:P * t + P] if t < 4 else ps[:, 2 + k % 2, P * (t - 4):P * (t - 4) + P]
                    last = TR(dst, xin[:, t, P * k:P * k + P], eye)
                last.then_inc(sem("xt_mm"), 1)
            pe.wait_ge(sem("ld_small"), 16 * 18)
            TR(ps[:, 7, 0:N_ROWS], rows_a[:, :], eye[0:N_ROWS, 0:N_ROWS])
            TR(ps[:, 7, N_ROWS:N_ROWS + N_BROWS], rows_b[:, :], eye[0:N_BROWS, 0:N_BROWS]).then_inc(sem("vc_mm"), 1)
            for i in range(8):
                last = TR(ps[:, 5 + i // 4, P * (i % 4):P * (i % 4) + P], cws[:, i, :], eye)
            last.then_inc(sem("ws_mm"), 1)
            pe.wait_ge(sem("c4_rdy"), 1)

            def start_panel(q):
                pe.wait_ge(sem("st_lo"), q + 1)
                wh_q, wl_q = [(wh[0], wl[0]), (wh[1], wl[1]), (wh_s, wl_s)][q % 3]
                for hh_ in range(2):
                    last = mod_half(2 * (q % 2) + hh_, wh_q[:, hh_, :], wl_q[:, hh_, :])
                last.then_inc(sem("st_use"), 1)

            start_panel(0)
            start_panel(1)
            norm(0, NT)
            pe.wait_ge(sem("vc_evac"), 1)
            for q in range(2, 8):
                if q % 2 == 0:
                    mod_finish(q // 2 - 1)
                start_panel(q)
            mod_finish(3)

            def three_pass(wt_h, wt_l, h, dsts, ctx, norm_u=None):
                for k in range(KC):
                    w = slice(P * k, P * k + P)
                    if norm_u is not None:
                        z_wait(pe, norm_u, k)
                    for c0, c1, s in parts(ctx):
                        dst = dsts[s]
                        MM(dst, wt_h[:, h, w], zh[:, k, c0:c1], start=(k == 0), stop=False)
                        MM(dst, wt_h[:, h, w], zl[:, k, c0:c1], start=False, stop=False)
                        last = MM(dst, wt_l[:, h, w], zh[:, k, c0:c1], start=False, stop=(k == KC - 1))
                return last

            def panel_half(a, h, ctx, norm_u=None):
                pe.wait_ge(sem("loA"), 2 * a + h + 1)
                three_pass(wh[0], wl[0], h, (ps[:, h, :], ps[:, h + 2, 0:SC]), ctx, norm_u).then_inc(sem("use_a"), 1)

            for l in range(DEPTH):
                W = NT if l == 0 else SX
                if l:
                    norm(2 * l, NT)

                def in_step(p, ctx, first=False):
                    for h in range(2):
                        if not first:
                            pe.wait_ge(sem(f"ev_in{l}"), 2 * p + h - 1)
                        panel_half(A_IN[l] + p, h, ctx, 2 * l if first and h == 0 else None)
                        if l == 0:
                            if h == 0 and not first:
                                mod_finish(J_IN + p - 1)
                            b = 2 * p + h
                            for hh_ in range(2):
                                pe.wait_ge(sem("lo_modb"), 2 * b + hh_ + 1)
                                last = mod_half(2 * h + hh_, wh[1][:, hh_, :], wl[1][:, hh_, :])
                                last.then_inc(sem("use_b"), 1)

                in_step(0, True, first=True)
                with pe.Fori(1, NP_CTX) as p:
                    in_step(p, True)
                in_step(NP_CTX, l == 0)

                def to_tokens(v, slot, ctx, order):
                    pe.wait_ge(sem(f"ev_in{l}"), order)
                    if v:
                        pe.wait_ge(sem(f"vtr_ev{l}"), v)
                    if l == 0:
                        pe.wait_ge(sem("modcol_rdy"), J_IN + (V_AT if v < 3 else CV_AT))
                    for t in range(6 if ctx else 4):
                        dst = ps[:, 5 + (v % 3) % 2, P * t:P * t + P] if t < 4 else ps[:, 7, P * (t - 4):P * (t - 4) + P]
                        last = TR(dst, vT[:, slot, P * t:P * t + P], eye)
                    last.then_inc(sem(f"vtr_mm{l}"), 1)

                for v in range(3):
                    to_tokens(v, v, True, 6)
                pe.wait_ge(sem(f"vtr_ev{l}"), 3)
                with pe.Fori(V_AT + 1, CV_AT + 1) as p:
                    in_step(p, l == 0)
                for v in range(2):
                    to_tokens(3 + v, v, l == 0, 10)
                pe.wait_ge(sem(f"vtr_ev{l}"), 5)
                with pe.Fori(CV_AT + 1, NP_IN) as p:
                    in_step(p, l == 0)
                if l == 0:
                    mod_finish(J_IN + NP_IN - 1)

                pe.wait_ge(sem("cm_vn"), l + 1)
                pe.wait_ge(sem(f"ev_in{l}"), 2 * NP_IN)
                if l == 0:
                    pe.wait_ge(sem("modcol_rdy"), J_IN + NP_IN)
                for s in range(2 if l == 0 else 1):
                    for r in range(2):
                        for t in range((4, 2)[s]):
                            for g2 in range(2):
                                cols = (0, SC * r)[s] + P * t
                                last = MM(ps[64 * g2:64 * g2 + 64, (3 + r, 7)[s], cols:cols + P],
                                          cvt[:, 4 * s + t, P * r + HD * g2:P * r + HD * g2 + HD],
                                          wsT[:, l, P * (2 * r + g2):P * (2 * r + g2) + P], start=True, stop=True)
                last.then_inc(sem("cm_mm"), 1)

                jobs = [(h, c, s) for h in range(4) for c, s in
                        [(c, 0) for c in range(6)] + ([(c, 1) for c in (4, 5)] if l == 0 else [])]
                pe.wait_ge(sem(f"rope_done{l}"), 9)

                def score(j):
                    h, c, s = jobs[j]
                    b, r = 64 * (h % 2), h // 2
                    q = slice(0, SX) if s == 0 else slice(SX, NT)
                    if j >= 3:
                        pe.wait_ge(sem(f"ret_p{l}"), j - 2)
                    MM(ps[:, j % 3, 0:q.stop - q.start], rk[b:b + 64, r, P * c:P * c + P], rq[b:b + 64, r, q],
                       start=True, stop=True).then_inc(sem(f"ret_sc{l}"), 1)

                def value(j):
                    h, c, s = jobs[j]
                    b = 64 * (h % 2)
                    n = (SX, SC)[s]
                    first = c == (0, 4)[s]
                    if h == 2 and first and s == 0:
                        pe.wait_ge(sem(f"osb_rdy{l}"), 1)
                    pe.wait_ge(sem(f"ret_p{l}"), j + 1)
                    last = MM(ps[b:b + 64, 5 + s, 0:n], vtok[:, c, HD * h:HD * h + HD], Pm[:, j % 3, 0:n],
                              start=first, stop=(c == 5))
                    last.then_inc(sem(f"ret_pv{l}"), 1)

                for j in range(len(jobs)):
                    score(j)
                    if j >= 2:
                        value(j - 2)
                value(len(jobs) - 2)
                value(len(jobs) - 1)
                gn_jobs = [(r, c0, c1) for r in range(2) for c0, c1, s in parts(l == 0)]

                def gn_mean(j):
                    if j < len(gn_jobs):
                        r, c0, c1 = gn_jobs[j]
                        pe.wait_ge(sem(f"osb_rdy{l}"), r + 1)
                        if j:
                            pe.wait_ge(sem(f"gstd_rdy{l}"), j)
                        MM(ps[:, 4, 0:c1 - c0], blk, osb[:, r, c0:c1], start=True, stop=True).then_inc(sem(f"gmean_mm{l}"), 1)

                def gn_var(j):
                    if j < len(gn_jobs):
                        n = gn_jobs[j][2] - gn_jobs[j][1]
                        pe.wait_ge(sem(f"gsq_rdy{l}"), j + 1)
                        MM(ps[:, 4, 0:n], blk, gsq[:, 0:n], start=True, stop=True).then_inc(sem(f"gvar_mm{l}"), 1)

                blocks = list(range(4)) + ([4, 5] if l == 0 else [])
                units = [(i, kv) for i in blocks for kv in range(2)]
                pe.wait_ge(sem(f"osb_rdy{l}"), 2)
                pe.wait_ge(sem(f"qk_lo{l}"), 6)
                pe.wait_ge(sem(f"cm_lo{l}"), 4 if l == 0 else 2)

                def local(i):
                    return list(range(max(i - 1, 0), min(i + 1, 3) + 1)) if i < 4 else []

                def scores(u):
                    i, kv = units[u]
                    loc = local(i)
                    nl = P * len(loc)
                    for c in range(4):
                        if 4 * u + c >= 2:
                            pe.wait_ge(sem(f"at_max{l}"), 4 * u + c - 1)
                        blk_q = slice(P * i, P * i + P)
                        areas = [(ps[:, 2 * (c % 2) + 1, 0:SC], slice(SX, NT))]
                        if loc:
                            areas.insert(0, (ps[:, 2 * (c % 2), SX - nl:SX], slice(P * loc[0], P * loc[0] + nl)))
                        for dst, keys in areas:
                            MM(dst, aqh[:, c, blk_q], akh[:, kv, keys], start=True, stop=False)
                            MM(dst, aqh[:, c, blk_q], akl[:, kv, keys], start=False, stop=False)
                            last = MM(dst, aql[:, c, blk_q], akh[:, kv, keys], start=False, stop=True)
                        last.then_inc(sem(f"at_sc{l}"), 1)

                g = 0

                def values(u):
                    nonlocal g
                    i, kv = units[u]
                    chunks = local(i) + [4, 5]
                    pe.wait_ge(sem(f"at_p{l}"), u + 1)
                    g0 = g
                    for kk in range(len(chunks)):
                        if g >= 2:
                            pe.wait_ge(sem(f"at_pt{l}"), g - 1)
                        for c in range(4):
                            last = TR(ps[:, 5 + g % 2, P * c:P * c + P], s_at[:, u % 2, c, P * kk:P * kk + P], eye)
                        last.then_inc(sem(f"at_tr{l}"), 1)
                        g += 1
                    if kv == 0 and i:
                        pe.wait_ge(sem(f"at_lo{l}"), i)
                    for kk, tile in enumerate(chunks):
                        pe.wait_ge(sem(f"at_pt{l}"), g0 + kk + 1)
                        last = MM(ps[64 * kv:64 * kv + 64, 7, :], vtok[:, tile, 256 + HD * kv:256 + HD * kv + HD], pT[:, kk, :],
                                  start=(kk == 0), stop=(kk == len(chunks) - 1))
                    last.then_inc(sem(f"at_o{l}"), 1)

                for u in range(len(units)):
                    scores(u)
                    if u % 2 == 0:
                        gn_mean(u // 2)
                    if u:
                        values(u - 1)
                    if u % 2 == 0:
                        gn_var(u // 2)
                values(len(units) - 1)

                pe.wait_ge(sem(f"at_lo{l}"), len(blocks))
                pe.wait_ge(sem(f"ret_lo{l}"), len(gn_jobs))

                def out_step(p, first=False):
                    for h in range(2):
                        if not first:
                            pe.wait_ge(sem(f"ev_out{l}"), 2 * p + h - 1)
                        panel_half(A_OUT[l] + p, h, l == 0)

                out_step(0, first=True)
                with pe.Fori(1, 4) as p:
                    out_step(p)

                norm(2 * l + 1, W)

                MODBANK[0], MODCOLS[0] = 6, 1

                def ffn_mod(s, h):
                    for hh_ in range(2):
                        pe.wait_ge(sem("loM"), 4 * s + 2 * h + hh_ + 1)
                        last = mod_half(2 * h + hh_, wh_m[:, hh_, :], wl_m[:, hh_, :])
                        last.then_inc(sem("use_m"), 1)

                def down(s, par, wd_h=wh_d, wd_l=wl_d):
                    pe.wait_ge(sem(f"loD{l}"), 2 * s + 2)
                    pe.wait_ge(sem(f"h_rdy{l}"), 2 * s + 2)
                    start = type(s) is int and s == 0
                    for n in range(KC):
                        w = slice(P * n, P * n + P)
                        for c0, c1, sc in parts(l == 0):
                            if sc == 0 and not (start and n == 0):
                                pe.wait_ge(sem(f"ev_d{l}"), KC * s + n)
                            if sc == 1 and not (start and n < 2):
                                pe.wait_ge(sem(f"ev_dc{l}"), KC * s + n - 1)
                            dst = ps[:, (0, 6)[n % 2], :] if sc == 0 else ps[:, (2, 7)[n % 2], 0:SC]
                            for k in range(2):
                                MM(dst, wd_h[:, k, w], hh[:, par, k, c0:c1], start=(k == 0), stop=False)
                                MM(dst, wd_h[:, k, w], hl[:, par, k, c0:c1], start=False, stop=False)
                                last = MM(dst, wd_l[:, k, w], hh[:, par, k, c0:c1], start=False, stop=(k == 1))
                            last.then_inc(sem(f"dn{sc}_mm{l}"), 1)

                def ffn_step(s, par, first=False):
                    a, b = A_GATE[l] + s, B_UP[l] + s
                    if not (type(s) is int and s < 2):
                        pe.wait_ge(sem(f"ev_d{l}"), KC * (s - 1))
                        if l == 0:
                            pe.wait_ge(sem("ev_dc0"), KC * (s - 1) - 1)
                    for h in range(2):
                        pe.wait_ge(sem("loA"), 2 * a + h + 1)
                        pe.wait_ge(sem(f"ev_h{l}"), 2 * s + h) if not first else None
                        last = three_pass(wh[0], wl[0], h, (ps[:, 3 * h, :], ps[:, 3 * h + 2, 0:SC]), l == 0,
                                          2 * l + 1 if first and h == 0 else None)
                        last.then_inc(sem("use_a"), 1)
                        if l == 0 and h:
                            ffn_mod(s, 1)
                        pe.wait_ge(sem("loB"), 2 * (b - N_MODB) + h + 1)
                        if l == 0 and h == 0 and not first:
                            pe.wait_ge(sem("modcol_rdy"), J_FFN + s)
                        last = three_pass(wh[1], wl[1], h, (ps[:, 3 * h + 1, :], ps[:, 3 * h + 2, SC:2 * SC]), l == 0)
                        last.then_inc(sem("use_b"), 1)
                        if l == 0 and h == 0:
                            if not first:
                                pe.wait_ge(sem("ev_d0"), KC * (s - 1) + 1)
                            ffn_mod(s, 0)
                    pe.wait_ge(sem(f"ev_h{l}"), 2 * s + 2)
                    if l == 0:
                        mod_finish(J_FFN + s)
                    if not first:
                        down(s - 1, 1 - par)

                ffn_step(0, 0, first=True)
                ffn_step(1, 1)
                with pe.Fori(0, 4) as i:
                    ffn_step(2 * i + 2, 0)
                    ffn_step(2 * i + 3, 1)
                ffn_step(FSTEPS - 1, 0)
                down(FSTEPS - 1, 0, wh[1], wl[1])
                MODBANK[0], MODCOLS[0] = 4, 7

            norm(4, SX)
            for half in range(2):
                pe.wait_ge(sem("fz_rdy"), 4 * half + 4)
                for t in range(4):
                    g = 4 * half + t
                    if g >= 2:
                        pe.wait_ge(sem("fin_evac"), g - 1)
                    for i in range(4):
                        last = TR(ps[:, 2 + g % 2, P * i:P * i + P], fz[:, 4 * half + i, P * t:P * t + P], eye)
                    last.then_inc(sem("fin_mm"), 1)


_INS = ['x', 'c', 'ctx', 'c_ctx', 'w_mod', 'b_mod', 'norm1_g', 'norm2_g', 'w_in', 'ret_decay_f', 'ret_decay_b',
        'ret_norm_g', 'attn_sink', 'cm_norm_g', 'cm_w_s', 'cm_b_s', 'w_out', 'w_gate', 'w_up', 'w_down', 'final_norm_g']


def shape_constants():
    import numpy as np
    k = np.zeros((P, K_ALL), np.float32)
    k[:, K_EYE:K_EYE + P] = np.eye(P)
    k[:, K_ONES:K_ONES + P] = 1.0
    for g in range(2):
        k[64 * g:64 * g + 64, K_BLK + 64 * g:K_BLK + 64 * g + 64] = 1.0 / HD
    k[[0, 2], K_SEL] = 1.0
    k[[1, 3], K_SEL + 1] = 1.0
    q, kk = np.arange(P)[:, None], np.arange(384)[None, :]
    band = np.where(np.abs(kk - P - q) <= P, 0.0, MASKED)
    k[:, K_MASK:K_MASK + 384] = band
    k[:, K_MASK3:K_MASK3 + 256] = band[:, 0:256]
    k[:, K_DIST:K_DIST + DIST_W] = np.arange(DIST_W)[None, :] - 384 - q
    pos = np.arange(SX)
    inv = (1.0 / np.float32(10000.0) ** (np.arange(16, dtype=np.float32) / np.float32(16))).astype(np.float32)
    for r in range(P):
        d = r % HD
        at = (pos // 64 if d < 32 else pos % 64).astype(np.float32)
        ang = at * inv[d % 16]
        k[r, K_RC:K_RC + SX] = np.cos(ang)
        k[r, K_RS:K_RS + SX] = np.sin(ang) * (-1.0 if d % 32 < 16 else 1.0)
    return k


def kernel(**inputs):
    import numpy as _np
    import concourse.bacc as _bacc
    from concourse.bass_utils import run_bass_kernel_spmd as _run

    nc = _bacc.Bacc("TRN2", target_bir_lowering=False, num_devices=1, dynamic_dma_scratch_size=1024)
    arrays, args = {}, []
    for name in _INS:
        a = _np.ascontiguousarray(inputs[name])
        arrays[f"in_{name}_dram"] = a
        args.append(nc.dram_tensor(f"in_{name}_dram", a.shape, F32, kind="ExternalInput").ap())
    arrays["consts_dram"] = shape_constants()
    args.append(nc.dram_tensor("consts_dram", (P, K_ALL), F32, kind="ExternalInput").ap())
    args.append(nc.dram_tensor("out_0_dram", (1, SX, D), F32, kind="ExternalOutput").ap())
    trunk(nc, *args)
    r = _run(nc, [arrays], core_ids=[0])
    return r.results[0]["out_0_dram"]
```
